# Optimizing a Trainium2 kernel written in Bass

```python
import math
import jax, jax.numpy as jnp
from jax import lax
import numpy as np
import jax
import jax.numpy as jnp

D_MODEL = 1024
BATCH = 1
SEQ = 512
DEPTH = 2

N_A = DEPTH // 2
N_B = DEPTH - N_A
POOL_WINDOWS = (2, 4, 8, 16)
POOL_GROUP = D_MODEL // len(POOL_WINDOWS)
N_HEADS = 16
HEAD_DIM = 64
N_KV_GROUPS = 4
HEADS_PER_GROUP = N_HEADS // N_KV_GROUPS
CMP_STRIDE = 16
CMP_LEN = 2 * CMP_STRIDE
CMP_HIDDEN = 128
SLC_BLOCK = 64
N_SELECT = 16
WINDOW = 512
Q_BLOCK = 64
N_BRANCH = 3
ROPE_THETA = 500000.0
ROT_DIM = HEAD_DIM // 4
D_FF = 2816
CONV_W = 3
PLE_DIM = 256

EPS = 1e-6
NEG = -1e30
FORCE_SCORE = 1e4


def rmsnorm(x, g):
    xf = x.astype(jnp.float32)
    y = xf * lax.rsqrt(jnp.mean(xf * xf, axis=-1, keepdims=True) + EPS) * g.astype(jnp.float32)
    return y.astype(x.dtype)

def rope_tables(pos):
    inv_freq = ROPE_THETA ** (-jnp.arange(0, ROT_DIM, 2, dtype=jnp.float32) / ROT_DIM)
    ang = pos.astype(jnp.float32)[..., None] * inv_freq
    return jnp.cos(ang), jnp.sin(ang)

def rope(x, cos, sin):
    xf = x.astype(jnp.float32)
    half = ROT_DIM // 2
    x1, x2, xp = xf[..., :half], xf[..., half:ROT_DIM], xf[..., ROT_DIM:]
    out = jnp.concatenate([x1 * cos - x2 * sin, x2 * cos + x1 * sin, xp], axis=-1)
    return out.astype(x.dtype)

def masked_softmax(s, mask):
    s = jnp.where(mask, s, NEG)
    m = jnp.max(s, axis=-1, keepdims=True)
    e = jnp.where(mask, jnp.exp(s - m), 0.0)
    return e / jnp.maximum(jnp.sum(e, axis=-1, keepdims=True), 1e-30)

def pool_mixer(h, w, scale):
    B, S, D = h.shape
    c = jnp.cumsum(h.astype(jnp.float32), axis=1)
    c = jnp.pad(c, ((0, 0), (1, 0), (0, 0)))
    t = jnp.arange(S)
    outs = []
    for gi, win in enumerate(POOL_WINDOWS):
        sl = slice(gi * POOL_GROUP, (gi + 1) * POOL_GROUP)
        cg = c[..., sl]
        lo = jnp.maximum(t + 1 - win, 0)
        cnt = jnp.minimum(t + 1, win).astype(jnp.float32)
        avg = (cg[:, t + 1] - cg[:, lo]) / cnt[:, None]
        u = (avg - h[..., sl].astype(jnp.float32)).astype(h.dtype)
        outs.append(jnp.einsum('bsc,cd->bsd', u, w[gi]))
    return jnp.concatenate(outs, axis=-1) * scale

def conv_ffn(h, w_up, conv_w, conv_b, w_down):
    S = h.shape[1]
    u = h @ w_up
    up = jnp.pad(u, ((0, 0), (CONV_W - 1, 0), (0, 0)))
    u = sum(conv_w[j] * up[:, j:j + S] for j in range(CONV_W)) + conv_b
    a, g = u[..., :D_FF], u[..., D_FF:]
    return (jax.nn.silu(g) * a) @ w_down

def compress(blocks, pos_emb, w1, w2):
    z = blocks + pos_emb
    z = z.reshape(z.shape[:3] + (CMP_LEN * HEAD_DIM,))
    return jax.nn.gelu(z @ w1) @ w2

def nsa_shared_kv(x, positions, norm_kv, w_kv, cmp_pos_k, cmp_w1_k, cmp_w2_k, cmp_pos_v, cmp_w1_v, cmp_w2_v):
    B, S, _ = x.shape
    h = rmsnorm(x, norm_kv)
    kv = (h @ w_kv).reshape(B, S, 2 * N_BRANCH, N_KV_GROUPS, HEAD_DIM).transpose(2, 0, 3, 1, 4)
    k_c, v_c, k_s, v_s, k_w, v_w = [kv[i] for i in range(2 * N_BRANCH)]
    cos, sin = rope_tables(positions)
    k_s = rope(k_s, cos[:, None], sin[:, None])
    k_w = rope(k_w, cos[:, None], sin[:, None])
    n_chunk = S // CMP_STRIDE
    n_cmp = n_chunk - 1
    def blocks_of(z):
        ch = z.reshape(B, N_KV_GROUPS, n_chunk, CMP_STRIDE, HEAD_DIM)
        return jnp.concatenate([ch[:, :, :-1], ch[:, :, 1:]], axis=3)
    kc = compress(blocks_of(k_c), cmp_pos_k, cmp_w1_k, cmp_w2_k)
    vc = compress(blocks_of(v_c), cmp_pos_v, cmp_w1_v, cmp_w2_v)
    end_idx = CMP_STRIDE * jnp.arange(n_cmp) + CMP_LEN - 1
    cos_c, sin_c = rope_tables(positions[:, end_idx])
    kc = rope(kc, cos_c[:, None], sin_c[:, None])
    n_slc = S // SLC_BLOCK
    ks_blk = k_s.reshape(B, N_KV_GROUPS, n_slc, SLC_BLOCK, HEAD_DIM)
    vs_blk = v_s.reshape(B, N_KV_GROUPS, n_slc, SLC_BLOCK, HEAD_DIM)
    pad = ((0, 0), (0, 0), (WINDOW, 0), (0, 0))
    kw_pad, vw_pad = jnp.pad(k_w, pad), jnp.pad(v_w, pad)
    return (kc, vc, ks_blk, vs_blk, kw_pad, vw_pad)

def nsa_attention(h, w_in, w_out, cos, sin, kv):
    kc, vc, ks_blk, vs_blk, kw_pad, vw_pad = kv
    B, S, _ = h.shape
    n_cmp = kc.shape[2]
    n_slc = ks_blk.shape[2]
    n_top = min(N_SELECT, n_slc)
    scale = HEAD_DIM ** -0.5
    proj = h @ w_in
    q = proj[..., :N_HEADS * HEAD_DIM].reshape(B, S, N_HEADS, HEAD_DIM)
    q = rope(q, cos[:, :, None], sin[:, :, None])
    q = q.reshape(B, S, N_KV_GROUPS, HEADS_PER_GROUP, HEAD_DIM).transpose(0, 2, 3, 1, 4)
    gates = jax.nn.sigmoid(proj[..., N_HEADS * HEAD_DIM:].astype(jnp.float32))
    gates = gates.reshape(B, S, N_KV_GROUPS, HEADS_PER_GROUP, N_BRANCH).transpose(0, 2, 3, 1, 4)

    c_idx = jnp.arange(n_cmp)
    c_end = CMP_STRIDE * c_idx + CMP_LEN - 1
    blk = jnp.arange(n_slc)
    c_start = CMP_STRIDE * c_idx
    overlap = ((c_start[:, None] < (blk[None] + 1) * SLC_BLOCK)
               & (c_start[:, None] + CMP_LEN > blk[None] * SLC_BLOCK)).astype(jnp.float32)
    gather = jax.vmap(jax.vmap(lambda kb, ix: kb[ix]))

    def block_fn(s):
        t = s + jnp.arange(Q_BLOCK)
        qb = lax.dynamic_slice_in_dim(q, s, Q_BLOCK, axis=3)
        gb = lax.dynamic_slice_in_dim(gates, s, Q_BLOCK, axis=3)
        sc = jnp.einsum('bghqd,bgcd->bghqc', qb, kc).astype(jnp.float32) * scale
        p_c = masked_softmax(sc, c_end[None, :] <= t[:, None])
        o_c = jnp.einsum('bghqc,bgcd->bghqd', p_c.astype(vc.dtype), vc)
        imp = jnp.einsum('bghqc,cn->bgqn', p_c, overlap)
        cur = t // SLC_BLOCK
        forced = (blk[None] == 0) | (blk[None] == cur[:, None]) | (blk[None] == cur[:, None] - 1)
        valid = blk[None] * SLC_BLOCK <= t[:, None]
        score = jnp.where(valid, jnp.where(forced, FORCE_SCORE, imp), NEG)
        vals, idx = lax.top_k(score, n_top)
        ok = vals > 0.5 * NEG
        ks_g = gather(ks_blk, idx).reshape(B, N_KV_GROUPS, Q_BLOCK, n_top * SLC_BLOCK, HEAD_DIM)
        vs_g = gather(vs_blk, idx).reshape(B, N_KV_GROUPS, Q_BLOCK, n_top * SLC_BLOCK, HEAD_DIM)
        kpos = idx[..., None] * SLC_BLOCK + jnp.arange(SLC_BLOCK)
        mask_s = (ok[..., None] & (kpos <= t[:, None, None])).reshape(B, N_KV_GROUPS, Q_BLOCK, n_top * SLC_BLOCK)
        ss = jnp.einsum('bghqd,bgqkd->bghqk', qb, ks_g).astype(jnp.float32) * scale
        p_s = masked_softmax(ss, mask_s[:, :, None])
        o_s = jnp.einsum('bghqk,bgqkd->bghqd', p_s.astype(vs_g.dtype), vs_g)
        kw = lax.dynamic_slice_in_dim(kw_pad, s, WINDOW + Q_BLOCK, axis=2)
        vw = lax.dynamic_slice_in_dim(vw_pad, s, WINDOW + Q_BLOCK, axis=2)
        kpos_w = s - WINDOW + jnp.arange(WINDOW + Q_BLOCK)
        diff = t[:, None] - kpos_w[None]
        mask_w = (diff >= 0) & (diff < WINDOW) & (kpos_w[None] >= 0)
        sw = jnp.einsum('bghqd,bgkd->bghqk', qb, kw).astype(jnp.float32) * scale
        p_w = masked_softmax(sw, mask_w)
        o_w = jnp.einsum('bghqk,bgkd->bghqd', p_w.astype(vw.dtype), vw)
        out = (gb[..., 0:1] * o_c.astype(jnp.float32) + gb[..., 1:2] * o_s.astype(jnp.float32)
               + gb[..., 2:3] * o_w.astype(jnp.float32))
        return out.astype(h.dtype)

    starts = jnp.arange(S // Q_BLOCK) * Q_BLOCK
    o = lax.map(block_fn, starts)
    o = o.transpose(1, 0, 4, 2, 3, 5).reshape(B, S, N_HEADS * HEAD_DIM)
    return o @ w_out

def first_inputs(seed: int = 0) -> dict:
    key = jax.random.key(seed)
    ks = iter(jax.random.split(key, 40))
    f32 = jnp.float32
    def w(shape, fan):
        return jax.random.normal(next(ks), shape, f32) * (fan ** -0.5)
    def gain(shape):
        return 1.0 + 0.05 * jax.random.normal(next(ks), shape, f32)
    def small(shape, s=0.02):
        return s * jax.random.normal(next(ks), shape, f32)
    q_cols = N_HEADS * HEAD_DIM + N_HEADS * N_BRANCH
    return {
        "x": jax.random.normal(next(ks), (BATCH, SEQ, D_MODEL), f32),
        "p": jax.random.normal(next(ks), (DEPTH, BATCH, SEQ, PLE_DIM), f32),
        "positions": jnp.broadcast_to(jnp.arange(SEQ, dtype=jnp.int32), (BATCH, SEQ)),
        "norm_mix": gain((DEPTH, D_MODEL)),
        "pool_w": w((N_A, len(POOL_WINDOWS), POOL_GROUP, POOL_GROUP), POOL_GROUP),
        "pool_scale": gain((N_A, D_MODEL)),
        "norm_kv": gain((D_MODEL,)),
        "w_kv": w((D_MODEL, 2 * N_BRANCH * N_KV_GROUPS * HEAD_DIM), D_MODEL),
        "cmp_pos_k": small((CMP_LEN, HEAD_DIM), 0.1),
        "cmp_w1_k": w((CMP_LEN * HEAD_DIM, CMP_HIDDEN), CMP_LEN * HEAD_DIM),
        "cmp_w2_k": w((CMP_HIDDEN, HEAD_DIM), CMP_HIDDEN),
        "cmp_pos_v": small((CMP_LEN, HEAD_DIM), 0.1),
        "cmp_w1_v": w((CMP_LEN * HEAD_DIM, CMP_HIDDEN), CMP_LEN * HEAD_DIM),
        "cmp_w2_v": w((CMP_HIDDEN, HEAD_DIM), CMP_HIDDEN),
        "w_in_b": w((N_B, D_MODEL, q_cols), D_MODEL),
        "w_out_b": w((N_B, N_HEADS * HEAD_DIM, D_MODEL), N_HEADS * HEAD_DIM),
        "norm_ffn": gain((DEPTH, D_MODEL)),
        "ffn_up": w((DEPTH, D_MODEL, 2 * D_FF), D_MODEL),
        "ffn_conv": w((DEPTH, CONV_W, 2 * D_FF), CONV_W),
        "ffn_conv_b": small((DEPTH, 2 * D_FF)),
        "ffn_down": w((DEPTH, D_FF, D_MODEL), D_FF),
        "norm_ple": gain((DEPTH, D_MODEL)),
        "ple_gate": w((DEPTH, D_MODEL, D_MODEL), D_MODEL),
        "ple_proj": w((DEPTH, PLE_DIM, D_MODEL), PLE_DIM),
        "norm_final": gain((D_MODEL,)),
    }

def first_block(x, p, positions, norm_mix, pool_w, pool_scale, norm_kv, w_kv,
              cmp_pos_k, cmp_w1_k, cmp_w2_k, cmp_pos_v, cmp_w1_v, cmp_w2_v,
              w_in_b, w_out_b, norm_ffn, ffn_up, ffn_conv, ffn_conv_b, ffn_down,
              norm_ple, ple_gate, ple_proj, norm_final):
    cos, sin = rope_tables(positions)
    kv = None
    for i in range(DEPTH):
        if i < N_A:
            x = x + pool_mixer(rmsnorm(x, norm_mix[i]), pool_w[i], pool_scale[i])
        else:
            if i == N_A:
                kv = nsa_shared_kv(x, positions, norm_kv, w_kv, cmp_pos_k, cmp_w1_k, cmp_w2_k,
                                   cmp_pos_v, cmp_w1_v, cmp_w2_v)
            j = i - N_A
            x = x + nsa_attention(rmsnorm(x, norm_mix[i]), w_in_b[j], w_out_b[j], cos, sin, kv)
        x = x + conv_ffn(rmsnorm(x, norm_ffn[i]), ffn_up[i], ffn_conv[i], ffn_conv_b[i], ffn_down[i])
        gate = jax.nn.sigmoid(rmsnorm(x, norm_ple[i]) @ ple_gate[i])
        x = x + gate * (p[i] @ ple_proj[i])
    return rmsnorm(x, norm_final)


N_Q_HEADS = 8
N_KV_HEADS = 2
GROUP = N_Q_HEADS // N_KV_HEADS
WINDOW_2 = 128
ATTN_BLOCK = WINDOW_2
Q_WIDTH = N_Q_HEADS * HEAD_DIM
KV_WIDTH = N_KV_HEADS * HEAD_DIM
NUM_BUCKETS = 32
MAX_DISTANCE = 128
CONV_CHANNELS = D_MODEL // 2
CONV_WIDTH = 31
EVEN_IN = Q_WIDTH + 2 * KV_WIDTH + 2 * CONV_CHANNELS
EVEN_CAT = Q_WIDTH + CONV_CHANNELS
LRU_WIDTH = D_MODEL
LRU_HEADS = 8
LRU_BLOCK = LRU_WIDTH // LRU_HEADS
LRU_CONV_WIDTH = 4
RG_LRU_C = 8.0
RMS_EPS = 1e-6
LN_EPS = 1e-5
NEG_INF = -1e30
N_EVEN = (DEPTH + 1) // 2
N_ODD = DEPTH // 2


def _rmsnorm(x, g):
    xf = x.astype(jnp.float32)
    y = xf * lax.rsqrt(jnp.mean(xf * xf, axis=-1, keepdims=True) + RMS_EPS)
    return (y * g.astype(jnp.float32)).astype(x.dtype)

def _layernorm(x, g, b):
    xf = x.astype(jnp.float32)
    mu = jnp.mean(xf, axis=-1, keepdims=True)
    var = jnp.mean(jnp.square(xf - mu), axis=-1, keepdims=True)
    y = (xf - mu) * lax.rsqrt(var + LN_EPS)
    return (y * g.astype(jnp.float32) + b.astype(jnp.float32)).astype(x.dtype)

def _swiglu(x, wg, wu, wd):
    return (jax.nn.silu(x @ wg) * (x @ wu)) @ wd

def _causal_depthwise_conv(x, w, b):
    k_width, chans = w.shape
    y = lax.conv_general_dilated(
        x, w[:, None, :].astype(x.dtype), window_strides=(1,),
        padding=[(k_width - 1, 0)], dimension_numbers=("NWC", "WIO", "NWC"),
        feature_group_count=chans)
    return y + b.astype(x.dtype)

def _t5_bucket(dist):
    n = jnp.maximum(dist, 0)
    max_exact = NUM_BUCKETS // 2
    nf = jnp.maximum(n, max_exact).astype(jnp.float32)
    large = max_exact + (jnp.log(nf / max_exact) / math.log(MAX_DISTANCE / max_exact)
                         * (NUM_BUCKETS - max_exact)).astype(jnp.int32)
    large = jnp.minimum(large, NUM_BUCKETS - 1)
    return jnp.where(n < max_exact, n, large)

def _swa_sink_attention(q, k, v, sinks, rel_bias):
    bsz, seq = q.shape[:2]
    nb = seq // ATTN_BLOCK
    qb = q.reshape(bsz, nb, ATTN_BLOCK, N_KV_HEADS, GROUP, HEAD_DIM)
    kb = k.reshape(bsz, nb, ATTN_BLOCK, N_KV_HEADS, HEAD_DIM)
    vb = v.reshape(bsz, nb, ATTN_BLOCK, N_KV_HEADS, HEAD_DIM)
    kk = jnp.concatenate([jnp.concatenate([jnp.zeros_like(kb[:, :1]), kb[:, :-1]], axis=1), kb], axis=2)
    vv = jnp.concatenate([jnp.concatenate([jnp.zeros_like(vb[:, :1]), vb[:, :-1]], axis=1), vb], axis=2)
    scores = jnp.einsum("bnqhgd,bnshd->bnhgqs", qb, kk,
                        preferred_element_type=jnp.float32) * (1.0 / math.sqrt(HEAD_DIM))
    qi = jnp.arange(ATTN_BLOCK)[:, None]
    sj = jnp.arange(2 * ATTN_BLOCK)[None, :]
    dist = qi + ATTN_BLOCK - sj
    bias = rel_bias.astype(jnp.float32)[_t5_bucket(dist)]
    bias = jnp.transpose(bias, (2, 0, 1)).reshape(N_KV_HEADS, GROUP, ATTN_BLOCK, 2 * ATTN_BLOCK)
    in_window = (dist >= 0) & (dist < WINDOW_2)
    key_pos = jnp.arange(nb)[:, None, None] * ATTN_BLOCK + sj[None] - ATTN_BLOCK
    mask = in_window[None] & (key_pos >= 0)
    scores = jnp.where(mask[None, :, None, None], scores + bias[None, None], NEG_INF)
    sink = sinks.astype(jnp.float32).reshape(N_KV_HEADS, GROUP)[None, None, :, :, None, None]
    sink = jnp.broadcast_to(sink, scores.shape[:-1] + (1,))
    probs = jax.nn.softmax(jnp.concatenate([scores, sink], axis=-1), axis=-1)[..., :-1]
    out = jnp.einsum("bnhgqs,bnshd->bnqhgd", probs.astype(v.dtype), vv)
    return out.reshape(bsz, seq, Q_WIDTH)

def _attn_conv_mixer(h, w_in, sinks, conv_w, conv_b, ln_g, ln_b, w_out, rel_bias):
    bsz, seq, _ = h.shape
    u = h @ w_in
    o1 = Q_WIDTH
    o2 = o1 + KV_WIDTH
    o3 = o2 + KV_WIDTH
    o4 = o3 + CONV_CHANNELS
    q = u[..., :o1].reshape(bsz, seq, N_Q_HEADS, HEAD_DIM)
    k = u[..., o1:o2].reshape(bsz, seq, N_KV_HEADS, HEAD_DIM)
    v = u[..., o2:o3].reshape(bsz, seq, N_KV_HEADS, HEAD_DIM)
    attn = _swa_sink_attention(q, k, v, sinks, rel_bias)
    glu = u[..., o3:o4] * jax.nn.sigmoid(u[..., o4:])
    c = jax.nn.silu(_layernorm(_causal_depthwise_conv(glu, conv_w, conv_b), ln_g, ln_b))
    return jnp.concatenate([attn, c], axis=-1) @ w_out

def _rg_lru(x, ga_w, ga_b, gx_w, gx_b, lam):
    bsz, seq, width = x.shape
    xh = x.reshape(bsz, seq, LRU_HEADS, LRU_BLOCK)
    r = jax.nn.sigmoid(jnp.einsum("bshi,hij->bshj", xh, ga_w).reshape(bsz, seq, width) + ga_b)
    i = jax.nn.sigmoid(jnp.einsum("bshi,hij->bshj", xh, gx_w).reshape(bsz, seq, width) + gx_b)
    log_a = RG_LRU_C * r.astype(jnp.float32) * jax.nn.log_sigmoid(lam.astype(jnp.float32))
    a = jnp.exp(log_a)
    bx = jnp.sqrt(-jnp.expm1(2.0 * log_a)) * (i * x).astype(jnp.float32)

    def combine(left, right):
        a1, b1 = left
        a2, b2 = right
        return a1 * a2, a2 * b1 + b2

    _, hs = lax.associative_scan(combine, (a, bx), axis=1)
    return hs.astype(x.dtype)

def _recurrent_mixer(h, w_in, conv_w, conv_b, ga_w, ga_b, gx_w, gx_b, lam, w_out):
    u = h @ w_in
    gate = jax.nn.gelu(u[..., :LRU_WIDTH])
    rec = _causal_depthwise_conv(u[..., LRU_WIDTH:], conv_w, conv_b)
    rec = _rg_lru(rec, ga_w, ga_b, gx_w, gx_b, lam)
    return (gate * rec) @ w_out

def second_inputs(seed: int = 0) -> dict:
    key = jax.random.key(seed)
    ks = iter(jax.random.split(key, 40))

    def nrm(shape, scale):
        return jax.random.normal(next(ks), shape, jnp.float32) * scale

    def gain(shape):
        return 1.0 + nrm(shape, 0.02)

    x = nrm((BATCH, SEQ, D_MODEL), 1.0)
    u = jax.random.uniform(next(ks), (N_ODD, LRU_WIDTH), jnp.float32, 0.9, 0.999)
    a0 = u ** (1.0 / RG_LRU_C)
    lru_lambda = jnp.log(a0) - jnp.log1p(-a0)
    return {
        "x": x,
        "norm_ffn1": gain((DEPTH, D_MODEL)),
        "ffn1_wg": nrm((DEPTH, D_MODEL, D_FF), D_MODEL ** -0.5),
        "ffn1_wu": nrm((DEPTH, D_MODEL, D_FF), D_MODEL ** -0.5),
        "ffn1_wd": nrm((DEPTH, D_FF, D_MODEL), D_FF ** -0.5),
        "norm_mix": gain((DEPTH, D_MODEL)),
        "norm_ffn2": gain((DEPTH, D_MODEL)),
        "ffn2_wg": nrm((DEPTH, D_MODEL, D_FF), D_MODEL ** -0.5),
        "ffn2_wu": nrm((DEPTH, D_MODEL, D_FF), D_MODEL ** -0.5),
        "ffn2_wd": nrm((DEPTH, D_FF, D_MODEL), D_FF ** -0.5),
        "rel_bias": nrm((NUM_BUCKETS, N_Q_HEADS), 0.3),
        "even_w_in": nrm((N_EVEN, D_MODEL, EVEN_IN), D_MODEL ** -0.5),
        "attn_sinks": nrm((N_EVEN, N_Q_HEADS), 1.0),
        "conv_b_w": nrm((N_EVEN, CONV_WIDTH, CONV_CHANNELS), CONV_WIDTH ** -0.5),
        "conv_b_b": nrm((N_EVEN, CONV_CHANNELS), 0.02),
        "conv_ln_g": gain((N_EVEN, CONV_CHANNELS)),
        "conv_ln_b": nrm((N_EVEN, CONV_CHANNELS), 0.02),
        "even_w_out": nrm((N_EVEN, EVEN_CAT, D_MODEL), EVEN_CAT ** -0.5),
        "odd_w_in": nrm((N_ODD, D_MODEL, 2 * LRU_WIDTH), D_MODEL ** -0.5),
        "lru_conv_w": nrm((N_ODD, LRU_CONV_WIDTH, LRU_WIDTH), LRU_CONV_WIDTH ** -0.5),
        "lru_conv_b": nrm((N_ODD, LRU_WIDTH), 0.02),
        "gate_a_w": nrm((N_ODD, LRU_HEADS, LRU_BLOCK, LRU_BLOCK), LRU_BLOCK ** -0.5),
        "gate_a_b": nrm((N_ODD, LRU_WIDTH), 0.02),
        "gate_x_w": nrm((N_ODD, LRU_HEADS, LRU_BLOCK, LRU_BLOCK), LRU_BLOCK ** -0.5),
        "gate_x_b": nrm((N_ODD, LRU_WIDTH), 0.02),
        "lru_lambda": lru_lambda,
        "odd_w_out": nrm((N_ODD, LRU_WIDTH, D_MODEL), LRU_WIDTH ** -0.5),
        "norm_final": gain((D_MODEL,)),
    }

def second_block(x, norm_ffn1, ffn1_wg, ffn1_wu, ffn1_wd, norm_mix, norm_ffn2, ffn2_wg, ffn2_wu, ffn2_wd,
              rel_bias, even_w_in, attn_sinks, conv_b_w, conv_b_b, conv_ln_g, conv_ln_b, even_w_out,
              odd_w_in, lru_conv_w, lru_conv_b, gate_a_w, gate_a_b, gate_x_w, gate_x_b, lru_lambda,
              odd_w_out, norm_final):
    h = x
    for layer in range(DEPTH):
        h = h + 0.5 * _swiglu(_rmsnorm(h, norm_ffn1[layer]), ffn1_wg[layer], ffn1_wu[layer], ffn1_wd[layer])
        hn = _rmsnorm(h, norm_mix[layer])
        if layer % 2 == 0:
            e = layer // 2
            h = h + _attn_conv_mixer(hn, even_w_in[e], attn_sinks[e], conv_b_w[e], conv_b_b[e],
                                     conv_ln_g[e], conv_ln_b[e], even_w_out[e], rel_bias)
        else:
            o = layer // 2
            h = h + _recurrent_mixer(hn, odd_w_in[o], lru_conv_w[o], lru_conv_b[o], gate_a_w[o],
                                     gate_a_b[o], gate_x_w[o], gate_x_b[o], lru_lambda[o], odd_w_out[o])
        h = h + 0.5 * _swiglu(_rmsnorm(h, norm_ffn2[layer]), ffn2_wg[layer], ffn2_wu[layer], ffn2_wd[layer])
    return _rmsnorm(h, norm_final)


def setup_inputs(seed=0):
    out = dict(first_inputs(seed))
    for name, value in second_inputs(seed + 1).items():
        if name != "x":
            out[name + "_2"] = value
    return out


def reference(
    x, p, positions, norm_mix, pool_w, pool_scale, norm_kv, w_kv, cmp_pos_k, cmp_w1_k, cmp_w2_k,
    cmp_pos_v, cmp_w1_v, cmp_w2_v, w_in_b, w_out_b, norm_ffn, ffn_up, ffn_conv, ffn_conv_b,
    ffn_down, norm_ple, ple_gate, ple_proj, norm_final, norm_ffn1_2, ffn1_wg_2, ffn1_wu_2,
    ffn1_wd_2, norm_mix_2, norm_ffn2_2, ffn2_wg_2, ffn2_wu_2, ffn2_wd_2, rel_bias_2,
    even_w_in_2, attn_sinks_2, conv_b_w_2, conv_b_b_2, conv_ln_g_2, conv_ln_b_2, even_w_out_2,
    odd_w_in_2, lru_conv_w_2, lru_conv_b_2, gate_a_w_2, gate_a_b_2, gate_x_w_2, gate_x_b_2,
    lru_lambda_2, odd_w_out_2, norm_final_2,
):
    x = first_block(
        x, p, positions, norm_mix, pool_w, pool_scale, norm_kv, w_kv, cmp_pos_k, cmp_w1_k,
        cmp_w2_k, cmp_pos_v, cmp_w1_v, cmp_w2_v, w_in_b, w_out_b, norm_ffn, ffn_up, ffn_conv,
        ffn_conv_b, ffn_down, norm_ple, ple_gate, ple_proj, norm_final,
    )
    return second_block(
        x, norm_ffn1_2, ffn1_wg_2, ffn1_wu_2, ffn1_wd_2, norm_mix_2, norm_ffn2_2, ffn2_wg_2,
        ffn2_wu_2, ffn2_wd_2, rel_bias_2, even_w_in_2, attn_sinks_2, conv_b_w_2, conv_b_b_2,
        conv_ln_g_2, conv_ln_b_2, even_w_out_2, odd_w_in_2, lru_conv_w_2, lru_conv_b_2,
        gate_a_w_2, gate_a_b_2, gate_x_w_2, gate_x_b_2, lru_lambda_2, odd_w_out_2, norm_final_2,
    )


_drawn_inputs = setup_inputs


def setup_inputs(seed=0):
    import zlib

    import numpy as np

    out = dict(_drawn_inputs(seed))
    spreads = {}
    factors = {'norm_kv': 4.431,
     'cmp_pos_k': 8.0,
     'ffn_conv_b': 2.669,
     'norm_ple': 5.079,
     'norm_ffn1_2': 4.685,
     'norm_mix_2': 3.375,
     'norm_ffn2_2': 5.568,
     'attn_sinks_2': 27.675,
     'conv_ln_g_2': 22.066,
     'conv_ln_b_2': 22.727,
     'gate_a_b_2': 47.764,
     'gate_x_b_2': 31.503,
     'norm_final_2': 22.041,
     'conv_b_b_2': 8.0,
     'lru_conv_b_2': 4.387,
     'rel_bias_2': 3.17}
    for name, (base, spread) in spreads.items():
        noise = np.random.default_rng([zlib.crc32(name.encode()), seed]).standard_normal(out[name].shape)
        drawn = base * np.exp(spread * noise) if base else spread * noise
        out[name] = jnp.asarray(drawn.astype(out[name].dtype))
    for name, factor in factors.items():
        out[name] = (out[name] * factor).astype(out[name].dtype)
    return out
```

```python
from contextlib import ExitStack

import concourse.bass as bass
import numpy as np
from concourse import mybir

F32 = mybir.dt.float32
F32R = mybir.dt.float32r
BF16 = mybir.dt.bfloat16
I32 = mybir.dt.int32
ALU = mybir.AluOpType
ACT = mybir.ActivationFunctionType
AX = mybir.AxisListType.X

P = 128
T = 512
NT = T // P
D = 1024
ND = D // P
DFF = 2816
NF = DFF // P
HALF_F = NF // 2
SLOT = 16
EPS = 1e-6
LN_EPS = 1e-5
NEG = -1e30
HD = 64
QK_SCALE = HD ** -0.5
POOL_WINDOWS = (2, 4, 8, 16)
NH = 16
NG = 4
CS = 16
NCMP = T // CS - 1
NC = 32
TAPS = 31
PAD = 3
CC = 4
BLOCK_F = 383
MAGIC = 12582912.0
TWO_PI = float(2 * np.pi)
PI32 = 3.1415925
C1 = 6.28125
C2 = float(np.float32(np.floor((TWO_PI - C1) * 2 ** 20) / 2 ** 20))
C3 = float(np.float32(TWO_PI - C1 - C2))

VEC_LIST = [
    ("mix0", 8), ("pool_scale", 8), ("ffn0", 8), ("ple0", 8), ("kv", 8), ("mix1", 8), ("ffn1", 8), ("ple1", 8),
    ("final1", 8), ("conv0_0", 44), ("conv0_1", 44), ("conv0_2", 44), ("conv0_b", 44),
    ("conv1_0", 44), ("conv1_1", 44), ("conv1_2", 44), ("conv1_b", 44),
    ("ffn2", 8), ("mixe", 8), ("ffn3", 8), ("ffn4", 8), ("mixo", 8), ("ffn5", 8), ("final2", 8),
    ("cb_w", TAPS * CC), ("cb_b", 4), ("ln_g", 4), ("ln_b", 4), ("lru_w", 32), ("lru_b", 8), ("ga_b", 8),
    ("gx_b", 8), ("lam", 8), ("freq", 1),
]
VC, _at = {}, 0
for _name, _n in VEC_LIST:
    VC[_name] = _at
    _at += _n
NVEC = _at

STAGES = [("pool", 1, 16, 8)]
for _l in range(2):
    if _l == 1:
        STAGES += [("kproj", 4, 16, 2), ("vproj", 2, 16, 0), ("gates", 1, 3, 4), ("qproj", 4, 16, 2),
                   ("wout0", 4, 16, 2)]
    STAGES += [(f"up{_l}", 22, 16, 2), (f"down{_l}", 16, 11, 1), (f"ple{_l}", 8, 10, 2)]
STAGES += [("up2", 22, 16, 2), ("down2", 16, 11, 1), ("ein", 6, 16, 2), ("einv", 1, 16, 5), ("wout1", 4, 16, 2),
           ("up3", 22, 16, 2), ("down3", 16, 11, 1), ("up4", 22, 16, 2), ("down4", 16, 11, 1),
           ("rec", 4, 16, 2), ("lgate", 1, 16, 16), ("ogate", 4, 16, 2), ("wout2", 4, 16, 2),
           ("up5", 22, 16, 2), ("down5", 16, 11, 1)]
J0, TILES, SEGS_BEFORE = {}, [], [0]
for _name, _jobs, _tiles, _segs in STAGES:
    J0[_name] = len(TILES)
    for _j in range(_jobs):
        TILES.append(_tiles)
        SEGS_BEFORE.append(SEGS_BEFORE[-1] + ({0: 1, 1: 4}[_j] if _name == "vproj" else _segs))
NJOBS = len(TILES)
JOBS_OF = {n: j for n, j, _, _ in STAGES}
SEG0 = {n: SEGS_BEFORE[J0[n]] for n, _, _, _ in STAGES}

PREPS = ["start", "up0", "ple0", "kv", "up1", "ple1", "final1", "up2", "mixe", "up3", "up4", "mixo", "up5", "final2"]
GAIN = {"up0": "ffn0", "ple0": "ple0", "kv": "kv", "up1": "ffn1", "ple1": "ple1", "up2": "ffn2", "mixe": "mixe",
        "up3": "ffn3", "up4": "ffn4", "mixo": "mixo", "up5": "ffn5"}
PREP_OF = {n: i for i, n in enumerate(PREPS)}
H_COUNT = {}
_at = 0
for _name in PREPS:
    H_COUNT[_name] = _at
    if _name in GAIN:
        _at += ND

ACC_READS = {"pool": 0, "up": 44, "down": 0, "ple": 16, "kproj": 8, "vproj": 4, "gates": 4, "qproj": 8, "wout": 0,
             "ein": 12, "einv": 5, "rec": 8, "lgate": 0, "ogate": 8}
FREE0, _at = {}, 4
for _name, _, _, _ in STAGES:
    FREE0[_name] = _at
    _at += ACC_READS[_name.rstrip("0123456789")]


STAGE_ORDER = []
for _name, _, _, _ in STAGES:
    STAGE_ORDER.append(_name)
    if _name == "qproj":
        STAGE_ORDER.append("attn")
    if _name == "ple1":
        STAGE_ORDER.append("final1")
STAGE_ORDER.append("final2")
NEXT_PREP = {"pool": "up0", "down0": "ple0", "ple0": "kv", "wout0": "up1", "down1": "ple1", "ple1": "final1",
             "final1": "up2", "down2": "mixe", "wout1": "up3", "down3": "up4", "down4": "mixo", "wout2": "up5",
             "down5": "final2"}
POOL_U, _at = [], ND
for _g in range(len(POOL_WINDOWS)):
    _at += _g + 3
    POOL_U.append(_at)
ROPE_FREE = [FREE0["kproj"] + 5 + _r for _r in range(4)] + [None] + [FREE0["qproj"] + 1 + _r for _r in range(8)]
CS_STEPS = 12
UNITS = 2 * NH
LAM_STEPS = 18
E_SCALED0, E_TURNED0, E_PV0, E_EXP0, E_KEPT_A0, E_FAC0 = 4 * UNITS, 4 * UNITS, 4 * UNITS, 4 * UNITS, 2 * UNITS, 2 * UNITS


def head_of(c, half):
    g = 2 * (c // 4) + half
    return g, 4 * g + c % 4


def unit(u):
    c, half, b = u // 4, u // 2 % 2, u % 2
    return (c, half, b, *head_of(c, half))


def x_before(prep):
    return ND * (PREP_OF[prep] - 1)


def pairs(eng, n, body):
    if n > 2:
        with eng.Fori(0, n - 1) as i:
            body(i)
        body(n - 1)
    else:
        for i in range(n):
            body(i)


def build(nc, a, stop_after=None):
    with ExitStack() as ctx:
        def sb(name, shape, dt=F32, to=ctx):
            return to.enter_context(nc.sbuf_tensor(name, shape, dt))

        def sem(name):
            return ctx.enter_context(nc.semaphore(name))

        x = sb("x", [P, ND, T])
        h_hi = sb("h_hi", [P, ND, T], F32R)
        h_lo = sb("h_lo", [P, ND, T], F32R)
        w_raw = [sb(f"w_raw{s}", [P, SLOT * P]) for s in range(2)]
        w_hi = [sb(f"w_hi{s}", [P, SLOT * P], F32R) for s in range(2)]
        w_lo = [sb(f"w_lo{s}", [P, SLOT * P], F32R) for s in range(2)]
        vec = sb("vec", [P, NVEC])
        rs = sb("rs", [P, T])
        sq = sb("sq", [P, T])
        sq_sum = sb("sq_sum", [P, T])
        taps_in = sb("taps_in", [P, 2, PAD + T])
        silu_g = sb("silu_g", [P, T])
        hid = sb("hid", [P, 2, T])
        ones = sb("ones", [P, P])
        ident = sb("ident", [P, P])
        eps = sb("eps", [P, 2])

        with ExitStack() as part:
            pool_h = sb("pool_h", [P, ND, CS + T], to=part)
            pool_w = [sb(f"pool_w{i}", [P, 2, CS + T], to=part) for i in range(2)]
            pool_u = sb("pool_u", [P, 2, 2, T], to=part)
            pool_fix = sb("pool_fix", [P, 4, CS], to=part)
            pool_tap = sb("pool_tap", [P, 1], to=part)
        with ExitStack() as part:
            act_hi = sb("act_hi", [P, NF, T], F32R, to=part)
            act_lo = sb("act_lo", [P, NF, T], F32R, to=part)
        with ExitStack() as part:
            p_hi = sb("p_hi", [P, 2, T], F32R, to=part)
            p_lo = sb("p_lo", [P, 2, T], F32R, to=part)
            ple_t = sb("ple_t", [P, 2, T], to=part)
        with ExitStack() as part:
            o_hi = sb("o_hi", [P, ND, T], F32R, to=part)
            o_lo = sb("o_lo", [P, ND, T], F32R, to=part)
            with ExitStack() as sub:
                cw1 = sb("cw1", [P, 2, CS, P], to=sub)
            qT = sb("qT", [P, ND, T], to=part)
            kT = sb("kT", [P, 4, T], to=part)
            vsw = sb("vsw", [P, NT, T], to=part)
            kcT = sb("kcT", [P, NG, NC], to=part)
            vcm = sb("vcm", [P, NG, HD], to=part)
            gates = sb("gates", [P, NT, 48], to=part)
            rs_col = sb("rs_col", [P, NT], to=part)
            cmask = sb("cmask", [P, 2, NT, NC], to=part)
            cw2 = sb("cw2", [P, 3, HD], to=part)
            cpos = sb("cpos", [P, 2, CS], to=part)
            cpos_b = sb("cpos_b", [P, 2], to=part)
            rot = sb("rot", [P, P], to=part)
            mask_bf = sb("mask_bf", [P, 2, P], BF16, to=part)
            stat4 = sb("stat4", [P, 2, 4, NT], to=part)
            cstat = sb("cstat", [P, 2, 2, NH], to=part)
            with ExitStack() as sub:
                rcos = sb("rcos", [P, T], to=sub)
                rsin = sb("rsin", [P, T], to=sub)
                with ExitStack() as sub2:
                    pos_i = sb("pos_i", [P, T], I32, to=sub2)
                    ang = [sb(f"ang{i}", [P, T], to=sub2) for i in range(4)]
                kvc = sb("kvc", [P, 2, NG, T], to=sub)
            with ExitStack() as sub:
                pcT = sb("pcT", [P, NG, T], to=sub)
                probs = [sb(f"probs{i}", [P, 10 * P], to=sub) for i in range(2)]
        with ExitStack() as part:
            e_hi = sb("e_hi", [P, ND, T], F32R, to=part)
            e_lo = sb("e_lo", [P, ND, T], F32R, to=part)
            eq = sb("eq", [P, 5, T], to=part)
            ev = sb("ev", [P, NT, P], to=part)
            e_rs = sb("e_rs", [P, NT], to=part)
            ebias = sb("ebias", [P, 8, 2 * P], to=part)
            glu = sb("glu", [P, CC, TAPS - 1 + T], to=part)
            cy = sb("cy", [P, CC, T], to=part)
            eprobs = [sb(f"eprobs{i}", [P, NT, 2 * P], to=part) for i in range(2)]
            estat = sb("estat", [P, 2, 4, NT], to=part)
            sinks = sb("sinks", [P, 8], to=part)
            with ExitStack() as sub:
                relb = sb("relb", [32, 8], to=sub)
                onehot = sb("onehot", [32, BLOCK_F + 1], to=sub)
                outside = sb("outside", [8, BLOCK_F + 1], to=sub)
                diag = sb("diag", [8, BLOCK_F + 1], to=sub)
                flip = sb("flip", [P, P], to=sub)
        with ExitStack() as part:
            r_hi = sb("r_hi", [P, ND, T], F32R, to=part)
            r_lo = sb("r_lo", [P, ND, T], F32R, to=part)
            rc = sb("rc", [P, ND, T], to=part)
            ra = sb("ra", [P, ND, T], to=part)
            ri = sb("ri", [P, ND, T], to=part)
            sp4 = sb("sp4", [P, ND], to=part)
            sp8 = sb("sp8", [P, ND], to=part)
            expv = sb("expv", [P, 4, T], to=part)
            lt = sb("lt", [P, 6, ND], to=part)

        bank = [ctx.enter_context(nc.psum_tensor(f"bank{i}", [P, T], F32)) for i in range(8)]
        STAT, CONV_A, CONV_G, MISC = 4, 5, 6, 7
        scratch = nc.dram_tensor("diag_scratch", [8 * (BLOCK_F + 1)], F32, kind="Internal")

        x_loaded, vec_loaded = sem("x_loaded"), sem("vec_loaded")
        w_loaded = [sem("w_loaded0"), sem("w_loaded1")]
        w_hi_done, w_lo_done = sem("w_hi_done"), sem("w_lo_done")
        const_set = sem("const_set")
        ident_set = sem("ident_set")
        seg_done = sem("seg_done")
        acc_free = sem("acc_free")
        x_ready = sem("x_ready")
        h_hi_done, h_lo_done = sem("h_hi_done"), sem("h_lo_done")
        sq_done, sq_added = sem("sq_done"), sem("sq_added")
        stat_done, root_done, rs_done = sem("stat_done"), sem("root_done"), sem("rs_done")
        seeded, tapped, silu_done, hid_done = sem("seeded"), sem("tapped"), sem("silu_done"), sem("hid_done")
        act_hi_done, act_lo_done = sem("act_hi_done"), sem("act_lo_done")
        p_loaded, p_hi_done, p_lo_done = sem("p_loaded"), sem("p_hi_done"), sem("p_lo_done")
        sig_done, prod_done = sem("sig_done"), sem("prod_done")
        pool_step, pool_hi_done, pool_lo_done = sem("pool_step"), sem("pool_hi_done"), sem("pool_lo_done")
        aux_loaded, pos_loaded = sem("aux_loaded"), sem("pos_loaded")
        trig_step, sin_done = sem("trig_step"), sem("sin_done")
        h2_hi_done, h2_lo_done = sem("h2_hi_done"), sem("h2_lo_done")
        kvc_done = sem("kvc_done")
        rot_done, cos_mul, sin_mul, roped = sem("rot_done"), sem("cos_mul"), sem("sin_mul"), sem("roped")
        rs_turned, rs_col_done = sem("rs_turned"), sem("rs_col_done")
        gates_done = sem("gates_done")
        cmp_mm, cmp_act, cmp_vec = sem("cmp_mm"), sem("cmp_act"), sem("cmp_vec")
        cs_mm, cs_vec, cs_exp, cs_turned, cs_kept = (sem(n) for n in ("cs_mm", "cs_vec", "cs_exp", "cs_turned", "cs_kept"))
        qk_done, max_done, nmax_done, exp_done = sem("qk_done"), sem("max_done"), sem("nmax_done"), sem("exp_done")
        fac_done, scaled, turned = sem("fac_done"), sem("scaled"), sem("turned")
        kept_v, kept_a, pv_done = sem("kept_v"), sem("kept_a"), sem("pv_done")
        o_hi_done, o_lo_done = sem("o_hi_done"), sem("o_lo_done")
        e_loaded, diag_mm, diag_vec, diag_out, diag_in, flipped, bias_kept = (
            sem(n) for n in ("e_loaded", "diag_mm", "diag_vec", "diag_out", "diag_in", "flipped", "bias_kept"))
        glu_sig, glu_done, y_seed, y_tap = sem("glu_sig"), sem("glu_done"), sem("y_seed"), sem("y_tap")
        ln_add, ln_mm, ln_vec, ln_sq, ln_act, ln_hi, ln_lo = (
            sem(n) for n in ("ln_add", "ln_mm", "ln_vec", "ln_sq", "ln_act", "ln_hi", "ln_lo"))
        u_done, r_seed, r_tap, rc_hi, rc_lo = (sem(n) for n in ("u_done", "r_seed", "r_tap", "rc_hi", "rc_lo"))
        lam_vec, lam_act, g_sig, lru_act, lru_vec = (sem(n) for n in ("lam_vec", "lam_act", "g_sig", "lru_act", "lru_vec"))
        gel_done, y_done, y_hi, y_lo, e_norm, glu_zero = (sem(n) for n in ("gel_done", "y_done", "y_hi", "y_lo", "e_norm", "glu_zero"))
        out_ready, stored = sem("out_ready"), sem("stored")

        def col(name, m):
            at = VC[name] + m
            return vec[:, at:at + 1] if isinstance(at, int) else vec[:, bass.ds(at, 1)]

        enabled = STAGE_ORDER if stop_after is None else STAGE_ORDER[:STAGE_ORDER.index(stop_after) + 1]
        n_jobs = max([J0[s] + JOBS_OF[s] for s in enabled if s in J0])

        def job_tiles(j):
            return TILES[j] * P

        block = ctx.enter_context(nc.Block())

        @block.sync
        def _(sp):
            sp.dma_start(x[:], a["x"]).then_inc(x_loaded, 16)
            sp.dma_start(vec[:], a["vec"]).then_inc(vec_loaded, 16)
            sp.dma_start(ident[:], a["consts"][:, 0:P]).then_inc(vec_loaded, 16)
            sp.dma_start(pool_fix[:], a["pool_fix"]).then_inc(vec_loaded, 16)

            def load(stage, q, u):
                j = J0[stage] + u
                n = TILES[j] * P
                if j >= 1:
                    sp.wait_ge(w_lo_done, J0[stage] + q - 1)
                sp.dma_start(w_raw[j % 2][:, 0:n], a["w_" + stage][q]).then_inc(w_loaded[j % 2], 16)

            def load_all(stage):
                n = JOBS_OF[stage]
                if n < 8:
                    for q in range(n):
                        load(stage, q, q)
                else:
                    pairs(sp, n // 2, lambda i: [load(stage, 2 * i + u, u) for u in range(2)])

            ffn_seen = 0
            for stage in enabled:
                if stage in J0:
                    load_all(stage)
                if stage in ("down0", "down1"):
                    l = int(stage[-1])
                    sp.wait_ge(hid_done, NF * (l + 1))
                    sp.dma_start(taps_in[:, :, PAD:], a["p"][l]).then_inc(p_loaded, 16)
                if stage == "ple0" and "kproj" in enabled:
                    sp.wait_ge(w_lo_done, J0["ple0"] + 4)
                    for i, n in enumerate(("cmp_w1_k", "cmp_w1_v")):
                        sp.dma_start(cw1[:, i], a[n]).then_inc(aux_loaded, 16)
                    for i, n in enumerate(("cmp_w2_k", "cmp_w2_k", "cmp_w2_v")):
                        sp.dma_start(cw2[:, i], a[n]).then_inc(aux_loaded, 16)
                    for i, n in enumerate(("cmp_pos_k", "cmp_pos_v")):
                        sp.dma_start(cpos[:, i], a[n]).then_inc(aux_loaded, 16)
                    sp.dma_start(rot[:], a["consts"][:, P:2 * P]).then_inc(aux_loaded, 16)
                    sp.dma_start(mask_bf[:], a["mask_bf"]).then_inc(aux_loaded, 16)
                    sp.dma_start(cmask[:], a["cmask"]).then_inc(aux_loaded, 16)
                    sp.dma_start(pos_i[:], a["positions"].broadcast_to([P, T])).then_inc(pos_loaded, 16)
                if stage == "ein":
                    sp.wait_ge(seg_done, SEG0["ein"])
                    sp.dma_start(sinks[:], a["sinks"].broadcast_to([P, 8])).then_inc(e_loaded, 16)
                    sp.dma_start(relb[:], a["rel_bias"]).then_inc(e_loaded, 16)
                    sp.dma_start(onehot[:], a["onehot"]).then_inc(e_loaded, 16)
                    sp.dma_start(outside[:], a["outside"]).then_inc(e_loaded, 16)
                    sp.dma_start(flip[:], a["consts"][:, 2 * P:3 * P]).then_inc(e_loaded, 16)
                if stage == "einv":
                    sp.wait_ge(diag_vec, 1)
                    sp.dma_start(scratch.ap().rearrange("(h d) -> h d", h=8), diag[:]).then_inc(diag_out, 16)
                    sp.wait_ge(diag_out, 16)
                    spread = bass.AP(tensor=scratch.ap().tensor, offset=0, ap=[[1, P], [BLOCK_F + 1, 8], [1, 2 * P]])
                    sp.dma_start(ebias[:], spread).then_inc(diag_in, 16)
            if stop_after is None:
                for m in range(ND):
                    sp.wait_ge(out_ready, m + 1)
                    sp.dma_start(a["out"][m], x[:, m, :]).then_inc(stored, 16)
                sp.wait_ge(stored, 16 * ND)
            else:
                sp.wait_ge(x_ready, x_before(NEXT_PREP[stop_after]) + ND)
                sp.dma_start(a["out"].rearrange("m p t -> p m t"), x[:]).then_inc(stored, 16)
                sp.wait_ge(stored, 16)

        @block.tensor
        def _(pe):
            def three(out, wh, wl, mh, ml, first, final):
                pe.matmul(out, wh, mh, start=first, stop=False)
                pe.matmul(out, wh, ml, start=False, stop=False)
                return pe.matmul(out, wl, mh, start=False, stop=final)

            def tile_of(slot, n):
                return w_hi[slot][:, n * P:(n + 1) * P], w_lo[slot][:, n * P:(n + 1) * P]

            def stats(prep):
                n = PREP_OF[prep]
                if n == 0:
                    pe.wait_ge(const_set, 3)
                pe.wait_ge(sq_added, 9 * (n + 1))
                pe.matmul(bank[STAT][:], ones[:], sq_sum[:], start=True, stop=True).then_inc(stat_done, 1)

            def up(n):
                stage = f"up{n}"
                stats(stage)

                def body(i):
                    for u in range(2):
                        f, slot = 2 * i + u, (J0[stage] + u) % 2
                        pe.wait_ge(w_lo_done, J0[stage] + f + 1)
                        for g in range(2):
                            pe.wait_ge(acc_free, FREE0[stage] + 2 * f + g - 3)
                            for k in range(ND):
                                if u == 0 and g == 0:
                                    pe.wait_ge(h_lo_done, H_COUNT[stage] + k + 1)
                                mm = three(bank[2 * u + g][:], *tile_of(slot, g * ND + k), h_hi[:, k], h_lo[:, k],
                                           k == 0, k == ND - 1)
                            mm.then_inc(seg_done, 1)
                pairs(pe, NF // 2, body)

            def down(n):
                stage, nxt = f"down{n}", NEXT_PREP[f"down{n}"]
                pe.wait_ge(acc_free, FREE0[stage])

                def body(i):
                    for u in range(4):
                        m, half, slot = 2 * i + u // 2, u % 2, (J0[stage] + u) % 2
                        pe.wait_ge(w_lo_done, J0[stage] + 4 * i + u + 1)
                        if half == 0:
                            pe.wait_ge(x_ready, x_before(nxt) + m - 1)
                        pe.wait_ge(act_lo_done, NF * n + HALF_F * (half + 1) + 1)
                        for k in range(HALF_F):
                            kk = half * HALF_F + k
                            mm = three(bank[u // 2][:], *tile_of(slot, k), act_hi[:, kk], act_lo[:, kk],
                                       kk == 0, kk == NF - 1)
                        mm.then_inc(seg_done, 1)
                pairs(pe, ND // 2, body)

            def ple(l):
                stage = f"ple{l}"
                stats(stage)

                def body(i):
                    for u in range(2):
                        m, slot = 2 * i + u, (J0[stage] + u) % 2
                        pe.wait_ge(w_lo_done, J0[stage] + m + 1)
                        pe.wait_ge(acc_free, FREE0[stage] + 2 * m - 3)
                        for k in range(ND):
                            if u == 0:
                                pe.wait_ge(h_lo_done, H_COUNT[stage] + k + 1)
                            mm = three(bank[2 * u][:], *tile_of(slot, k), h_hi[:, k], h_lo[:, k], k == 0, k == ND - 1)
                        mm.then_inc(seg_done, 1)
                        pe.wait_ge(acc_free, FREE0[stage] + 2 * m - 2)
                        pe.wait_ge(p_lo_done, 2 * (l + 1))
                        for k in range(2):
                            mm = three(bank[2 * u + 1][:], *tile_of(slot, ND + k), p_hi[:, k], p_lo[:, k], k == 0, k == 1)
                        mm.then_inc(seg_done, 1)
                pairs(pe, ND // 2, body)

            def dense(stage, q, hi, lo, ready, base, residual=None, after=None):
                j = J0[stage] + q
                pe.wait_ge(w_lo_done, j + 1)
                for g in range(2):
                    n = 2 * q + g
                    if residual is None:
                        pe.wait_ge(acc_free, FREE0[stage] + n - 3)
                    elif n >= 4:
                        pe.wait_ge(x_ready, x_before(residual) + n - 3)
                    for k in range(ND):
                        if n == 0:
                            pe.wait_ge(ready, base + k + 1)
                        mm = three(bank[n % 4][:], *tile_of(j % 2, g * ND + k), hi[:, k], lo[:, k], k == 0, k == ND - 1)
                    mm.then_inc(seg_done, 1)
                    if after is not None:
                        after(n)

            def rotate(r, width=T):
                pe.wait_ge(cmp_vec if r == 4 else acc_free, 2 if r == 4 else ROPE_FREE[r])
                if r >= 2:
                    pe.wait_ge(roped, r - 1)
                pe.matmul(bank[5 + r % 2][:, 0:width], rot[:], hid[:, r % 2, 0:width], start=True, stop=True)\
                    .then_inc(rot_done, 1)

            def turn_rs(count):
                pe.wait_ge(rs_done, count)
                for t in range(NT):
                    mm = pe.transpose(bank[MISC][:, t * P:(t + 1) * P], rs[:, t * P:(t + 1) * P], ident[:])
                mm.then_inc(rs_turned, 1)

            def pool():
                stats("start")
                pe.wait_ge(w_lo_done, 1)
                for m in range(ND):
                    if m >= 4:
                        pe.wait_ge(x_ready, m - 3)
                    for k in range(2):
                        if m % 2 == 0:
                            pe.wait_ge(pool_lo_done, m + k + 1)
                        mm = three(bank[m % 4][:], *tile_of(0, 2 * m + k), h_hi[:, m // 2 * 2 + k],
                                   h_lo[:, m // 2 * 2 + k], k == 0, k == 1)
                    mm.then_inc(seg_done, 1)

            def attention_inputs():
                pe.wait_ge(aux_loaded, 16 * 10)
                stats("kv")
                for q in range(4):
                    dense("kproj", q, h_hi, h_lo, h_lo_done, H_COUNT["kv"],
                          after=lambda n: rotate(n - 5) if n >= 5 else None)
                turn_rs(PREP_OF["kv"] + 1)
                for q in range(2):
                    j = J0["vproj"] + q
                    pe.wait_ge(w_lo_done, j + 1)
                    for kk in range(4):
                        k = 4 * q + kk
                        for t in range(NT):
                            if k == 0:
                                pe.wait_ge(acc_free, FREE0["vproj"] + t - 3)
                            cols = slice(t * P, (t + 1) * P)
                            w = slice(kk * T, (kk + 1) * T)
                            mm = three(bank[t][:], h_hi[:, k, cols], h_lo[:, k, cols], w_hi[j % 2][:, w],
                                       w_lo[j % 2][:, w], k == 0, k == ND - 1)
                            if k == ND - 1 or (k == 3 and t == NT - 1):
                                mm.then_inc(seg_done, 1)
                        if k == 0:
                            rotate(3)
                j = J0["gates"]
                pe.wait_ge(w_lo_done, j + 1)
                pe.wait_ge(h2_lo_done, ND)
                for t in range(NT):
                    pe.wait_ge(acc_free, FREE0["gates"] + t - 3)
                    for k in range(ND):
                        cols, w = slice(t * P, (t + 1) * P), slice(k * 48, (k + 1) * 48)
                        mm = three(bank[t][:, 0:48], o_hi[:, k, cols], o_lo[:, k, cols], w_hi[j % 2][:, w],
                                   w_lo[j % 2][:, w], k == 0, k == ND - 1)
                    mm.then_inc(seg_done, 1)
                pe.wait_ge(acc_free, FREE0["kproj"] + 4)
                for i in range(2):
                    for jj in range(CS):
                        pe.matmul(bank[STAT][:, 256 + i:257 + i], cw1[:, i, jj], cpos[:, i, jj:jj + 1],
                                  start=jj == 0, stop=jj == CS - 1)
                    for jj in range(CS):
                        blocks = kvc[:, i, :, 2 * jj:2 * jj + CS * (NCMP - 1) + 1:CS]
                        mm = pe.matmul(bank[STAT][:, 128 * i:128 * i + NG * NCMP], cw1[:, i, jj], blocks,
                                       start=jj == 0, stop=jj == CS - 1)
                    mm.then_inc(cmp_mm, 1)
                dense("qproj", 0, o_hi, o_lo, h2_lo_done, 0)
                pe.wait_ge(cmp_act, 6)
                pe.wait_ge(cmp_vec, 1)
                pe.matmul(bank[MISC][:, 0:NG * NC], cw2[:, 0:2].rearrange("p a d -> p (a d)"),
                          taps_in[:, 0, PAD:PAD + NG * NC], start=True, stop=True)
                for g in range(NG):
                    at = PAD + g * P
                    mm = pe.matmul(bank[MISC][:, P + g * HD:P + (g + 1) * HD], taps_in[:, 1, at:at + P], cw2[:, 2],
                                   start=True, stop=True)
                mm.then_inc(cmp_mm, 1)
                for q in range(1, 4):
                    def after(n):
                        if n == 2:
                            rotate(4, NG * NC)
                        rotate(5 + n - 2)
                        if n == 7:
                            rotate(11)
                            rotate(12)
                    dense("qproj", q, o_hi, o_lo, h2_lo_done, 0, after=after)

            def attention():
                pe.wait_ge(roped, 13)
                pe.wait_ge(acc_free, FREE0["qproj"] + 8)

                def cscores(t):
                    for c in range(ND):
                        for half in range(2):
                            rows = slice(half * HD, (half + 1) * HD)
                            g, s = head_of(c, half)
                            mm = pe.matmul(bank[4 * half + t][:, s * NC:(s + 1) * NC], qT[rows, c, t * P:(t + 1) * P],
                                           kcT[rows, g], start=True, stop=True)
                    mm.then_inc(cs_mm, 1)

                for t in range(NT):
                    cscores(t)
                for t in range(NT):
                    pe.wait_ge(cs_vec, CS_STEPS * t + CS_STEPS)
                    if t >= 2:
                        pe.wait_ge(cs_kept, t - 1)
                    for g in range(NG):
                        mm = pe.transpose(bank[4 + t % 2][:, g * P:(g + 1) * P], hid[:, t % 2, g * P:(g + 1) * P],
                                          ident[:])
                    mm.then_inc(cs_turned, 1)

                def qk(u):
                    c, half, b, g, s = unit(u)
                    rows = slice(half * HD, (half + 1) * HD)
                    for t in range(NT):
                        n = (t + 1) * P
                        if u >= 1:
                            pe.wait_ge(exp_done, 4 * (u - 1) + t + 1)
                        else:
                            pe.wait_ge(cs_vec, CS_STEPS * t + 4)
                        pe.matmul(bank[t][:, 0:n], qT[rows, c, t * P:(t + 1) * P], kT[rows, 2 * b + g // 2, 0:n],
                                  start=True, stop=False)
                        pe.matmul(bank[t][:, t * P:n], mask_bf[:, 0], mask_bf[:, 1], start=False, stop=True)\
                            .then_inc(qk_done, 1)

                def turn(u, kb):
                    n = 4 * u + kb
                    if kb == 0:
                        pe.wait_ge(scaled, 4 * u + 4)
                    if n >= 2:
                        pe.wait_ge(kept_v if kb % 2 == 0 else kept_a, (n - 2) // 2 + 1)
                    else:
                        pe.wait_ge(cs_kept, NT)
                    for t in range(kb, NT):
                        at = t * (t + 1) // 2 * P + kb * P
                        mm = pe.transpose(bank[4 + kb % 2][:, t * P:(t + 1) * P], probs[u % 2][:, at:at + P], ident[:])
                    mm.then_inc(turned, 1)

                def pv(u, kb):
                    c, half, b, g, s = unit(u)
                    out = bank[6 + c % 2][half * HD:(half + 1) * HD, :]
                    if b == 0 and kb == 0:
                        if c >= 2:
                            pe.wait_ge(o_lo_done, c - 1)
                        rep = slice(32 * (s % 4), 32 * (s % 4) + 32)
                        pe.matmul(out, vcm[rep, g], pcT[rep, g], start=True, stop=False)
                    pe.wait_ge(kept_v if kb % 2 == 0 else kept_a, 2 * u + kb // 2 + 1)
                    v = vsw[:, kb, 256 * b + g * HD:256 * b + (g + 1) * HD]
                    pe.matmul(out[:, kb * P:T], v, hid[:, kb % 2, kb * P:T], start=False,
                              stop=(b == 1 and kb == NT - 1)).then_inc(pv_done, 1)

                qk(0)
                for u in range(UNITS):
                    if u + 1 < UNITS:
                        qk(u + 1)
                    turn(u, 0)
                    for kb in range(1, NT):
                        turn(u, kb)
                        pv(u, kb - 1)
                    pv(u, NT - 1)

            def even():
                stats("mixe")
                for q in range(6):
                    dense("ein", q, h_hi, h_lo, h_lo_done, H_COUNT["mixe"])
                pe.wait_ge(e_loaded, 16 * 5)
                pe.matmul(bank[MISC][0:8, 0:BLOCK_F + 1], relb[:], onehot[:], start=True, stop=True).then_inc(diag_mm, 1)
                j = J0["einv"]
                pe.wait_ge(w_lo_done, j + 1)
                pe.wait_ge(acc_free, FREE0["einv"] - 3)
                for k in range(ND):
                    mm = three(bank[0][:], *tile_of(j % 2, k), h_hi[:, k], h_lo[:, k], k == 0, k == ND - 1)
                mm.then_inc(seg_done, 1)
                for t in range(NT):
                    pe.wait_ge(acc_free, FREE0["einv"] + t - 2)
                    cols = slice(t * P, (t + 1) * P)
                    for k in range(ND):
                        wh, wl = tile_of(j % 2, ND + k)
                        mm = three(bank[(t + 1) % 4][:, 0:P], h_hi[:, k, cols], h_lo[:, k, cols], wh, wl, k == 0,
                                   k == ND - 1)
                    mm.then_inc(seg_done, 1)
                pe.wait_ge(diag_vec, 1)
                turn_rs(PREP_OF["mixe"] + 1)
                pe.wait_ge(diag_in, 16)
                for i in range(4):
                    if i >= 2:
                        pe.wait_ge(bias_kept, i - 1)
                    pe.matmul(bank[5 + i % 2][:], flip[:], ebias[:, 2 * i:2 * i + 2].rearrange("p h s -> p (h s)"),
                              start=True, stop=True).then_inc(flipped, 1)
                pe.wait_ge(acc_free, FREE0["einv"] + 5)

                def qk(u):
                    r, half = u // 2, u % 2
                    rows = slice(half * HD, (half + 1) * HD)
                    for t in range(NT):
                        lo, n = (0, P) if t == 0 else ((t - 1) * P, 2 * P)
                        if u >= 1:
                            pe.wait_ge(scaled, E_SCALED0 + 4 * (u - 1) + t + 1)
                        pe.matmul(bank[t][:, 0:n], eq[rows, r, t * P:(t + 1) * P], eq[rows, 4, lo:lo + n],
                                  start=True, stop=True).then_inc(qk_done, 1)

                def tile_out(u, t):
                    r, half = u // 2, u % 2
                    pe.wait_ge(e_norm, 4 * u + t + 1)
                    n = 4 * u + t
                    if n >= 2:
                        pe.wait_ge(kept_a, E_KEPT_A0 + n - 1)
                    for b in range(0 if t else 1, 2):
                        mm = pe.transpose(bank[4 + t % 2][:, b * P:(b + 1) * P], eprobs[u % 2][:, t, b * P:(b + 1) * P],
                                          ident[:])
                    mm.then_inc(turned, 1)

                def tile_pv(u, t):
                    r, half = u // 2, u % 2
                    out = bank[6 + r % 2][half * HD:(half + 1) * HD, t * P:(t + 1) * P]
                    if half == 0 and t == 0 and r >= 2:
                        pe.wait_ge(o_lo_done, ND + r - 1)
                    pe.wait_ge(kept_a, E_KEPT_A0 + 4 * u + t + 1)
                    for b in range(0 if t else 1, 2):
                        mm = pe.matmul(out, ev[:, t - 1 + b, half * HD:(half + 1) * HD],
                                       hid[:, t % 2, b * P:(b + 1) * P], start=(b == 0 or t == 0), stop=b == 1)
                    mm.then_inc(pv_done, 1)

                qk(0)
                for u in range(8):
                    if u + 1 < 8:
                        qk(u + 1)
                    tile_out(u, 0)
                    for t in range(1, NT):
                        tile_out(u, t)
                        tile_pv(u, t - 1)
                    tile_pv(u, NT - 1)
                for i in range(2):
                    pe.wait_ge(ln_add, 4 * i + 4)
                    pe.matmul(bank[STAT][:], ones[:], sq[:] if i == 0 else sq_sum[:], start=True, stop=True)\
                        .then_inc(ln_mm, 1)

            def odd():
                stats("mixo")
                for q in range(4):
                    dense("rec", q, h_hi, h_lo, h_lo_done, H_COUNT["mixo"])
                j = J0["lgate"]
                pe.wait_ge(w_lo_done, j + 1)
                for c in range(ND):
                    for g in range(2):
                        n = 2 * c + g
                        if n < 4:
                            pe.wait_ge(acc_free, FREE0["lgate"] + n - 3)
                        else:
                            pe.wait_ge(g_sig, n - 3)
                        pe.wait_ge(rc_lo, c + 1)
                        three(bank[n % 4][:], *tile_of(j % 2, g * ND + c), r_hi[:, c], r_lo[:, c], True, True)\
                            .then_inc(seg_done, 1)
                pe.wait_ge(g_sig, 2 * ND)
                for q in range(4):
                    dense("ogate", q, h_hi, h_lo, h_lo_done, H_COUNT["mixo"])

            for stage in enabled:
                if stage == "pool":
                    pool()
                elif stage.startswith("up"):
                    up(int(stage[2:]))
                elif stage.startswith("down"):
                    down(int(stage[4:]))
                elif stage.startswith("ple"):
                    ple(int(stage[3:]))
                elif stage == "kproj":
                    attention_inputs()
                elif stage == "attn":
                    attention()
                elif stage == "final1":
                    stats("final1")
                elif stage == "ein":
                    even()
                elif stage == "rec":
                    odd()
                elif stage == "final2":
                    stats("final2")
                elif stage == "wout0":
                    for q in range(4):
                        dense(stage, q, o_hi, o_lo, o_lo_done, 0, residual="up1")
                elif stage == "wout1":
                    pe.wait_ge(ln_lo, 4)
                    pe.wait_ge(o_lo_done, ND + 4)
                    for q in range(4):
                        dense(stage, q, e_hi, e_lo, o_lo_done, ND - 4, residual="up3")
                elif stage == "wout2":
                    pe.wait_ge(acc_free, FREE0["ogate"] + ND)
                    for q in range(4):
                        dense(stage, q, r_hi, r_lo, y_lo, 0, residual="up5")

        @block.scalar
        def _(act):
            def split_w(j, count=None, segs=None):
                if j >= n_jobs:
                    return
                act.wait_ge(w_loaded[j % 2], 16 * (j // 2 + 1) if count is None else count)
                if j >= 2:
                    act.wait_ge(seg_done, SEGS_BEFORE[j - 1] if segs is None else segs)
                n = TILES[j] * P
                act.activation(w_hi[j % 2][:, 0:n], w_raw[j % 2][:, 0:n], ACT.Copy).then_inc(w_hi_done, 1)

            def wait_apart(s, count):
                act.wait_ge(s, count)
                if not isinstance(count, int):
                    act.wait_ge(const_set, 3)

            def root(prep):
                n = PREP_OF[prep]
                act.wait_ge(stat_done, n + 1)
                act.activation(rs[:], bank[STAT][:], ACT.Sqrt, bias=eps[:, 0:1], scale=1.0 / D).then_inc(root_done, 1)

            def prepare(prep, m):
                n = PREP_OF[prep]
                if n == 0:
                    if m == 0:
                        act.wait_ge(x_loaded, 16)
                else:
                    if not isinstance(m, int):
                        act.wait_ge(sq_added, 9 * n + m + 1)
                    wait_apart(x_ready, x_before(prep) + m + 1)
                if prep in GAIN:
                    act.activation(h_hi[:, m], x[:, m], ACT.Copy, scale=col(GAIN[prep], m)).then_inc(h_hi_done, 1)
                if isinstance(m, int):
                    act.wait_ge(sq_added, 9 * n + m + 1)
                act.activation(sq[:], x[:, m], ACT.Square).then_inc(sq_done, 1)

            def conv_up(l):
                stage = f"up{l}"
                n0, j0, s0 = l * NF, J0[stage], SEG0[stage]

                def body(i):
                    for u in range(2):
                        f, j = 2 * i + u, j0 + u
                        if isinstance(i, int):
                            split_w(j0 + f + 1)
                        else:
                            split_w(j + 1, 16 * ((j + 1) // 2 + 1) + 16 * i, s0 + 2 * f)
                        for g in range(2):
                            if g == 0:
                                act.wait_ge(hid_done, n0 + f)
                            wait_apart(acc_free, FREE0[stage] + 2 * f + g + 1)
                            act.activation(bank[CONV_A + g][:], taps_in[:, g, PAD:], ACT.Identity,
                                           bias=col(f"conv{l}_b", g * NF + f), scale=col(f"conv{l}_2", g * NF + f))\
                                .then_inc(seeded, 1)
                        act.wait_ge(tapped, 4 * (n0 + f) + 4)
                        act.activation(silu_g[:], bank[CONV_G][:], ACT.Silu).then_inc(silu_done, 1)
                        wait_apart(hid_done, n0 + f + 1)
                        act.activation(act_hi[:, f], hid[:, u], ACT.Copy).then_inc(act_hi_done, 1)
                pairs(act, NF // 2, body)

            def glu_up(n):
                stage = f"up{n}"
                n0, j0, s0 = n * NF, J0[stage], SEG0[stage]

                def body(i):
                    for u in range(2):
                        f, j = 2 * i + u, j0 + u
                        if isinstance(i, int):
                            split_w(j0 + f + 1)
                        else:
                            split_w(j + 1, 16 * ((j + 1) // 2 + 1) + 16 * i, s0 + 2 * f)
                        act.wait_ge(acc_free, FREE0[stage] + 2 * f + 1)
                        act.wait_ge(hid_done, n0 + f)
                        act.activation(silu_g[:], taps_in[:, u, PAD:], ACT.Silu).then_inc(silu_done, 1)
                        wait_apart(hid_done, n0 + f + 1)
                        act.activation(act_hi[:, f], hid[:, u], ACT.Copy).then_inc(act_hi_done, 1)
                pairs(act, NF // 2, body)

            def down(n):
                stage, nxt = f"down{n}", NEXT_PREP[f"down{n}"]
                j0, s0 = J0[stage], SEG0[stage]

                def body(i):
                    for u in range(4):
                        q, j = 4 * i + u, j0 + u
                        if isinstance(i, int):
                            split_w(j0 + q + 1)
                        else:
                            split_w(j + 1, 16 * ((j + 1) // 2 + 1) + 32 * i, s0 + q)
                        if u % 2 == 1:
                            prepare(nxt, 2 * i + u // 2)
                pairs(act, ND // 2, body)

            def ple(l):
                stage = f"ple{l}"
                j0, s0 = J0[stage], SEG0[stage]
                act.wait_ge(p_loaded, 16 * (l + 1))
                for k in range(2):
                    act.activation(p_hi[:, k], taps_in[:, k, PAD:], ACT.Copy).then_inc(p_hi_done, 1)
                root(stage)

                def body(i):
                    for u in range(2):
                        m, j = 2 * i + u, j0 + u
                        if isinstance(i, int):
                            split_w(j0 + m + 1)
                        else:
                            split_w(j + 1, 16 * ((j + 1) // 2 + 1) + 16 * i, s0 + 2 * m)
                        act.wait_ge(acc_free, FREE0[stage] + 2 * m + 1)
                        act.activation(ple_t[:, u], ple_t[:, u], ACT.Sigmoid).then_inc(sig_done, 1)
                pairs(act, ND // 2, body)
                for m in range(ND):
                    prepare(NEXT_PREP[stage], m)

            def start():
                act.wait_ge(const_set, 3)
                act.wait_ge(vec_loaded, 48)
                for m in range(ND):
                    prepare("start", m)
                split_w(0)
                root("start")

            def pool():
                split_w(1)
                for m in range(ND):
                    act.wait_ge(pool_step, POOL_U[m // 2])
                    act.activation(h_hi[:, m], pool_u[:, m // 2 % 2, m % 2], ACT.Copy).then_inc(pool_hi_done, 1)
                act.wait_ge(seg_done, ND)
                for m in range(ND):
                    prepare("up0", m)

            def attention_inputs():
                for m in range(ND):
                    act.activation(o_hi[:, m], x[:, m], ACT.Copy, scale=col("mix1", m)).then_inc(h2_hi_done, 1)
                root("kv")
                split_w(J0["kproj"] + 1)
                for i in range(2):
                    act.wait_ge(trig_step, 9 + 3 * i)
                    act.activation(rsin[:] if i == 0 else rcos[:], ang[2 + i][:], ACT.Sin).then_inc(sin_done, 1)
                for j in range(J0["kproj"] + 2, J0["qproj"] + 1):
                    split_w(j)
                act.wait_ge(acc_free, FREE0["gates"] + NT)
                act.activation(gates[:], gates[:], ACT.Sigmoid).then_inc(gates_done, 1)
                act.wait_ge(cmp_mm, 2)
                act.activation(cpos_b[:], bank[STAT][:, 256:258], ACT.Copy).then_inc(cmp_act, 1)
                act.wait_ge(cmp_act, 1)
                act.wait_ge(cmp_vec, 1)
                hk = taps_in[:, 0, PAD:PAD + NG * NC].rearrange("p (g c) -> p g c", g=NG)
                act.activation(hk[:, :, 0:NCMP], bank[STAT][:, 0:NG * NCMP].rearrange("p (g c) -> p g c", g=NG),
                               ACT.Gelu_apprx_tanh, bias=cpos_b[:, 0:1]).then_inc(cmp_act, 1)
                hv = taps_in[:, 1, PAD:].rearrange("p (g r c) -> p g r c", g=NG, r=4)
                for r in range(4):
                    act.activation(hv[:, :, r, 0:NCMP],
                                   bank[STAT][:, P:P + NG * NCMP].rearrange("p (g c) -> p g c", g=NG),
                                   ACT.Gelu_apprx_tanh, bias=cpos_b[:, 1:2]).then_inc(cmp_act, 1)
                for j in range(J0["qproj"] + 1, J0["wout0"] + 1):
                    split_w(j)

            def attention():
                for t in range(NT):
                    act.wait_ge(cs_vec, CS_STEPS * t + 6)
                    act.activation(hid[:, t % 2], hid[:, t % 2], ACT.Exp, scale=QK_SCALE).then_inc(cs_exp, 1)
                    act.wait_ge(cs_turned, t + 1)
                    act.activation(pcT[:, :, t * P:(t + 1) * P],
                                   bank[4 + t % 2][:].rearrange("p (g q) -> p g q", g=NG), ACT.Copy).then_inc(cs_kept, 1)

                def exps(u):
                    st = stat4[:, u % 2]
                    act.wait_ge(nmax_done, u + 1)
                    for t in range(NT):
                        at, n = t * (t + 1) // 2 * P, (t + 1) * P
                        if t == 0 and u >= 2:
                            act.wait_ge(turned, 4 * (u - 1))
                        act.activation(probs[u % 2][:, at:at + n], bank[t][:, 0:n], ACT.Exp, bias=st[:, 1, t:t + 1],
                                       scale=QK_SCALE, accum_out=st[:, 2, t:t + 1]).then_inc(exp_done, 1)

                def keep_o(c):
                    act.wait_ge(pv_done, 16 * (c + 1))
                    act.activation(o_hi[:, c], bank[6 + c % 2][:], ACT.Copy).then_inc(o_hi_done, 1)
                exps(0)
                for u in range(UNITS):
                    if u + 1 < UNITS:
                        exps(u + 1)
                    if u % 4 == 0 and u:
                        keep_o(u // 4 - 1)
                    for kb in (1, 3):
                        act.wait_ge(turned, 4 * u + kb + 1)
                        if 4 * u + kb >= 2:
                            act.wait_ge(pv_done, 4 * u + kb - 1)
                        act.activation(hid[:, 1, kb * P:T], bank[5][:, kb * P:T], ACT.Copy).then_inc(kept_a, 1)
                keep_o(ND - 1)

            def residual(stage):
                nxt = NEXT_PREP[stage]
                for q in range(4):
                    split_w(J0[stage] + q + 1)
                    for g in range(2):
                        prepare(nxt, 2 * q + g)

            def even():
                root("mixe")
                for c in range(6):
                    split_w(J0["ein"] + c + 1)
                    if c < 4:
                        act.wait_ge(acc_free, FREE0["ein"] + 2 * c + 2)
                        act.activation(taps_in[:, c % 2, PAD:], taps_in[:, c % 2, PAD:], ACT.Sigmoid).then_inc(glu_sig, 1)
                        act.wait_ge(glu_done, c + 1)
                        act.activation(cy[:, c], glu[:, c, TAPS - 1:], ACT.Identity, bias=col("cb_b", c),
                                       scale=col("cb_w", (TAPS - 1) * CC + c)).then_inc(y_seed, 1)
                split_w(J0["wout1"])

                def exps(u):
                    st = estat[:, u % 2]
                    act.wait_ge(nmax_done, UNITS + u + 1)
                    for t in range(NT):
                        cols = slice(P if t == 0 else 0, 2 * P)
                        e = eprobs[u % 2][:, t, cols]
                        act.activation(e, e, ACT.Exp, bias=st[:, 1, t:t + 1], accum_out=st[:, 2, t:t + 1])\
                            .then_inc(exp_done, 1)
                    act.activation(st[:, 0], st[:, 1], ACT.Exp, bias=sinks[:, u:u + 1]).then_inc(exp_done, 1)
                exps(0)
                for u in range(8):
                    if u + 1 < 8:
                        exps(u + 1)
                    for t in range(NT):
                        n = 4 * u + t
                        act.wait_ge(turned, E_TURNED0 + n + 1)
                        if n >= 2:
                            act.wait_ge(pv_done, E_PV0 + n - 1)
                        cols = slice(P if t == 0 else 0, 2 * P)
                        act.activation(hid[:, t % 2, cols], bank[4 + t % 2][:, cols], ACT.Copy).then_inc(kept_a, 1)
                    if u % 2 == 1:
                        r = u // 2
                        act.wait_ge(pv_done, E_PV0 + 4 * u + 4)
                        act.activation(e_hi[:, r], bank[6 + r % 2][:], ACT.Copy).then_inc(o_hi_done, 1)
                for c in range(CC):
                    act.wait_ge(ln_vec, c + 1)
                    if c >= 1:
                        act.wait_ge(ln_add, 4 + c)
                    act.activation(sq[:], cy[:, c], ACT.Square).then_inc(ln_sq, 1)
                act.wait_ge(ln_mm, 2)
                act.activation(silu_g[:], bank[STAT][:], ACT.Sqrt, bias=eps[:, 1:2], scale=1.0 / (CC * P)).then_inc(ln_act, 1)
                for c in range(CC):
                    act.wait_ge(ln_vec, CC + 2 + c)
                    act.activation(cy[:, c], cy[:, c], ACT.Silu, bias=col("ln_b", c), scale=col("ln_g", c)).then_inc(ln_act, 1)
                for c in range(CC):
                    act.wait_ge(ln_act, 2 + c)
                    act.activation(e_hi[:, CC + c], cy[:, c], ACT.Copy).then_inc(ln_hi, 1)

            def odd():
                act.wait_ge(lam_vec, 1)
                act.activation(lt[:, 1], lt[:, 0], ACT.Exp, scale=-1.0).then_inc(lam_act, 1)
                root("mixo")
                for q in range(4):
                    split_w(J0["rec"] + q + 1)
                    for g in range(2):
                        c = 2 * q + g
                        act.wait_ge(acc_free, FREE0["rec"] + c + 1)
                        act.activation(rc[:, c], taps_in[:, g, PAD:], ACT.Identity, bias=col("lru_b", c),
                                       scale=col("lru_w", 3 * ND + c)).then_inc(r_seed, 1)
                        act.wait_ge(r_tap, 3 * c + 3)
                        act.activation(r_hi[:, c], rc[:, c], ACT.Copy).then_inc(rc_hi, 1)
                split_w(J0["lgate"] + 1)
                for c in range(ND):
                    for g, (to, bias) in enumerate(((ra, "ga_b"), (ri, "gx_b"))):
                        act.wait_ge(seg_done, SEG0["lgate"] + 2 * c + g + 1)
                        act.activation(to[:, c], bank[(2 * c + g) % 4][:], ACT.Sigmoid, bias=col(bias, c)).then_inc(g_sig, 1)
                split_w(J0["ogate"] + 1)
                act.wait_ge(lam_vec, LAM_STEPS)
                act.wait_ge(g_sig, 2 * ND)

                def factors(hh):
                    for k in range(4):
                        if hh:
                            act.wait_ge(lru_vec, 28)
                        c = 4 * hh + k
                        act.activation(expv[:, k], ra[:, c], ACT.Exp, scale=sp8[:, c:c + 1]).then_inc(lru_act, 1)
                    for k in range(4):
                        c = 4 * hh + k
                        act.wait_ge(lru_act, 12 * hh + k + 1)
                        act.activation(ra[:, c], ra[:, c], ACT.Tanh, scale=sp4[:, c:c + 1]).then_inc(lru_act, 1)
                    for k in range(4):
                        c = 4 * hh + k
                        act.wait_ge(lru_act, 12 * hh + 4 + k + 1)
                        act.wait_ge(lru_vec, 28 * hh + k + 1)
                        act.activation(rc[:, c], ra[:, c], ACT.Sqrt).then_inc(lru_act, 1)

                def gate_chunk(c):
                    act.wait_ge(acc_free, FREE0["ogate"] + c + 1)
                    act.activation(taps_in[:, c % 2, PAD:], taps_in[:, c % 2, PAD:], ACT.Gelu_apprx_tanh)\
                        .then_inc(gel_done, 1)
                    act.wait_ge(y_done, c + 1)
                    act.activation(r_hi[:, c], hid[:, c % 2], ACT.Copy).then_inc(y_hi, 1)

                factors(0)
                factors(1)
                for c in range(ND):
                    if c % 2 == 0 and c < 6:
                        split_w(J0["ogate"] + 2 + c // 2)
                    gate_chunk(c)

            for stage in enabled:
                if stage == "pool":
                    start()
                    pool()
                elif stage in ("up0", "up1"):
                    root(stage)
                    conv_up(int(stage[2:]))
                elif stage.startswith("up"):
                    root(stage)
                    glu_up(int(stage[2:]))
                elif stage.startswith("down"):
                    down(int(stage[4:]))
                elif stage.startswith("ple"):
                    ple(int(stage[3:]))
                elif stage == "kproj":
                    attention_inputs()
                elif stage == "attn":
                    attention()
                elif stage == "final1":
                    root("final1")
                    for m in range(ND):
                        prepare("up2", m)
                elif stage == "final2":
                    root("final2")
                elif stage in ("wout0", "wout1", "wout2"):
                    residual(stage)
                elif stage == "ein":
                    even()
                elif stage == "rec":
                    odd()

        @block.vector
        def _(dve):
            def split_w(j, count=None):
                if j >= n_jobs:
                    return
                dve.wait_ge(w_hi_done, j + 1 if count is None else count)
                n = TILES[j] * P
                dve.tensor_tensor(w_lo[j % 2][:, 0:n], w_raw[j % 2][:, 0:n], w_hi[j % 2][:, 0:n].bitcast(F32),
                                  ALU.subtract).then_inc(w_lo_done, 1)

            def norm_factors(prep):
                n = PREP_OF[prep]
                dve.wait_ge(root_done, n + 1)
                dve.reciprocal(rs[:], rs[:]).then_inc(rs_done, 1)
                dve.wait_ge(rs_done, n + 1)

            def split_x(prep, m):
                dve.wait_ge(h_hi_done, H_COUNT[prep] + m + 1)
                dve.scalar_tensor_tensor(out=h_lo[:, m], in0=x[:, m], scalar=col(GAIN[prep], m),
                                         in1=h_hi[:, m].bitcast(F32), op0=ALU.mult, op1=ALU.subtract).then_inc(h_lo_done, 1)

            def add_to_x(prep, m, acc, factor):
                dve.scalar_tensor_tensor(out=x[:, m], in0=acc, scalar=factor, in1=x[:, m], op0=ALU.mult,
                                         op1=ALU.add).then_inc(x_ready, 1)
                dve.wait_ge(x_ready, x_before(prep) + m + 1)

            def start():
                dve.memset(ones[:], 1.0).then_inc(const_set, 1)
                dve.memset(eps[:, 0:1], EPS).then_inc(const_set, 1)
                dve.memset(eps[:, 1:2], LN_EPS).then_inc(const_set, 1)
                dve.memset(taps_in[:], 0.0).then_inc(acc_free, 1)
                dve.memset(pool_h[:, :, 0:CS], 0.0).then_inc(acc_free, 1)
                for i in range(2):
                    dve.memset(pool_w[i][:, :, 0:CS], 0.0).then_inc(acc_free, 1)
                dve.wait_ge(acc_free, 4)
                dve.wait_ge(x_loaded, 16)
                dve.wait_ge(vec_loaded, 48)
                split_w(0)
                norm_factors("start")

            def pool():
                for m in range(ND):
                    dve.scalar_tensor_tensor(out=pool_h[:, m, CS:], in0=x[:, m], scalar=col("mix0", m), in1=rs[:],
                                             op0=ALU.mult, op1=ALU.mult).then_inc(pool_step, 1)
                step = ND
                for g, w in enumerate(POOL_WINDOWS):
                    pair = pool_h[:, 2 * g:2 * g + 2]
                    cur = pair
                    for s in range(g + 1):
                        dve.wait_ge(pool_step, step)
                        to = pool_w[s % 2]
                        dve.tensor_tensor(to[:, :, CS:], cur[:, :, CS:], cur[:, :, CS - 2 ** s:CS - 2 ** s + T], ALU.add)\
                            .then_inc(pool_step, 1)
                        step += 1
                        cur = to
                    dve.wait_ge(pool_step, step)
                    fix = pool_fix[:, g].unsqueeze(1).broadcast_to([P, 2, CS])
                    dve.tensor_tensor(cur[:, :, CS:2 * CS], cur[:, :, CS:2 * CS], fix, ALU.mult).then_inc(pool_step, 1)
                    dve.wait_ge(pool_step, step + 1)
                    dve.scalar_tensor_tensor(out=pool_u[:, g % 2], in0=cur[:, :, CS:], scalar=1.0 / w, in1=pair[:, :, CS:],
                                             op0=ALU.mult, op1=ALU.subtract).then_inc(pool_step, 1)
                    step += 2
                    for k in range(2):
                        m = 2 * g + k
                        dve.wait_ge(pool_hi_done, m + 1)
                        dve.tensor_tensor(h_lo[:, m], pool_u[:, g % 2, k], h_hi[:, m].bitcast(F32), ALU.subtract)\
                            .then_inc(pool_lo_done, 1)
                split_w(1)
                for m in range(ND):
                    dve.wait_ge(seg_done, m + 1)
                    add_to_x("up0", m, bank[m % 4][:], col("pool_scale", m))
                for m in range(ND):
                    split_x("up0", m)

            def conv_up(l):
                stage = f"up{l}"
                n0, j0, s0 = l * NF, J0[stage], SEG0[stage]

                def body(i):
                    for u in range(2):
                        f = 2 * i + u
                        split_w(j0 + u + 1 if not isinstance(i, int) else j0 + f + 1, j0 + f + 2)
                        for g in range(2):
                            dve.wait_ge(seg_done, s0 + 2 * f + g + 1)
                            dve.tensor_tensor(taps_in[:, g, PAD:], bank[2 * u + g][:], rs[:], ALU.mult).then_inc(acc_free, 1)
                        for tap in (1, 0):
                            for g in range(2):
                                if tap == 1:
                                    dve.wait_ge(seeded, 2 * (n0 + f) + g + 1)
                                else:
                                    dve.wait_ge(tapped, 4 * (n0 + f) + g + 1)
                                acc, back = bank[CONV_A + g][:], 2 - tap
                                dve.scalar_tensor_tensor(out=acc, in0=taps_in[:, g, PAD - back:PAD - back + T],
                                                         scalar=col(f"conv{l}_{tap}", g * NF + f), in1=acc,
                                                         op0=ALU.mult, op1=ALU.add).then_inc(tapped, 1)
                        dve.wait_ge(silu_done, n0 + f + 1)
                        dve.wait_ge(act_lo_done, n0 + f)
                        dve.tensor_tensor(hid[:, u], bank[CONV_A][:], silu_g[:], ALU.mult).then_inc(hid_done, 1)
                        dve.wait_ge(hid_done, n0 + f + 1)
                pairs(dve, NF // 2, body)

            def glu_up(n):
                stage = f"up{n}"
                n0, j0, s0 = n * NF, J0[stage], SEG0[stage]

                def body(i):
                    for u in range(2):
                        f = 2 * i + u
                        split_w(j0 + u + 1 if not isinstance(i, int) else j0 + f + 1, j0 + f + 2)
                        dve.wait_ge(seg_done, s0 + 2 * f + 1)
                        dve.tensor_tensor(taps_in[:, u, PAD:], bank[2 * u][:], rs[:], ALU.mult).then_inc(acc_free, 1)
                        dve.wait_ge(seg_done, s0 + 2 * f + 2)
                        dve.wait_ge(act_lo_done, n0 + f)
                        dve.tensor_tensor(hid[:, u], bank[2 * u + 1][:], rs[:], ALU.mult).then_inc(acc_free, 1)
                        dve.wait_ge(acc_free, FREE0[stage] + 2 * f + 2)
                        dve.wait_ge(silu_done, n0 + f + 1)
                        dve.tensor_tensor(hid[:, u], hid[:, u], silu_g[:], ALU.mult).then_inc(hid_done, 1)
                pairs(dve, NF // 2, body)

            def down(n):
                stage, nxt = f"down{n}", NEXT_PREP[f"down{n}"]
                j0, s0 = J0[stage], SEG0[stage]
                factor = 1.0 if n < 2 else 0.5

                def body(i):
                    for u in range(4):
                        q = 4 * i + u
                        split_w(j0 + u + 1 if not isinstance(i, int) else j0 + q + 1, j0 + q + 2)
                        if u % 2 == 1:
                            m = 2 * i + u // 2
                            dve.wait_ge(seg_done, s0 + q + 1)
                            add_to_x(nxt, m, bank[u // 2][:], factor)
                            if nxt in GAIN:
                                split_x(nxt, m)
                pairs(dve, ND // 2, body)

            def ple(l):
                stage, nxt = f"ple{l}", NEXT_PREP[f"ple{l}"]
                j0, s0 = J0[stage], SEG0[stage]
                for k in range(2):
                    dve.wait_ge(p_hi_done, 2 * l + k + 1)
                    dve.tensor_tensor(p_lo[:, k], taps_in[:, k, PAD:], p_hi[:, k].bitcast(F32), ALU.subtract)\
                        .then_inc(p_lo_done, 1)
                norm_factors(stage)

                def body(i):
                    for u in range(2):
                        m = 2 * i + u
                        split_w(j0 + u + 1 if not isinstance(i, int) else j0 + m + 1, j0 + m + 2)
                        dve.wait_ge(seg_done, s0 + 2 * m + 1)
                        dve.tensor_tensor(ple_t[:, u], bank[2 * u][:], rs[:], ALU.mult).then_inc(acc_free, 1)
                        dve.wait_ge(seg_done, s0 + 2 * m + 2)
                        dve.wait_ge(sig_done, ND * l + m + 1)
                        dve.tensor_tensor(ple_t[:, u], bank[2 * u + 1][:], ple_t[:, u], ALU.mult).then_inc(acc_free, 1)
                        dve.wait_ge(acc_free, FREE0[stage] + 2 * m + 2)
                        add_to_x(nxt, m, ple_t[:, u], 1.0)
                pairs(dve, ND // 2, body)
                if nxt in GAIN:
                    for m in range(ND):
                        split_x(nxt, m)

            def rope_start(r, acc):
                if r >= 2:
                    dve.wait_ge(roped, r - 1)
                dve.tensor_tensor(hid[:, r % 2], acc, rs[:], ALU.mult).then_inc(acc_free, 1)

            def rope_end(r, out):
                dve.wait_ge(rot_done, r + 1)
                dve.wait_ge(cos_mul, r + 1)
                if r == 4:
                    s = rsin[:, 2 * CS - 1::CS].unsqueeze(1).broadcast_to([P, NG, NCMP])
                    t = hid[:, 0, 0:NG * NC].rearrange("p (g c) -> p g c", g=NG)[:, :, 0:NCMP]
                    partner = bank[5][:, 0:NG * NC].rearrange("p (g c) -> p g c", g=NG)[:, :, 0:NCMP]
                    c = silu_g[:, 0:NG * NC].rearrange("p (g c) -> p g c", g=NG)[:, :, 0:NCMP]
                else:
                    s, t, partner, c = rsin[:], hid[:, r % 2], bank[5 + r % 2][:], silu_g[:]
                dve.tensor_tensor(t, partner, s, ALU.mult).then_inc(sin_mul, 1)
                dve.wait_ge(sin_mul, r + 1)
                dve.tensor_tensor(out, t, c, ALU.add).then_inc(roped, 1)

            def attention_inputs():
                norm_factors("kv")
                dve.memset(taps_in[:, :, PAD:], 0.0).then_inc(cmp_vec, 1)
                dve.memset(kcT[:], 0.0).then_inc(trig_step, 1)
                for m in range(ND):
                    dve.wait_ge(h2_hi_done, m + 1)
                    dve.scalar_tensor_tensor(out=o_lo[:, m], in0=x[:, m], scalar=col("mix1", m),
                                             in1=o_hi[:, m].bitcast(F32), op0=ALU.mult, op1=ALU.subtract)\
                        .then_inc(h2_lo_done, 1)
                split_w(J0["kproj"] + 1)
                dve.wait_ge(pos_loaded, 16)
                dve.tensor_copy(ang[0][:], pos_i[:]).then_inc(trig_step, 1)
                dve.wait_ge(trig_step, 2)
                dve.tensor_scalar(ang[1][:], ang[0][:], col("freq", 0), None, ALU.mult).then_inc(trig_step, 1)
                dve.wait_ge(trig_step, 3)
                dve.tensor_scalar(ang[0][:], ang[1][:], 1.0 / TWO_PI, MAGIC, ALU.mult, ALU.add).then_inc(trig_step, 1)
                dve.wait_ge(trig_step, 4)
                dve.tensor_scalar(ang[0][:], ang[0][:], -MAGIC, None, ALU.add).then_inc(trig_step, 1)
                for i, c in enumerate((C1, C2, C3)):
                    dve.wait_ge(trig_step, 5 + i)
                    dve.scalar_tensor_tensor(out=ang[2 if i == 2 else 1][:], in0=ang[0][:], scalar=-c, in1=ang[1][:],
                                             op0=ALU.mult, op1=ALU.add).then_inc(trig_step, 1)
                dve.wait_ge(trig_step, 8)
                dve.tensor_scalar(ang[2][:], ang[2][:], PI32, -PI32, ALU.min, ALU.max).then_inc(trig_step, 1)
                dve.wait_ge(trig_step, 9)
                dve.tensor_scalar(ang[0][:], ang[2][:], np.pi / 2, -TWO_PI, ALU.is_gt, ALU.mult).then_inc(trig_step, 1)
                dve.wait_ge(trig_step, 10)
                dve.scalar_tensor_tensor(out=ang[3][:], in0=ang[2][:], scalar=np.pi / 2, in1=ang[0][:], op0=ALU.add,
                                         op1=ALU.add).then_inc(trig_step, 1)
                dve.wait_ge(trig_step, 11)
                dve.tensor_scalar(ang[3][:], ang[3][:], PI32, -PI32, ALU.min, ALU.max).then_inc(trig_step, 1)
                dve.wait_ge(sin_done, 2)
                for q in range(4):
                    split_w(J0["kproj"] + q + 2)
                    for n in (2 * q, 2 * q + 1):
                        dve.wait_ge(seg_done, SEG0["kproj"] + n + 1)
                        if n < 4:
                            for half in range(2):
                                src = slice(half * HD, (half + 1) * HD)
                                g = 2 * (n % 2) + half
                                dve.tensor_tensor(kvc[0:HD, n // 2, g], bank[n % 4][src], rs[src], ALU.mult).then_inc(kvc_done, 1)
                                ins = dve.tensor_tensor(kvc[HD:P, n // 2, g, 0:T - 1], bank[n % 4][src, 1:T],
                                                        rs[src, 1:T], ALU.mult)
                                ins.then_inc(acc_free if half else kvc_done, 1)
                        else:
                            r = n - 4
                            if r >= 2:
                                rope_end(r - 2, kT[:, r - 2])
                            rope_start(r, bank[n % 4][:])
                rope_end(2, kT[:, 2])
                rope_end(3, kT[:, 3])
                dve.wait_ge(rs_turned, 1)
                dve.tensor_copy(rs_col[:], bank[MISC][:].rearrange("p (t q) -> p t q", t=NT)[:, :, 0]).then_inc(rs_col_done, 1)
                dve.wait_ge(rs_col_done, 1)
                split_w(J0["gates"])
                for t in range(NT):
                    dve.wait_ge(seg_done, SEG0["vproj"] + t + 2)
                    dve.tensor_scalar(vsw[:, t], bank[t][:], rs_col[:, t:t + 1], None, ALU.mult).then_inc(acc_free, 1)
                split_w(J0["qproj"])
                for t in range(NT):
                    dve.wait_ge(seg_done, SEG0["gates"] + t + 1)
                    dve.tensor_scalar(gates[:, t], bank[t][:, 0:48], rs_col[:, t:t + 1], None, ALU.mult).then_inc(acc_free, 1)
                split_w(J0["qproj"] + 1)
                dve.wait_ge(cmp_mm, 3)
                dve.tensor_copy(hid[:, 0, 0:NG * NC], bank[MISC][:, 0:NG * NC]).then_inc(cmp_vec, 1)
                dve.tensor_copy(vcm[:], bank[MISC][:, P:P + NG * HD].rearrange("p (g d) -> p g d", g=NG)).then_inc(cmp_vec, 1)
                for n in range(2 * 4):
                    if n % 2 == 0 and n:
                        split_w(J0["qproj"] + n // 2 + 1)
                    dve.wait_ge(seg_done, SEG0["qproj"] + n + 1)
                    if n == 1:
                        rope_end(4, kcT[:, :, 0:NCMP])
                    if n >= 2:
                        rope_end(n + 3, qT[:, n - 2])
                    rope_start(n + 5, bank[n % 4][:])
                rope_end(11, qT[:, 6])
                rope_end(12, qT[:, 7])

            def attention():
                dve.wait_ge(gates_done, 1)
                count = 0

                def step(ins):
                    nonlocal count
                    ins.then_inc(cs_vec, 1)
                    count += 1
                    dve.wait_ge(cs_vec, count)

                for t in range(NT):
                    e = hid[:, t % 2].rearrange("p (s c) -> p s c", s=NH)
                    s, f = cstat[:, t % 2, 0], cstat[:, t % 2, 1]
                    keep = cmask[:, 1, t].unsqueeze(1).broadcast_to([P, NH, NC])
                    dve.wait_ge(cs_mm, t + 1)
                    if t >= 2:
                        dve.wait_ge(cs_turned, t - 1)
                    if t == 0:
                        dve.wait_ge(roped, 13)
                    for half in range(2):
                        to, got = (v.rearrange("p (i g s c) -> p i g s c", i=2, g=2, s=4)[:, :, half]
                                   for v in (hid[:, t % 2], bank[4 * half + t][:]))
                        for i in range(2):
                            step(dve.tensor_tensor(to[:, i], got[:, i],
                                                   cmask[:, 0, t].unsqueeze(1).broadcast_to([P, 4, NC]), ALU.add))
                    step(dve.tensor_reduce(s, e, AX, ALU.max))
                    step(dve.tensor_tensor(e, e, s.unsqueeze(2).broadcast_to([P, NH, NC]), ALU.subtract))
                    dve.wait_ge(cs_exp, t + 1)
                    step(dve.tensor_tensor(e, e, keep, ALU.mult))
                    step(dve.tensor_reduce(s, e, AX, ALU.add))
                    step(dve.tensor_scalar(s, s, 1e-30, None, ALU.max))
                    step(dve.reciprocal(f, s))
                    step(dve.tensor_tensor(f, f, gates[:, t, 0:NH], ALU.mult))
                    step(dve.tensor_tensor(e, e, f.unsqueeze(2).broadcast_to([P, NH, NC]), ALU.mult))

                def maxima(u):
                    st = stat4[:, u % 2]
                    for t in range(NT):
                        dve.wait_ge(qk_done, 4 * u + t + 1)
                        dve.tensor_reduce(st[:, 0, t:t + 1], bank[t][:, 0:(t + 1) * P], AX, ALU.max).then_inc(max_done, 1)
                    dve.wait_ge(max_done, 4 * u + 4)
                    dve.tensor_scalar(st[:, 1], st[:, 0], -QK_SCALE, None, ALU.mult).then_inc(nmax_done, 1)

                def keep_o(c):
                    dve.wait_ge(o_hi_done, c + 1)
                    dve.tensor_tensor(o_lo[:, c], bank[6 + c % 2][:], o_hi[:, c].bitcast(F32), ALU.subtract)\
                        .then_inc(o_lo_done, 1)

                maxima(0)
                for u in range(UNITS):
                    c, half, b, g, s = unit(u)
                    if u + 1 < UNITS:
                        maxima(u + 1)
                    st = stat4[:, u % 2]
                    dve.wait_ge(exp_done, 4 * u + 4)
                    dve.reciprocal(st[:, 3], st[:, 2]).then_inc(fac_done, 1)
                    dve.wait_ge(fac_done, 2 * u + 1)
                    dve.tensor_tensor(st[:, 3], st[:, 3], gates[:, :, (1 + b) * NH + s], ALU.mult).then_inc(fac_done, 1)
                    dve.wait_ge(fac_done, 2 * u + 2)
                    for t in range(NT):
                        at, n = t * (t + 1) // 2 * P, (t + 1) * P
                        dve.tensor_scalar(probs[u % 2][:, at:at + n], probs[u % 2][:, at:at + n], st[:, 3, t:t + 1], None,
                                          ALU.mult).then_inc(scaled, 1)
                    if u % 4 == 0 and u:
                        keep_o(u // 4 - 1)
                    for kb in (0, 2):
                        dve.wait_ge(turned, 4 * u + kb + 1)
                        if 4 * u + kb >= 2:
                            dve.wait_ge(pv_done, 4 * u + kb - 1)
                        else:
                            dve.wait_ge(cs_turned, NT)
                        dve.tensor_copy(hid[:, 0, kb * P:T], bank[4][:, kb * P:T]).then_inc(kept_v, 1)
                keep_o(ND - 1)

            def residual(stage):
                nxt = NEXT_PREP[stage]
                for q in range(4):
                    split_w(J0[stage] + q + 1)
                    for m in (2 * q, 2 * q + 1):
                        dve.wait_ge(seg_done, SEG0[stage] + m + 1)
                        add_to_x(nxt, m, bank[m % 4][:], 1.0)
                        split_x(nxt, m)

            def final(prep, gain, done, base):
                norm_factors(prep)
                for m in range(ND):
                    dve.scalar_tensor_tensor(out=x[:, m], in0=x[:, m], scalar=col(gain, m), in1=rs[:], op0=ALU.mult,
                                             op1=ALU.mult).then_inc(done, 1)
                    dve.wait_ge(done, base + m + 1)

            def even():
                norm_factors("mixe")
                dve.memset(glu[:, :, 0:TAPS - 1], 0.0).then_inc(glu_zero, 1)
                for q in range(6):
                    split_w(J0["ein"] + q + 1)
                    for n in (2 * q, 2 * q + 1):
                        dve.wait_ge(seg_done, SEG0["ein"] + n + 1)
                        c = n // 2
                        to = eq[:, n - 8] if n >= 8 else hid[:, c % 2] if n % 2 == 0 else taps_in[:, c % 2, PAD:]
                        dve.tensor_tensor(to, bank[n % 4][:], rs[:], ALU.mult).then_inc(acc_free, 1)
                    if q < 4:
                        dve.wait_ge(glu_sig, q + 1)
                        dve.tensor_tensor(glu[:, q, TAPS - 1:], hid[:, q % 2], taps_in[:, q % 2, PAD:], ALU.mult)\
                            .then_inc(glu_done, 1)
                dve.wait_ge(diag_mm, 1)
                dve.tensor_tensor(diag[:], bank[MISC][0:8, 0:BLOCK_F + 1], outside[:], ALU.add).then_inc(diag_vec, 1)
                dve.wait_ge(seg_done, SEG0["einv"] + 1)
                dve.tensor_tensor(eq[:, 4], bank[0][:], rs[:], ALU.mult).then_inc(acc_free, 1)
                dve.wait_ge(rs_turned, 2)
                dve.tensor_copy(e_rs[:], bank[MISC][:].rearrange("p (t q) -> p t q", t=NT)[:, :, 0]).then_inc(rs_col_done, 1)
                dve.wait_ge(rs_col_done, 2)
                for t in range(NT):
                    dve.wait_ge(seg_done, SEG0["einv"] + t + 2)
                    dve.tensor_scalar(ev[:, t], bank[(t + 1) % 4][:, 0:P], e_rs[:, t:t + 1], None, ALU.mult)\
                        .then_inc(acc_free, 1)
                for i in range(4):
                    dve.wait_ge(flipped, i + 1)
                    dve.tensor_copy(ebias[:, 2 * i:2 * i + 2].rearrange("p h s -> p (h s)"), bank[5 + i % 2][:])\
                        .then_inc(bias_kept, 1)
                dve.wait_ge(bias_kept, 4)
                split_w(J0["wout1"])

                todo = [(c + k, tap) for c in (0, 2) for tap in range(TAPS - 1) for k in range(2)]
                dve.wait_ge(glu_zero, 1)
                dve.wait_ge(glu_done, CC)

                def conv_taps(first, end):
                    for i in range(first, end):
                        c, tap = todo[i]
                        dve.wait_ge(y_seed, c + 1)
                        if i >= 2:
                            dve.wait_ge(y_tap, i - 1)
                        dve.scalar_tensor_tensor(out=cy[:, c], in0=glu[:, c, tap:tap + T], scalar=col("cb_w", tap * CC + c),
                                                 in1=cy[:, c], op0=ALU.mult, op1=ALU.add).then_inc(y_tap, 1)

                def scores(u):
                    st = estat[:, u % 2]
                    for t in range(NT):
                        cols = slice(P if t == 0 else 0, 2 * P)
                        if u >= 2 and t == 0:
                            dve.wait_ge(turned, E_TURNED0 + 4 * (u - 1))
                        dve.wait_ge(qk_done, 4 * UNITS + 4 * u + t + 1)
                        dve.scalar_tensor_tensor(out=eprobs[u % 2][:, t, cols], in0=bank[t][:, 0:P if t == 0 else 2 * P],
                                                 scalar=QK_SCALE, in1=ebias[:, u, cols], op0=ALU.mult, op1=ALU.add)\
                            .then_inc(scaled, 1)
                    for t in range(NT):
                        cols = slice(P if t == 0 else 0, 2 * P)
                        dve.wait_ge(scaled, E_SCALED0 + 4 * u + t + 1)
                        dve.tensor_reduce(st[:, 0, t:t + 1], eprobs[u % 2][:, t, cols], AX, ALU.max).then_inc(max_done, 1)
                    dve.wait_ge(max_done, 4 * UNITS + 4 * u + 4)
                    dve.tensor_scalar(st[:, 1], st[:, 0], sinks[:, u:u + 1], -1.0, ALU.max, ALU.mult).then_inc(nmax_done, 1)

                def keep_o(r):
                    dve.wait_ge(o_hi_done, ND + r + 1)
                    dve.tensor_tensor(e_lo[:, r], bank[6 + r % 2][:], e_hi[:, r].bitcast(F32), ALU.subtract)\
                        .then_inc(o_lo_done, 1)

                scores(0)
                for u in range(8):
                    if u + 1 < 8:
                        scores(u + 1)
                    st = estat[:, u % 2]
                    dve.wait_ge(exp_done, E_EXP0 + 5 * (u + 1))
                    dve.tensor_tensor(st[:, 2], st[:, 2], st[:, 0], ALU.add).then_inc(fac_done, 1)
                    dve.wait_ge(fac_done, E_FAC0 + 2 * u + 1)
                    dve.reciprocal(st[:, 3], st[:, 2]).then_inc(fac_done, 1)
                    dve.wait_ge(fac_done, E_FAC0 + 2 * u + 2)
                    for t in range(NT):
                        cols = slice(P if t == 0 else 0, 2 * P)
                        e = eprobs[u % 2][:, t, cols]
                        dve.tensor_scalar(e, e, st[:, 3, t:t + 1], None, ALU.mult).then_inc(e_norm, 1)
                    if u % 2 == 0 and u:
                        keep_o(u // 2 - 1)
                    conv_taps(15 * u, 15 * (u + 1))
                keep_o(3)
                dve.wait_ge(ln_mm, 1)
                for c in range(CC):
                    dve.scalar_tensor_tensor(out=cy[:, c], in0=bank[STAT][:], scalar=-1.0 / (CC * P), in1=cy[:, c],
                                             op0=ALU.mult, op1=ALU.add).then_inc(ln_vec, 1)
                dve.wait_ge(ln_act, 1)
                dve.reciprocal(silu_g[:], silu_g[:]).then_inc(ln_vec, 1)
                dve.wait_ge(ln_vec, CC + 1)
                for c in range(CC):
                    dve.tensor_tensor(cy[:, c], cy[:, c], silu_g[:], ALU.mult).then_inc(ln_vec, 1)
                for c in range(CC):
                    dve.wait_ge(ln_hi, c + 1)
                    dve.tensor_tensor(e_lo[:, CC + c], cy[:, c], e_hi[:, CC + c].bitcast(F32), ALU.subtract).then_inc(ln_lo, 1)

            def odd():
                lam = vec[:, VC["lam"]:VC["lam"] + ND]
                count = 0

                def step(ins):
                    nonlocal count
                    ins.then_inc(lam_vec, 1)
                    count += 1
                    dve.wait_ge(lam_vec, count)

                step(dve.scalar_tensor_tensor(out=lt[:, 0], in0=lam, scalar=-1.0, in1=lam, op0=ALU.mult, op1=ALU.max))
                dve.wait_ge(lam_act, 1)
                step(dve.tensor_scalar(lt[:, 2], lt[:, 1], 2.0, None, ALU.add))
                step(dve.reciprocal(lt[:, 2], lt[:, 2]))
                step(dve.tensor_tensor(lt[:, 3], lt[:, 1], lt[:, 2], ALU.mult))
                step(dve.tensor_tensor(lt[:, 4], lt[:, 3], lt[:, 3], ALU.mult))
                step(dve.tensor_scalar(lt[:, 5], lt[:, 4], 1.0 / 17, None, ALU.mult))
                for d in (15, 13, 11, 9, 7, 5, 3):
                    step(dve.scalar_tensor_tensor(out=lt[:, 5], in0=lt[:, 5], scalar=1.0 / d, in1=lt[:, 4], op0=ALU.add,
                                                  op1=ALU.mult))
                step(dve.scalar_tensor_tensor(out=lt[:, 5], in0=lt[:, 5], scalar=1.0, in1=lt[:, 3], op0=ALU.add, op1=ALU.mult))
                step(dve.tensor_scalar(lt[:, 2], lam, -1.0, 0.0, ALU.mult, ALU.max))
                step(dve.scalar_tensor_tensor(out=lt[:, 0], in0=lt[:, 5], scalar=2.0, in1=lt[:, 2], op0=ALU.mult, op1=ALU.add))
                step(dve.tensor_scalar(sp4[:], lt[:, 0], 4.0, None, ALU.mult))
                step(dve.tensor_scalar(sp8[:], lt[:, 0], -8.0, None, ALU.mult))
                assert count == LAM_STEPS
                norm_factors("mixo")
                for q in range(4):
                    split_w(J0["rec"] + q + 1)
                    for c in (2 * q, 2 * q + 1):
                        dve.wait_ge(seg_done, SEG0["rec"] + c + 1)
                        src = taps_in[:, c % 2]
                        dve.tensor_tensor(src[:, PAD:], bank[c % 4][:], rs[:], ALU.mult).then_inc(acc_free, 1)
                        dve.wait_ge(r_seed, c + 1)
                        for i, tap in enumerate((2, 1, 0)):
                            if i:
                                dve.wait_ge(r_tap, 3 * c + i)
                            dve.scalar_tensor_tensor(out=rc[:, c], in0=src[:, tap:tap + T], scalar=col("lru_w", tap * ND + c),
                                                     in1=rc[:, c], op0=ALU.mult, op1=ALU.add).then_inc(r_tap, 1)
                        dve.wait_ge(rc_hi, c + 1)
                        dve.tensor_tensor(r_lo[:, c], rc[:, c], r_hi[:, c].bitcast(F32), ALU.subtract).then_inc(rc_lo, 1)
                split_w(J0["lgate"] + 1)
                split_w(J0["ogate"] + 1)
                for hh in range(2):
                    at = 28 * hh
                    for k in range(4):
                        c = 4 * hh + k
                        dve.wait_ge(g_sig, 2 * c + 2)
                        dve.tensor_tensor(ri[:, c], ri[:, c], rc[:, c], ALU.mult).then_inc(lru_vec, 1)
                    for k in range(4):
                        c, n = 4 * hh + k, at + 4 + 6 * k
                        dve.wait_ge(lru_vec, at + 4)
                        dve.wait_ge(lru_act, 12 * hh + 8 + k + 1)
                        dve.tensor_scalar(expv[:, k], expv[:, k], 1.0, None, ALU.add).then_inc(lru_vec, 1)
                        dve.wait_ge(lru_vec, n + 1)
                        dve.tensor_tensor(ri[:, c], ri[:, c], expv[:, k], ALU.mult).then_inc(lru_vec, 1)
                        dve.wait_ge(lru_vec, n + 2)
                        dve.tensor_tensor(expv[:, k], expv[:, k], ra[:, c], ALU.mult).then_inc(lru_vec, 1)
                        dve.wait_ge(lru_vec, n + 3)
                        dve.tensor_tensor(ri[:, c], ri[:, c], rc[:, c], ALU.mult).then_inc(lru_vec, 1)
                        dve.tensor_scalar(ra[:, c], expv[:, k], -1.0, 1.0, ALU.mult, ALU.add).then_inc(lru_vec, 1)
                        dve.wait_ge(lru_vec, n + 5)
                        dve.tensor_tensor_scan(rc[:, c], ra[:, c], ri[:, c], 0.0, ALU.mult, ALU.add).then_inc(lru_vec, 1)
                for c in range(ND):
                    if c % 2 == 0 and c < 6:
                        split_w(J0["ogate"] + 2 + c // 2)
                    dve.wait_ge(seg_done, SEG0["ogate"] + c + 1)
                    dve.tensor_tensor(taps_in[:, c % 2, PAD:], bank[c % 4][:], rs[:], ALU.mult).then_inc(acc_free, 1)
                    dve.wait_ge(gel_done, c + 1)
                    dve.wait_ge(lru_vec, 56)
                    dve.tensor_tensor(hid[:, c % 2], taps_in[:, c % 2, PAD:], rc[:, c], ALU.mult).then_inc(y_done, 1)
                    dve.wait_ge(y_hi, c + 1)
                    dve.tensor_tensor(r_lo[:, c], hid[:, c % 2], r_hi[:, c].bitcast(F32), ALU.subtract).then_inc(y_lo, 1)

            for stage in enabled:
                if stage == "pool":
                    start()
                    pool()
                elif stage in ("up0", "up1"):
                    norm_factors(stage)
                    conv_up(int(stage[2:]))
                elif stage.startswith("up"):
                    norm_factors(stage)
                    glu_up(int(stage[2:]))
                elif stage.startswith("down"):
                    down(int(stage[4:]))
                elif stage.startswith("ple"):
                    ple(int(stage[3:]))
                elif stage == "kproj":
                    attention_inputs()
                elif stage == "attn":
                    attention()
                elif stage == "final1":
                    final("final1", "final1", x_ready, x_before("up2"))
                    for m in range(ND):
                        split_x("up2", m)
                elif stage == "final2":
                    final("final2", "final2", out_ready, 0)
                elif stage in ("wout0", "wout1", "wout2"):
                    residual(stage)
                elif stage == "ein":
                    even()
                elif stage == "rec":
                    odd()

        @block.gpsimd
        def _(pool):
            def clear(prep):
                n = PREP_OF[prep]
                if n:
                    pool.wait_ge(stat_done, n)
                pool.memset(sq_sum[:], 0.0).then_inc(sq_added, 1)

            def add(prep, m):
                n = PREP_OF[prep]
                pool.wait_ge(sq_done, ND * n + m + 1)
                pool.wait_ge(sq_added, 9 * n + m + 1)
                pool.tensor_tensor(sq_sum[:], sq_sum[:], sq[:], ALU.add).then_inc(sq_added, 1)

            def squares(prep):
                clear(prep)
                for m in range(ND):
                    add(prep, m)

            def split_hidden(n):
                def body(i):
                    for u in range(2):
                        f = 2 * i + u
                        pool.wait_ge(act_hi_done, NF * n + f + 1)
                        pool.tensor_tensor(act_lo[:, f], hid[:, u], act_hi[:, f].bitcast(F32), ALU.subtract)\
                            .then_inc(act_lo_done, 1)
                pairs(pool, NF // 2, body)

            def down(n):
                prep = NEXT_PREP[f"down{n}"]
                clear(prep)
                pairs(pool, ND // 2, lambda i: [add(prep, 2 * i + u) for u in range(2)])

            def rope_cos():
                for r in range(13):
                    pool.wait_ge(cmp_vec if r == 4 else acc_free, 2 if r == 4 else ROPE_FREE[r])
                    if r:
                        pool.wait_ge(roped, r)
                    if r == 4:
                        c = rcos[:, 2 * CS - 1::CS].unsqueeze(1).broadcast_to([P, NG, NCMP])
                        to, src = (b[:, 0:NG * NC].rearrange("p (g c) -> p g c", g=NG)[:, :, 0:NCMP]
                                   for b in (silu_g, hid[:, 0]))
                        pool.tensor_tensor(to, src, c, ALU.mult).then_inc(cos_mul, 1)
                    else:
                        pool.tensor_tensor(silu_g[:], hid[:, r % 2], rcos[:], ALU.mult).then_inc(cos_mul, 1)

            def layer_norm_sums():
                pool.wait_ge(y_tap, 2 * (TAPS - 1) * 2)
                pool.tensor_copy(sq[:], cy[:, 0]).then_inc(ln_add, 1)
                for c in range(1, CC):
                    pool.wait_ge(ln_add, c)
                    pool.tensor_tensor(sq[:], sq[:], cy[:, c], ALU.add).then_inc(ln_add, 1)
                for c in range(CC):
                    pool.wait_ge(ln_sq, c + 1)
                    if c == 0:
                        pool.tensor_copy(sq_sum[:], sq[:]).then_inc(ln_add, 1)
                    else:
                        pool.wait_ge(ln_add, 4 + c)
                        pool.tensor_tensor(sq_sum[:], sq_sum[:], sq[:], ALU.add).then_inc(ln_add, 1)
                pool.wait_ge(ln_mm, 2)

            pool.memset(pool_tap[:], 0.0).then_inc(act_lo_done, 1)
            squares("start")
            for stage in enabled:
                if stage.startswith("up"):
                    split_hidden(int(stage[2:]))
                elif stage.startswith("down"):
                    down(int(stage[4:]))
                elif stage == "kproj":
                    rope_cos()
                elif stage == "ein":
                    layer_norm_sums()
                elif stage in NEXT_PREP:
                    squares(NEXT_PREP[stage])


def constants():
    c, freq = np.zeros((P, 3 * P), np.float32), np.zeros(P, np.float32)
    c[:, 0:P] = np.eye(P)
    half = HD // 8
    for base in (0, HD):
        for d in range(half):
            c[base + d + half, P + base + d] = -1.0
            c[base + d, P + base + d + half] = 1.0
            f = np.float32(500000.0) ** np.float32(-2.0 * d / (2 * half))
            freq[base + d] = freq[base + d + half] = f
    c[:, 2 * P:3 * P] = np.eye(P)[::-1]
    return c, freq


def pool_fixes():
    t = np.arange(CS)
    fix = np.stack([w / np.minimum(t + 1, w) for w in POOL_WINDOWS]).astype(np.float32)
    return np.ascontiguousarray(np.broadcast_to(fix, (P, 4, CS)))


def compression_masks():
    t = np.arange(P)[:, None, None] + P * np.arange(NT)[None, :, None]
    end = CS * np.arange(NC) + 2 * CS - 1
    seen = (end <= t) & (np.arange(NC) < NCMP)
    return np.ascontiguousarray(np.stack([np.where(seen, 0.0, NEG), np.where(seen, 1.0, 0.0)], 1).astype(np.float32))


def relative_buckets():
    dist = 2 * P - 1 - np.arange(BLOCK_F + 1)
    n = np.maximum(dist, 0)
    nf = np.maximum(n, 16).astype(np.float32)
    large = 16 + (np.log(nf / np.float32(16)) / np.float32(np.log(8.0)) * np.float32(16)).astype(np.int32)
    bucket = np.where(n < 16, n, np.minimum(large, 31))
    onehot = (np.arange(32)[:, None] == bucket[None]).astype(np.float32)
    outside = np.where((dist >= 0) & (dist < P), 0.0, NEG).astype(np.float32)
    return onehot, np.ascontiguousarray(np.broadcast_to(outside, (8, BLOCK_F + 1)))


Q_ORDER = [h for i in range(2) for r in range(4) for h in (8 * i + r, 8 * i + 4 + r)]
E_ORDER = [h for r in range(4) for h in (r, 4 + r)]


def tiles(w):
    k, m = w.shape
    return w.reshape(k // P, P, m // P, P).transpose(2, 1, 0, 3)


def jobs(*parts):
    t = np.concatenate([tiles(w) for w in parts], 0)
    n, p, k, m = t.shape
    return np.ascontiguousarray(t.reshape(n // 2, 2, p, k, m).transpose(0, 2, 1, 3, 4)).reshape(n // 2, p, 2 * k * m)


def interleaved(a, b):
    t = np.stack([tiles(a), tiles(b)], 1)
    n, _, p, k, m = t.shape
    return np.ascontiguousarray(t.transpose(0, 2, 1, 3, 4)).reshape(n, p, 2 * k * m)


def halves(w):
    t = tiles(w)
    n, p, k, m = t.shape
    return np.ascontiguousarray(t.reshape(n, p, 2, k // 2, m).transpose(0, 2, 1, 3, 4)).reshape(2 * n, p, k // 2 * m)


def by_rows(w, k0, k1):
    return w.reshape(-1, P, w.shape[1])[k0:k1].transpose(1, 0, 2).reshape(P, -1)


def heads(w, order, axis):
    shape = list(w.shape)
    shape[axis:axis + 1] = [shape[axis] // HD, HD]
    return np.take(w.reshape(shape), order, axis).reshape(w.shape)


def layout(i):
    a = {k: np.asarray(v) for k, v in i.items()}
    cols = lambda v: np.asarray(v).reshape(-1, P).T
    parts = {
        "mix0": a["norm_mix"][0], "mix1": a["norm_mix"][1], "pool_scale": a["pool_scale"][0], "kv": a["norm_kv"],
        "ffn0": a["norm_ffn"][0], "ffn1": a["norm_ffn"][1], "ple0": a["norm_ple"][0], "ple1": a["norm_ple"][1],
        "final1": a["norm_final"], "ffn2": a["norm_ffn1_2"][0], "ffn3": a["norm_ffn2_2"][0],
        "ffn4": a["norm_ffn1_2"][1], "ffn5": a["norm_ffn2_2"][1], "mixe": a["norm_mix_2"][0], "mixo": a["norm_mix_2"][1],
        "final2": a["norm_final_2"], "cb_w": a["conv_b_w_2"][0], "cb_b": a["conv_b_b_2"][0], "ln_g": a["conv_ln_g_2"][0],
        "ln_b": a["conv_ln_b_2"][0], "lru_w": a["lru_conv_w_2"][0], "lru_b": a["lru_conv_b_2"][0],
        "ga_b": a["gate_a_b_2"][0], "gx_b": a["gate_x_b_2"][0], "lam": a["lru_lambda_2"][0],
    }
    consts, parts["freq"] = constants()
    for l in range(2):
        for j in range(3):
            parts[f"conv{l}_{j}"] = a["ffn_conv"][l, j]
        parts[f"conv{l}_b"] = a["ffn_conv_b"][l]
    out = {"x": a["x"][0].T.reshape(ND, P, T).transpose(1, 0, 2), "vec": np.concatenate([cols(parts[n]) for n, _ in VEC_LIST], 1)}
    out["p"] = a["p"][:, 0].transpose(0, 2, 1).reshape(2, 2, P, T).transpose(0, 2, 1, 3)
    out["positions"] = a["positions"]
    out["w_pool"] = a["pool_w"][0].reshape(4, 2, P, 2, P).transpose(2, 0, 3, 1, 4).reshape(1, P, SLOT * P)
    for l in range(2):
        up = a["ffn_up"][l]
        out[f"w_up{l}"] = interleaved(up[:, :DFF], up[:, DFF:])
        out[f"w_down{l}"] = halves(a["ffn_down"][l])
        gate, proj = tiles(a["ple_gate"][l]), tiles(a["ple_proj"][l])
        out[f"w_ple{l}"] = np.concatenate([gate, proj], 2).reshape(ND, P, 10 * P)
    kv = a["w_kv"]
    out["w_kproj"] = jobs(kv[:, 0:512], kv[:, 512:768], kv[:, 1024:1280])
    v = np.concatenate([kv[:, 768:1024], kv[:, 1280:1536]], 1)
    out["w_vproj"] = np.stack([by_rows(v, 0, 4), by_rows(v, 4, 8)])
    w_in = a["w_in_b"][0]
    gate = w_in[:, D:].reshape(D, NH, 3).transpose(0, 2, 1).reshape(D, 48)
    out["w_gates"] = by_rows(gate, 0, 8)[None]
    out["w_qproj"] = jobs(heads(w_in[:, :D], Q_ORDER, 1))
    out["w_wout0"] = jobs(heads(a["w_out_b"][0], Q_ORDER, 0))
    for n, (kind, l) in enumerate((("ffn1", 0), ("ffn2", 0), ("ffn1", 1), ("ffn2", 1))):
        out[f"w_up{n + 2}"] = interleaved(a[kind + "_wg_2"][l], a[kind + "_wu_2"][l])
        out[f"w_down{n + 2}"] = halves(a[kind + "_wd_2"][l])
    e = a["even_w_in_2"][0]
    ga, gb = tiles(e[:, 768:1280]), tiles(e[:, 1280:1792])
    glu = np.stack([ga, gb], 1).transpose(0, 2, 1, 3, 4).reshape(4, P, SLOT * P)
    out["w_ein"] = np.concatenate([glu, jobs(heads(e[:, 0:512], E_ORDER, 1))], 0)
    out["w_einv"] = np.concatenate([tiles(e[:, 512:640])[0].reshape(P, -1), by_rows(e[:, 640:768], 0, 8)], 1)[None]
    eo = a["even_w_out_2"][0]
    out["w_wout1"] = jobs(np.concatenate([heads(eo[:512], E_ORDER, 0), eo[512:]], 0))
    o = a["odd_w_in_2"][0]
    out["w_rec"] = jobs(o[:, D:])
    out["w_ogate"] = jobs(o[:, :D])
    gates = np.stack([a["gate_a_w_2"][0], a["gate_x_w_2"][0]])
    out["w_lgate"] = gates.transpose(2, 0, 1, 3).reshape(1, P, SLOT * P)
    out["w_wout2"] = jobs(a["odd_w_out_2"][0])
    for s in "kv":
        out[f"cmp_w1_{s}"] = a[f"cmp_w1_{s}"].reshape(CS, P, P).transpose(1, 0, 2)
        out[f"cmp_w2_{s}"] = a[f"cmp_w2_{s}"]
        out[f"cmp_pos_{s}"] = a[f"cmp_pos_{s}"].reshape(CS, P).T
    out["rel_bias"] = a["rel_bias_2"][:, E_ORDER]
    out["sinks"] = a["attn_sinks_2"][:, E_ORDER]
    out["consts"] = consts
    out["pool_fix"] = pool_fixes()
    out["cmask"] = compression_masks()
    out["onehot"], out["outside"] = relative_buckets()
    return {k: np.ascontiguousarray(v) for k, v in out.items()}


def kernel(stop_after=None, **inputs):
    import concourse.bacc as bacc
    from concourse.bass_utils import run_bass_kernel_spmd
    from ml_dtypes import bfloat16

    arrays = layout(inputs)
    ahead = np.arange(P)[None, :] > np.arange(P)[:, None]
    arrays["mask_bf"] = np.ascontiguousarray(np.stack([np.eye(P), np.where(ahead, NEG, 0.0)], 1).astype(bfloat16))
    nc = bacc.Bacc("TRN2", target_bir_lowering=False, num_devices=1)
    a = {n: nc.dram_tensor("in_" + n, v.shape, mybir.dt.from_np(v.dtype), kind="ExternalInput").ap()
         for n, v in arrays.items()}
    a["out"] = nc.dram_tensor("out", (ND, P, T), F32, kind="ExternalOutput").ap()
    build(nc, a, stop_after)
    r = run_bass_kernel_spmd(nc, [{"in_" + n: v for n, v in arrays.items()}], core_ids=[0])
    return r.results[0]["out"].reshape(D, T).T.reshape(1, T, D)
```

```python
from contextlib import ExitStack

import concourse.bass as bass
import numpy as np
from concourse import mybir

F32 = mybir.dt.float32
F32R = mybir.dt.float32r
BF16 = mybir.dt.bfloat16
I32 = mybir.dt.int32
ALU = mybir.AluOpType
ACT = mybir.ActivationFunctionType
AX = mybir.AxisListType.X

P = 128
T = 512
NT = T // P
D = 1024
ND = D // P
DFF = 2816
NF = DFF // P
HALF_F = NF // 2
SLOT = 16
EPS = 1e-6
LN_EPS = 1e-5
NEG = -1e30
HD = 64
QK_SCALE = HD ** -0.5
POOL_WINDOWS = (2, 4, 8, 16)
NH = 16
NG = 4
CS = 16
NCMP = T // CS - 1
NC = 32
TAPS = 31
PAD = 3
CC = 4
BLOCK_F = 383
MAGIC = 12582912.0
TWO_PI = float(2 * np.pi)
PI32 = 3.1415925
C1 = 6.28125
C2 = float(np.float32(np.floor((TWO_PI - C1) * 2 ** 20) / 2 ** 20))
C3 = float(np.float32(TWO_PI - C1 - C2))

VEC_LIST = [
    ("mix0", 8), ("pool_scale", 8), ("ffn0", 8), ("ple0", 8), ("kv", 8), ("mix1", 8), ("ffn1", 8), ("ple1", 8),
    ("final1", 8), ("conv0_0", 44), ("conv0_1", 44), ("conv0_2", 44), ("conv0_b", 44),
    ("conv1_0", 44), ("conv1_1", 44), ("conv1_2", 44), ("conv1_b", 44),
    ("ffn2", 8), ("mixe", 8), ("ffn3", 8), ("ffn4", 8), ("mixo", 8), ("ffn5", 8), ("final2", 8),
    ("cb_w", TAPS * CC), ("cb_b", 4), ("ln_g", 4), ("ln_b", 4), ("lru_w", 32), ("lru_b", 8), ("ga_b", 8),
    ("gx_b", 8), ("lam", 8), ("freq", 1),
]
VC, _at = {}, 0
for _name, _n in VEC_LIST:
    VC[_name] = _at
    _at += _n
NVEC = _at

STAGES = [("pool", 1, 16, 8)]
for _l in range(2):
    if _l == 1:
        STAGES += [("kproj", 4, 16, 2), ("vproj", 2, 16, 0), ("gates", 1, 3, 2), ("qproj", 4, 16, 2),
                   ("wout0", 4, 16, 2)]
    STAGES += [(f"up{_l}", 22, 16, 2), (f"down{_l}", 16, 11, 1), (f"ple{_l}", 8, 10, 2)]
STAGES += [("up2", 22, 16, 2), ("down2", 16, 11, 1), ("ein", 6, 16, 2), ("einv", 1, 16, 5), ("wout1", 4, 16, 2),
           ("up3", 22, 16, 2), ("down3", 16, 11, 1), ("up4", 22, 16, 2), ("down4", 16, 11, 1),
           ("rec", 4, 16, 2), ("lgate", 1, 16, 0), ("ogate", 4, 16, 2), ("wout2", 4, 16, 2),
           ("up5", 22, 16, 2), ("down5", 16, 11, 1)]
J0, TILES, SEGS_BEFORE = {}, [], [0]
for _name, _jobs, _tiles, _segs in STAGES:
    J0[_name] = len(TILES)
    for _j in range(_jobs):
        TILES.append(_tiles)
        SEGS_BEFORE.append(SEGS_BEFORE[-1] + ({0: 1, 1: 4}[_j] if _name == "vproj" else _segs))
NJOBS = len(TILES)
JOBS_OF = {n: j for n, j, _, _ in STAGES}
SEG0 = {n: SEGS_BEFORE[J0[n]] for n, _, _, _ in STAGES}

PREPS = ["start", "up0", "ple0", "kv", "up1", "ple1", "final1", "up2", "mixe", "up3", "up4", "mixo", "up5", "final2"]
GAIN = {"up0": "ffn0", "ple0": "ple0", "kv": "kv", "up1": "ffn1", "ple1": "ple1", "up2": "ffn2", "mixe": "mixe",
        "up3": "ffn3", "up4": "ffn4", "mixo": "mixo", "up5": "ffn5"}
PREP_OF = {n: i for i, n in enumerate(PREPS)}
H_COUNT = {}
_at = 0
for _name in PREPS:
    H_COUNT[_name] = _at
    if _name in GAIN:
        _at += ND

ACC_READS = {"pool": 0, "up": 44, "down": 0, "ple": 16, "kproj": 8, "vproj": 4, "gates": 2, "qproj": 8, "wout": 0,
             "ein": 12, "einv": 5, "rec": 8, "lgate": 0, "ogate": 8}
FREE0, _at = {}, 4
for _name, _, _, _ in STAGES:
    FREE0[_name] = _at
    _at += ACC_READS[_name.rstrip("0123456789")]


STAGE_ORDER = []
for _name, _, _, _ in STAGES:
    STAGE_ORDER.append(_name)
    if _name == "qproj":
        STAGE_ORDER.append("attn")
    if _name == "ple1":
        STAGE_ORDER.append("final1")
STAGE_ORDER.append("final2")
NEXT_PREP = {"pool": "up0", "down0": "ple0", "ple0": "kv", "wout0": "up1", "down1": "ple1", "ple1": "final1",
             "final1": "up2", "down2": "mixe", "wout1": "up3", "down3": "up4", "down4": "mixo", "wout2": "up5",
             "down5": "final2"}
POOL_U, _at = [], ND
for _g in range(len(POOL_WINDOWS)):
    _at += _g + 3
    POOL_U.append(_at)
ROPE_FREE = [FREE0["kproj"] + 5 + _r for _r in range(4)] + [None] + [FREE0["qproj"] + 1 + _r for _r in range(8)]
CS_SHIFTED, CS_DONE = NT + 2 * 2 + 1, NT + 2 * 7 + 1
UNIT_ORDER_PE = (("qk", 0), ("turn", 0), ("qk", 1), ("pv", 3), ("turn", 1), ("qk", 2), ("pv", 0), ("turn", 2),
                 ("pv", 1), ("qk", 3), ("turn", 3), ("pv", 2))
UNIT_ORDER_ACT = (("exp", 0), ("exp", 1), ("keep", 1), ("exp", 2), ("scale", 3), ("exp", 3), ("keep", 3))
UNIT_ORDER_DVE = (("peak", 0), ("keep", 0), ("negate", 0), ("peak", 1), ("factor", 0), ("negate", 1), ("factor", 1),
                  ("scale", 0), ("peak", 2), ("scale", 1), ("negate", 2), ("keep", 2), ("scale", 2), ("peak", 3),
                  ("negate", 3))
E_UNITS = 8
LN_AT = (5, 7)
UNITS = 2 * NH
LAM_STEPS = 18
E_SCALED0, E_TURNED0, E_PV0, E_EXP0, E_KEPT_A0, E_FAC0 = 3 * UNITS, 4 * UNITS, 4 * UNITS, 4 * UNITS, 2 * UNITS, 2 * UNITS


def unit(u):
    c, half, b = u // 4, u // 2 % 2, u % 2
    return c, half, b, 2 * (c // 4) + half, 2 * c + half


def x_before(prep):
    return ND * (PREP_OF[prep] - 1)


def pairs(eng, n, body, peel=0):
    if n > 2:
        for i in range(peel):
            body(i)
        with eng.Fori(peel, n - 1) as i:
            body(i)
        body(n - 1)
    else:
        for i in range(n):
            body(i)


def build(nc, a, stop_after=None):
    with ExitStack() as ctx:
        def sb(name, shape, dt=F32, to=ctx):
            return to.enter_context(nc.sbuf_tensor(name, shape, dt))

        def sem(name):
            return ctx.enter_context(nc.semaphore(name))

        x = sb("x", [P, ND, T])
        with ExitStack() as part:
            probs = [sb(f"probs{i}", [P, 10 * P], to=part) for i in range(3)]
            e4 = sb("e4", [P, NT, T], to=part)
        with ExitStack() as part:
            eprobs = [sb(f"eprobs{i}", [P, NT, 2 * P], to=part) for i in range(3)]
        h_hi = sb("h_hi", [P, ND, T], F32R)
        h_lo = sb("h_lo", [P, ND, T], F32R)
        w_raw = [sb(f"w_raw{s}", [P, SLOT * P]) for s in range(2)]
        w_hi = [sb(f"w_hi{s}", [P, SLOT * P], F32R) for s in range(2)]
        w_lo = [sb(f"w_lo{s}", [P, SLOT * P], F32R) for s in range(2)]
        vec = sb("vec", [P, NVEC])
        rs = sb("rs", [P, T])
        sq = sb("sq", [P, T])
        sq_sum = sb("sq_sum", [P, T])
        taps_in = sb("taps_in", [P, 2, PAD + T])
        silu_g = sb("silu_g", [P, T])
        hid = sb("hid", [P, 2, T])
        ones = sb("ones", [P, P])
        ident = sb("ident", [P, P])
        eps = sb("eps", [P, 2])

        with ExitStack() as part:
            pool_h = sb("pool_h", [P, ND, CS + T], to=part)
            pool_w = [sb(f"pool_w{i}", [P, 2, CS + T], to=part) for i in range(2)]
            pool_u = sb("pool_u", [P, 2, 2, T], to=part)
            pool_fix = sb("pool_fix", [P, 4, CS], to=part)
            pool_tap = sb("pool_tap", [P, 1], to=part)
        with ExitStack() as part:
            act_hi = sb("act_hi", [P, NF, T], F32R, to=part)
            act_lo = sb("act_lo", [P, NF, T], F32R, to=part)
        with ExitStack() as part:
            p_hi = sb("p_hi", [P, 2, T], F32R, to=part)
            p_lo = sb("p_lo", [P, 2, T], F32R, to=part)
            ple_t = sb("ple_t", [P, 2, T], to=part)
        with ExitStack() as part:
            o_hi = sb("o_hi", [P, ND, T], F32R, to=part)
            o_lo = sb("o_lo", [P, ND, T], F32R, to=part)
            with ExitStack() as sub:
                cw1 = sb("cw1", [P, 2, CS, P], to=sub)
            qT = sb("qT", [P, ND, T], to=part)
            kT = sb("kT", [P, 4, T], to=part)
            vsw = sb("vsw", [P, NT, T], to=part)
            kcT = sb("kcT", [P, 2, 2, NC], to=part)
            vcm = sb("vcm", [P, NG, HD], to=part)
            gates = sb("gates", [P, NT, 48], to=part)
            rs_col = sb("rs_col", [P, NT], to=part)
            cmask = sb("cmask", [P, NT, NC], to=part)
            cw2 = sb("cw2", [P, 3, HD], to=part)
            cpos = sb("cpos", [P, 2, CS], to=part)
            cpos_b = sb("cpos_b", [P, 2], to=part)
            rot = sb("rot", [P, P], to=part)
            mask_bf = sb("mask_bf", [P, 2, P], BF16, to=part)
            stat4 = sb("stat4", [P, 2, 4, NT], to=part)
            cstat = sb("cstat", [P, 2, NT, NH], to=part)
            with ExitStack() as sub:
                rcos = sb("rcos", [P, T], to=sub)
                rsin = sb("rsin", [P, T], to=sub)
                with ExitStack() as sub2:
                    pos_i = sb("pos_i", [P, T], I32, to=sub2)
                    ang = [sb(f"ang{i}", [P, T], to=sub2) for i in range(4)]
                kvc = sb("kvc", [P, 2, NG, T], to=sub)
            with ExitStack() as sub:
                pcT = sb("pcT", [P, NG, T], to=sub)
        with ExitStack() as part:
            e_hi = sb("e_hi", [P, ND, T], F32R, to=part)
            e_lo = sb("e_lo", [P, ND, T], F32R, to=part)
            eq = sb("eq", [P, 5, T], to=part)
            ev = sb("ev", [P, NT, P], to=part)
            e_rs = sb("e_rs", [P, NT], to=part)
            ebias = sb("ebias", [P, 8, 2 * P], to=part)
            glu = sb("glu", [P, CC, TAPS - 1 + T], to=part)
            cy = sb("cy", [P, CC, T], to=part)
            estat = sb("estat", [P, 2, 4, NT], to=part)
            sinks = sb("sinks", [P, 8], to=part)
            with ExitStack() as sub:
                relb = sb("relb", [32, 8], to=sub)
                onehot = sb("onehot", [32, BLOCK_F + 1], to=sub)
                outside = sb("outside", [8, BLOCK_F + 1], to=sub)
                diag = sb("diag", [8, BLOCK_F + 1], to=sub)
                flip = sb("flip", [P, P], to=sub)
        with ExitStack() as part:
            r_hi = sb("r_hi", [P, ND, T], F32R, to=part)
            r_lo = sb("r_lo", [P, ND, T], F32R, to=part)
            rc = sb("rc", [P, ND, T], to=part)
            ra = sb("ra", [P, ND, T], to=part)
            ri = sb("ri", [P, ND, T], to=part)
            sp4 = sb("sp4", [P, ND], to=part)
            sp8 = sb("sp8", [P, ND], to=part)
            expv = sb("expv", [P, 4, T], to=part)
            lt = sb("lt", [P, 6, ND], to=part)

        bank = [ctx.enter_context(nc.psum_tensor(f"bank{i}", [P, T], F32)) for i in range(8)]
        STAT, CONV_A, CONV_G, MISC, LN = 4, 5, 6, 7, 7
        scratch = nc.dram_tensor("diag_scratch", [8 * (BLOCK_F + 1)], F32, kind="Internal")

        x_loaded, vec_loaded = sem("x_loaded"), sem("vec_loaded")
        w_loaded = [sem("w_loaded0"), sem("w_loaded1")]
        w_hi_done, w_lo_done = sem("w_hi_done"), sem("w_lo_done")
        const_set = sem("const_set")
        ident_set = sem("ident_set")
        seg_done = sem("seg_done")
        acc_free = sem("acc_free")
        x_ready = sem("x_ready")
        h_hi_done, h_lo_done = sem("h_hi_done"), sem("h_lo_done")
        sq_done, sq_added = sem("sq_done"), sem("sq_added")
        stat_done, root_done, rs_done = sem("stat_done"), sem("root_done"), sem("rs_done")
        seeded, tapped, silu_done, hid_done = sem("seeded"), sem("tapped"), sem("silu_done"), sem("hid_done")
        act_hi_done, act_lo_done = sem("act_hi_done"), sem("act_lo_done")
        p_loaded, p_hi_done, p_lo_done = sem("p_loaded"), sem("p_hi_done"), sem("p_lo_done")
        sig_done, prod_done = sem("sig_done"), sem("prod_done")
        pool_step, pool_hi_done, pool_lo_done = sem("pool_step"), sem("pool_hi_done"), sem("pool_lo_done")
        aux_loaded, pos_loaded = sem("aux_loaded"), sem("pos_loaded")
        trig_step, sin_done = sem("trig_step"), sem("sin_done")
        h2_hi_done, h2_lo_done = sem("h2_hi_done"), sem("h2_lo_done")
        kvc_done = sem("kvc_done")
        rot_done, cos_mul, sin_mul, roped = sem("rot_done"), sem("cos_mul"), sem("sin_mul"), sem("roped")
        rs_turned, rs_col_done = sem("rs_turned"), sem("rs_col_done")
        gates_done = sem("gates_done")
        cmp_mm, cmp_act, cmp_vec = sem("cmp_mm"), sem("cmp_act"), sem("cmp_vec")
        cs_mm, cs_vec, cs_exp, cs_turned, cs_kept = (sem(n) for n in ("cs_mm", "cs_vec", "cs_exp", "cs_turned", "cs_kept"))
        qk_done, max_done, nmax_done, exp_done = sem("qk_done"), sem("max_done"), sem("nmax_done"), sem("exp_done")
        fac_done, scaled, scaled_a, turned = sem("fac_done"), sem("scaled"), sem("scaled_a"), sem("turned")
        kept_v, kept_a, pv_done = sem("kept_v"), sem("kept_a"), sem("pv_done")
        o_hi_done, o_lo_done = sem("o_hi_done"), sem("o_lo_done")
        e_loaded, diag_mm, diag_vec, diag_out, diag_in, flipped, bias_kept = (
            sem(n) for n in ("e_loaded", "diag_mm", "diag_vec", "diag_out", "diag_in", "flipped", "bias_kept"))
        glu_sig, glu_done, y_seed, y_tap, y_tap_p = (sem(n) for n in ("glu_sig", "glu_done", "y_seed", "y_tap", "y_tap_p"))
        ln_add, ln_mm, ln_vec, ln_sq, ln_act, ln_hi, ln_lo = (
            sem(n) for n in ("ln_add", "ln_mm", "ln_vec", "ln_sq", "ln_act", "ln_hi", "ln_lo"))
        u_done, r_seed, r_tap, rc_hi, rc_lo = (sem(n) for n in ("u_done", "r_seed", "r_tap", "rc_hi", "rc_lo"))
        lam_vec, lam_act, lgate_done, g_sig, lru_act, lru_vec, lru_pool = (
            sem(n) for n in ("lam_vec", "lam_act", "lgate_done", "g_sig", "lru_act", "lru_vec", "lru_pool"))
        gel_done, y_done, y_hi, y_lo, e_norm, glu_zero = (sem(n) for n in ("gel_done", "y_done", "y_hi", "y_lo", "e_norm", "glu_zero"))
        out_ready, stored = sem("out_ready"), sem("stored")

        def col(name, m):
            at = VC[name] + m
            return vec[:, at:at + 1] if isinstance(at, int) else vec[:, bass.ds(at, 1)]

        enabled = STAGE_ORDER if stop_after is None else STAGE_ORDER[:STAGE_ORDER.index(stop_after) + 1]
        n_jobs = max([J0[s] + JOBS_OF[s] for s in enabled if s in J0])

        def job_tiles(j):
            return TILES[j] * P

        block = ctx.enter_context(nc.Block())

        @block.sync
        def _(sp):
            sp.dma_start(x[:], a["x"]).then_inc(x_loaded, 16)
            sp.dma_start(vec[:], a["vec"]).then_inc(vec_loaded, 16)
            sp.dma_start(ident[:], a["consts"][:, 0:P]).then_inc(vec_loaded, 16)
            sp.dma_start(pool_fix[:], a["pool_fix"]).then_inc(vec_loaded, 16)

            def load(stage, q, u):
                j = J0[stage] + u
                n = TILES[j] * P
                if j >= 1:
                    sp.wait_ge(w_lo_done, J0[stage] + q - 1)
                sp.dma_start(w_raw[j % 2][:, 0:n], a["w_" + stage][q]).then_inc(w_loaded[j % 2], 16)

            def load_all(stage):
                n = JOBS_OF[stage]
                if n < 8:
                    for q in range(n):
                        load(stage, q, q)
                else:
                    pairs(sp, n // 2, lambda i: [load(stage, 2 * i + u, u) for u in range(2)])

            ffn_seen = 0
            for stage in enabled:
                if stage in J0:
                    load_all(stage)
                if stage in ("down0", "down1"):
                    l = int(stage[-1])
                    sp.wait_ge(hid_done, NF * (l + 1))
                    sp.dma_start(taps_in[:, :, PAD:], a["p"][l]).then_inc(p_loaded, 16)
                if stage == "ple0" and "kproj" in enabled:
                    sp.wait_ge(w_lo_done, J0["ple0"] + 4)
                    for i, n in enumerate(("cmp_w1_k", "cmp_w1_v")):
                        sp.dma_start(cw1[:, i], a[n]).then_inc(aux_loaded, 16)
                    for i, n in enumerate(("cmp_w2_k", "cmp_w2_k", "cmp_w2_v")):
                        sp.dma_start(cw2[:, i], a[n]).then_inc(aux_loaded, 16)
                    for i, n in enumerate(("cmp_pos_k", "cmp_pos_v")):
                        sp.dma_start(cpos[:, i], a[n]).then_inc(aux_loaded, 16)
                    sp.dma_start(rot[:], a["consts"][:, P:2 * P]).then_inc(aux_loaded, 16)
                    sp.dma_start(mask_bf[:], a["mask_bf"]).then_inc(aux_loaded, 16)
                    sp.dma_start(cmask[:], a["cmask"]).then_inc(aux_loaded, 16)
                    sp.dma_start(pos_i[:], a["positions"].broadcast_to([P, T])).then_inc(pos_loaded, 16)
                if stage == "ein":
                    sp.wait_ge(seg_done, SEG0["ein"])
                    sp.dma_start(sinks[:], a["sinks"].broadcast_to([P, 8])).then_inc(e_loaded, 16)
                    sp.dma_start(relb[:], a["rel_bias"]).then_inc(e_loaded, 16)
                    sp.dma_start(onehot[:], a["onehot"]).then_inc(e_loaded, 16)
                    sp.dma_start(outside[:], a["outside"]).then_inc(e_loaded, 16)
                    sp.dma_start(flip[:], a["consts"][:, 2 * P:3 * P]).then_inc(e_loaded, 16)
                if stage == "einv":
                    sp.wait_ge(diag_vec, 1)
                    sp.dma_start(scratch.ap().rearrange("(h d) -> h d", h=8), diag[:]).then_inc(diag_out, 16)
                    sp.wait_ge(diag_out, 16)
                    spread = bass.AP(tensor=scratch.ap().tensor, offset=0, ap=[[1, P], [BLOCK_F + 1, 8], [1, 2 * P]])
                    sp.dma_start(ebias[:], spread).then_inc(diag_in, 16)
            if stop_after is None:
                for m in range(ND):
                    sp.wait_ge(out_ready, m + 1)
                    sp.dma_start(a["out"][m], x[:, m, :]).then_inc(stored, 16)
                sp.wait_ge(stored, 16 * ND)
            else:
                sp.wait_ge(x_ready, x_before(NEXT_PREP[stop_after]) + ND)
                sp.dma_start(a["out"].rearrange("m p t -> p m t"), x[:]).then_inc(stored, 16)
                sp.wait_ge(stored, 16)

        @block.tensor
        def _(pe):
            def three(out, wh, wl, mh, ml, first, final):
                pe.matmul(out, wh, mh, start=first, stop=False)
                pe.matmul(out, wh, ml, start=False, stop=False)
                return pe.matmul(out, wl, mh, start=False, stop=final)

            def tile_of(slot, n):
                return w_hi[slot][:, n * P:(n + 1) * P], w_lo[slot][:, n * P:(n + 1) * P]

            def stats(prep):
                n = PREP_OF[prep]
                if n == 0:
                    pe.wait_ge(const_set, 3)
                pe.wait_ge(sq_added, 9 * (n + 1))
                pe.matmul(bank[STAT][:], ones[:], sq_sum[:], start=True, stop=True).then_inc(stat_done, 1)

            def up(n):
                stage = f"up{n}"

                def body(i):
                    for u in range(2):
                        f, slot = 2 * i + u, (J0[stage] + u) % 2
                        pe.wait_ge(w_lo_done, J0[stage] + f + 1)
                        for g in range(2):
                            pe.wait_ge(acc_free, FREE0[stage] + 2 * f + g - 3)
                            for k in range(ND):
                                if u == 0 and g == 0:
                                    pe.wait_ge(h_lo_done, H_COUNT[stage] + k + 1)
                                mm = three(bank[2 * u + g][:], *tile_of(slot, g * ND + k), h_hi[:, k], h_lo[:, k],
                                           k == 0, k == ND - 1)
                            mm.then_inc(seg_done, 1)
                            if isinstance(i, int) and 2 * f + g == 0:
                                stats(stage)
                pairs(pe, NF // 2, body, peel=1)

            def down(n):
                stage, nxt = f"down{n}", NEXT_PREP[f"down{n}"]
                pe.wait_ge(acc_free, FREE0[stage])

                def body(i):
                    for u in range(4):
                        m, half, slot = 2 * i + u // 2, u % 2, (J0[stage] + u) % 2
                        pe.wait_ge(w_lo_done, J0[stage] + 4 * i + u + 1)
                        if half == 0:
                            pe.wait_ge(x_ready, x_before(nxt) + m - 1)
                        pe.wait_ge(act_lo_done, NF * n + HALF_F * (half + 1) + 1)
                        for k in range(HALF_F):
                            kk = half * HALF_F + k
                            mm = three(bank[u // 2][:], *tile_of(slot, k), act_hi[:, kk], act_lo[:, kk],
                                       kk == 0, kk == NF - 1)
                        mm.then_inc(seg_done, 1)
                pairs(pe, ND // 2, body)

            def ple(l):
                stage = f"ple{l}"
                stats(stage)

                def body(i):
                    for u in range(2):
                        m, slot = 2 * i + u, (J0[stage] + u) % 2
                        pe.wait_ge(w_lo_done, J0[stage] + m + 1)
                        pe.wait_ge(acc_free, FREE0[stage] + 2 * m - 3)
                        for k in range(ND):
                            if u == 0:
                                pe.wait_ge(h_lo_done, H_COUNT[stage] + k + 1)
                            mm = three(bank[2 * u][:], *tile_of(slot, k), h_hi[:, k], h_lo[:, k], k == 0, k == ND - 1)
                        mm.then_inc(seg_done, 1)
                        pe.wait_ge(acc_free, FREE0[stage] + 2 * m - 2)
                        pe.wait_ge(p_lo_done, 2 * (l + 1))
                        for k in range(2):
                            mm = three(bank[2 * u + 1][:], *tile_of(slot, ND + k), p_hi[:, k], p_lo[:, k], k == 0, k == 1)
                        mm.then_inc(seg_done, 1)
                pairs(pe, ND // 2, body)

            def dense(stage, q, hi, lo, ready, base, residual=None, after=None, chunks=ND):
                j = J0[stage] + q
                pe.wait_ge(w_lo_done, j + 1)
                for g in range(2):
                    n = 2 * q + g
                    if residual is None:
                        pe.wait_ge(acc_free, FREE0[stage] + n - 3)
                    elif n >= 4:
                        pe.wait_ge(x_ready, x_before(residual) + n - 3)
                    for k in range(ND):
                        if n == 0 and k < chunks:
                            pe.wait_ge(ready, base + k + 1)
                        mm = three(bank[n % 4][:], *tile_of(j % 2, g * ND + k), hi[:, k], lo[:, k], k == 0, k == ND - 1)
                    mm.then_inc(seg_done, 1)
                    if after is not None:
                        after(n)

            def rotate(r, width=T):
                pe.wait_ge(cmp_vec if r == 4 else acc_free, 2 if r == 4 else ROPE_FREE[r])
                if r >= 2:
                    pe.wait_ge(roped, r - 1)
                pe.matmul(bank[5 + r % 2][:, 0:width], rot[:], hid[:, r % 2, 0:width], start=True, stop=True)\
                    .then_inc(rot_done, 1)

            def turn_rs(count):
                pe.wait_ge(rs_done, count)
                for t in range(NT):
                    mm = pe.transpose(bank[MISC][:, t * P:(t + 1) * P], rs[:, t * P:(t + 1) * P], ident[:])
                mm.then_inc(rs_turned, 1)

            def pool():
                stats("start")
                pe.wait_ge(w_lo_done, 1)
                for m in range(ND):
                    if m >= 4:
                        pe.wait_ge(x_ready, m - 3)
                    for k in range(2):
                        if m % 2 == 0:
                            pe.wait_ge(pool_lo_done, m + k + 1)
                        mm = three(bank[m % 4][:], *tile_of(0, 2 * m + k), h_hi[:, m // 2 * 2 + k],
                                   h_lo[:, m // 2 * 2 + k], k == 0, k == 1)
                    mm.then_inc(seg_done, 1)

            def attention_inputs():
                def after_key(n):
                    if n == 0:
                        stats("kv")
                    if n >= 5:
                        rotate(n - 5)

                pe.wait_ge(aux_loaded, 16 * 10)
                for q in range(4):
                    dense("kproj", q, h_hi, h_lo, h_lo_done, H_COUNT["kv"], after=after_key)
                turn_rs(PREP_OF["kv"] + 1)
                for q in range(2):
                    j = J0["vproj"] + q
                    pe.wait_ge(w_lo_done, j + 1)
                    for kk in range(4):
                        k = 4 * q + kk
                        for t in range(NT):
                            if k == 0:
                                pe.wait_ge(acc_free, FREE0["vproj"] + t - 3)
                            cols = slice(t * P, (t + 1) * P)
                            w = slice(kk * T, (kk + 1) * T)
                            mm = three(bank[t][:], h_hi[:, k, cols], h_lo[:, k, cols], w_hi[j % 2][:, w],
                                       w_lo[j % 2][:, w], k == 0, k == ND - 1)
                            if k == ND - 1 or (k == 3 and t == NT - 1):
                                mm.then_inc(seg_done, 1)
                        if k == 0:
                            rotate(3)
                j = J0["gates"]
                pe.wait_ge(w_lo_done, j + 1)
                pe.wait_ge(h2_lo_done, ND)
                pe.wait_ge(acc_free, FREE0["gates"] - 1)
                for k in range(ND):
                    w = slice(k * 3 * NH, (k + 1) * 3 * NH)
                    mm = three(bank[2][0:3 * NH, :], w_hi[j % 2][:, w], w_lo[j % 2][:, w], o_hi[:, k], o_lo[:, k],
                               k == 0, k == ND - 1)
                mm.then_inc(seg_done, 1)
                pe.wait_ge(acc_free, FREE0["kproj"] + 4)
                for i in range(2):
                    for jj in range(CS):
                        pe.matmul(bank[STAT][:, 256 + i:257 + i], cw1[:, i, jj], cpos[:, i, jj:jj + 1],
                                  start=jj == 0, stop=jj == CS - 1)
                    for jj in range(CS):
                        blocks = kvc[:, i, :, 2 * jj:2 * jj + CS * (NCMP - 1) + 1:CS]
                        mm = pe.matmul(bank[STAT][:, 128 * i:128 * i + NG * NCMP], cw1[:, i, jj], blocks,
                                       start=jj == 0, stop=jj == CS - 1)
                    mm.then_inc(cmp_mm, 1)
                pe.wait_ge(acc_free, FREE0["gates"] + 1)
                for t in range(NT):
                    mm = pe.transpose(bank[3][:, t * 3 * NH:(t + 1) * 3 * NH], sq[0:3 * NH, t * P:(t + 1) * P],
                                      ident[0:3 * NH, 0:3 * NH])
                mm.then_inc(seg_done, 1)
                dense("qproj", 0, o_hi, o_lo, h2_lo_done, 0)
                pe.wait_ge(cmp_act, 6)
                pe.wait_ge(cmp_vec, 1)
                pe.matmul(bank[MISC][:, 0:NG * NC], cw2[:, 0:2].rearrange("p a d -> p (a d)"),
                          taps_in[:, 0, PAD:PAD + NG * NC], start=True, stop=True)
                for g in range(NG):
                    at = PAD + g * P
                    mm = pe.matmul(bank[MISC][:, P + g * HD:P + (g + 1) * HD], taps_in[:, 1, at:at + P], cw2[:, 2],
                                   start=True, stop=True)
                mm.then_inc(cmp_mm, 1)
                for q in range(1, 4):
                    def after(n):
                        if n == 2:
                            rotate(4, NG * NC)
                        rotate(5 + n - 2)
                        if n == 7:
                            rotate(11)
                            rotate(12)
                    dense("qproj", q, o_hi, o_lo, h2_lo_done, 0, after=after)

            def attention():
                pe.wait_ge(roped, 13)
                pe.wait_ge(acc_free, FREE0["qproj"] + 8)

                def cscores(t):
                    for c in range(ND):
                        mm = pe.matmul(bank[t][:, 2 * c * NC:2 * (c + 1) * NC], qT[:, c, t * P:(t + 1) * P],
                                       kcT[:, c // 4].rearrange("p h c -> p (h c)"), start=True, stop=True)
                    mm.then_inc(cs_mm, 1)

                def compressed_turned():
                    for t in range(NT):
                        pe.wait_ge(cs_vec, CS_DONE + t // 2)
                        if t >= 2:
                            pe.wait_ge(cs_kept, t - 1)
                        for g in range(NG):
                            mm = pe.transpose(bank[4 + t % 2][:, g * P:(g + 1) * P], e4[:, t, g * P:(g + 1) * P], ident[:])
                        mm.then_inc(cs_turned, 1)

                for t in range(NT):
                    cscores(t)

                def qk(u, t):
                    c, half, b, g, s = unit(u)
                    rows, n = slice(half * HD, (half + 1) * HD), (t + 1) * P
                    if u >= 1:
                        pe.wait_ge(exp_done, 4 * (u - 1) + t + 1)
                    else:
                        pe.wait_ge(cs_vec, t + 1)
                    pe.matmul(bank[t][:, 0:n], qT[rows, c, t * P:(t + 1) * P], kT[rows, 2 * b + g // 2, 0:n],
                              start=True, stop=False)
                    pe.matmul(bank[t][:, t * P:n], mask_bf[:, 0], mask_bf[:, 1], start=False, stop=True)\
                        .then_inc(qk_done, 1)

                def turn(u, kb):
                    n = 4 * u + kb
                    if kb == 0:
                        pe.wait_ge(scaled, 3 * u + 3)
                        pe.wait_ge(scaled_a, u + 1)
                    if n >= 2:
                        pe.wait_ge(kept_v if kb % 2 == 0 else kept_a, (n - 2) // 2 + 1)
                    else:
                        pe.wait_ge(cs_kept, NT)
                    for t in range(kb, NT):
                        at = t * (t + 1) // 2 * P + kb * P
                        mm = pe.transpose(bank[4 + kb % 2][:, t * P:(t + 1) * P], probs[u % 3][:, at:at + P], ident[:])
                    mm.then_inc(turned, 1)

                def pv(u, kb):
                    c, half, b, g, s = unit(u)
                    out = bank[6 + c % 2][half * HD:(half + 1) * HD, :]
                    if b == 0 and kb == 0:
                        if c >= 2:
                            pe.wait_ge(o_lo_done, c - 1)
                        rep = slice(32 * (s % 4), 32 * (s % 4) + 32)
                        pe.matmul(out, vcm[rep, g], pcT[rep, s // 4], start=True, stop=False)
                    pe.wait_ge(kept_v if kb % 2 == 0 else kept_a, 2 * u + kb // 2 + 1)
                    v = vsw[:, kb, 256 * b + g * HD:256 * b + (g + 1) * HD]
                    pe.matmul(out[:, kb * P:T], v, hid[:, kb % 2, kb * P:T], start=False,
                              stop=(b == 1 and kb == NT - 1)).then_inc(pv_done, 1)

                for u in range(UNITS + 3):
                    now, back = u < UNITS, 2 <= u < UNITS + 2
                    for part, kb in UNIT_ORDER_PE:
                        if part == "qk" and now:
                            qk(u, kb)
                        elif part == "turn" and back:
                            turn(u - 2, kb)
                        elif part == "pv" and kb == 3 and u >= 3:
                            pv(u - 3, kb)
                        elif part == "pv" and kb < 3 and back:
                            pv(u - 2, kb)
                    if u == 0:
                        compressed_turned()

            def even():
                for q in range(6):
                    dense("ein", q, h_hi, h_lo, h_lo_done, H_COUNT["mixe"],
                          after=lambda n: stats("mixe") if n == 0 else None)
                pe.wait_ge(e_loaded, 16 * 5)
                pe.matmul(bank[MISC][0:8, 0:BLOCK_F + 1], relb[:], onehot[:], start=True, stop=True).then_inc(diag_mm, 1)
                j = J0["einv"]
                pe.wait_ge(w_lo_done, j + 1)
                pe.wait_ge(acc_free, FREE0["einv"] - 3)
                for k in range(ND):
                    mm = three(bank[0][:], *tile_of(j % 2, k), h_hi[:, k], h_lo[:, k], k == 0, k == ND - 1)
                mm.then_inc(seg_done, 1)
                for t in range(NT):
                    pe.wait_ge(acc_free, FREE0["einv"] + t - 2)
                    cols = slice(t * P, (t + 1) * P)
                    for k in range(ND):
                        wh, wl = tile_of(j % 2, ND + k)
                        mm = three(bank[(t + 1) % 4][:, 0:P], h_hi[:, k, cols], h_lo[:, k, cols], wh, wl, k == 0,
                                   k == ND - 1)
                    mm.then_inc(seg_done, 1)
                pe.wait_ge(diag_vec, 1)
                turn_rs(PREP_OF["mixe"] + 1)
                pe.wait_ge(diag_in, 16)
                for i in range(4):
                    if i >= 2:
                        pe.wait_ge(bias_kept, i - 1)
                    pe.matmul(bank[5 + i % 2][:], flip[:], ebias[:, 2 * i:2 * i + 2].rearrange("p h s -> p (h s)"),
                              start=True, stop=True).then_inc(flipped, 1)
                pe.wait_ge(acc_free, FREE0["einv"] + 5)

                def qk(u, t):
                    r, half = u // 2, u % 2
                    rows = slice(half * HD, (half + 1) * HD)
                    lo, n = (0, P) if t == 0 else ((t - 1) * P, 2 * P)
                    if u >= 1:
                        pe.wait_ge(scaled, E_SCALED0 + 4 * (u - 1) + t + 1)
                    pe.matmul(bank[t][:, 0:n], eq[rows, r, t * P:(t + 1) * P], eq[rows, 4, lo:lo + n],
                              start=True, stop=True).then_inc(qk_done, 1)

                def turn(u, t):
                    n = 4 * u + t
                    pe.wait_ge(e_norm, n + 1)
                    if n >= 2:
                        pe.wait_ge(kept_a, E_KEPT_A0 + n - 1)
                    for b in range(0 if t else 1, 2):
                        mm = pe.transpose(bank[4 + t % 2][:, b * P:(b + 1) * P], eprobs[u % 3][:, t, b * P:(b + 1) * P],
                                          ident[:])
                    mm.then_inc(turned, 1)

                def pv(u, t):
                    r, half = u // 2, u % 2
                    out = bank[6][half * HD:(half + 1) * HD, t * P:(t + 1) * P]
                    if half == 0 and t == 0 and r:
                        pe.wait_ge(o_lo_done, ND + r)
                    pe.wait_ge(kept_a, E_KEPT_A0 + 4 * u + t + 1)
                    for b in range(0 if t else 1, 2):
                        mm = pe.matmul(out, ev[:, t - 1 + b, half * HD:(half + 1) * HD],
                                       hid[:, t % 2, b * P:(b + 1) * P], start=(b == 0 or t == 0), stop=b == 1)
                    mm.then_inc(pv_done, 1)

                for u in range(E_UNITS + 3):
                    now, back = u < E_UNITS, 2 <= u < E_UNITS + 2
                    for part, t in UNIT_ORDER_PE:
                        if part == "qk" and now:
                            qk(u, t)
                        elif part == "turn" and back:
                            turn(u - 2, t)
                        elif part == "pv" and t == 3 and u >= 3:
                            pv(u - 3, t)
                        elif part == "pv" and t < 3 and back:
                            pv(u - 2, t)
                    if u in LN_AT:
                        i = LN_AT.index(u)
                        pe.wait_ge(ln_add, 4 * i + 4)
                        if i:
                            pe.wait_ge(ln_vec, CC)
                        pe.matmul(bank[LN][:], ones[:], sq[:] if i == 0 else sq_sum[:], start=True, stop=True)\
                            .then_inc(ln_mm, 1)

            def odd():
                for q in range(4):
                    dense("rec", q, h_hi, h_lo, h_lo_done, H_COUNT["mixo"],
                          after=lambda n: stats("mixo") if n == 0 else None)
                def lru_gates(c):
                    j = J0["lgate"]
                    pe.wait_ge(rc_lo, c + 1)
                    for g in range(2):
                        n = 2 * c + g
                        if n >= 4:
                            pe.wait_ge(g_sig, n - 3)
                        three(bank[4 + n % 4][:], *tile_of(j % 2, g * ND + c), r_hi[:, c], r_lo[:, c], True, True)\
                            .then_inc(lgate_done, 1)

                def half_the_heads(n):
                    if n < 2:
                        for c in range(4 * n, 4 * n + 4):
                            lru_gates(c)

                pe.wait_ge(w_lo_done, J0["lgate"] + 1)
                pe.wait_ge(root_done, PREP_OF["mixo"] + 1)
                for q in range(4):
                    dense("ogate", q, h_hi, h_lo, h_lo_done, H_COUNT["mixo"], after=half_the_heads)

            for stage in enabled:
                if stage == "pool":
                    pool()
                elif stage.startswith("up"):
                    up(int(stage[2:]))
                elif stage.startswith("down"):
                    down(int(stage[4:]))
                elif stage.startswith("ple"):
                    ple(int(stage[3:]))
                elif stage == "kproj":
                    attention_inputs()
                elif stage == "attn":
                    attention()
                elif stage == "final1":
                    stats("final1")
                elif stage == "ein":
                    even()
                elif stage == "rec":
                    odd()
                elif stage == "final2":
                    stats("final2")
                elif stage == "wout0":
                    for q in range(4):
                        dense(stage, q, o_hi, o_lo, o_lo_done, 0, residual="up1")
                elif stage == "wout1":
                    pe.wait_ge(ln_lo, 4)
                    for q in range(4):
                        dense(stage, q, e_hi, e_lo, o_lo_done, ND, residual="up3", chunks=4)
                elif stage == "wout2":
                    pe.wait_ge(acc_free, FREE0["ogate"] + ND)
                    for q in range(4):
                        dense(stage, q, r_hi, r_lo, y_lo, 0, residual="up5")

        @block.scalar
        def _(act):
            def split_w(j, count=None, segs=None):
                if j >= n_jobs:
                    return
                act.wait_ge(w_loaded[j % 2], 16 * (j // 2 + 1) if count is None else count)
                if j >= 2:
                    act.wait_ge(seg_done, SEGS_BEFORE[j - 1] if segs is None else segs)
                n = TILES[j] * P
                act.activation(w_hi[j % 2][:, 0:n], w_raw[j % 2][:, 0:n], ACT.Copy).then_inc(w_hi_done, 1)

            def wait_apart(s, count):
                act.wait_ge(s, count)
                if not isinstance(count, int):
                    act.wait_ge(const_set, 3)

            def root(prep):
                n = PREP_OF[prep]
                act.wait_ge(stat_done, n + 1)
                act.activation(rs[:], bank[STAT][:], ACT.Sqrt, bias=eps[:, 0:1], scale=1.0 / D).then_inc(root_done, 1)

            def wait_x(prep, m):
                n = PREP_OF[prep]
                act.wait_ge(sq_added, 9 * n + m + 1)
                if n:
                    wait_apart(x_ready, x_before(prep) + m + 1)
                else:
                    act.wait_ge(x_loaded, 16)

            def hi_of_x(prep, m):
                act.activation(h_hi[:, m], x[:, m], ACT.Copy, scale=col(GAIN[prep], m)).then_inc(h_hi_done, 1)

            def square(prep, m):
                act.activation(sq[:], x[:, m], ACT.Square).then_inc(sq_done, 1)

            def prepare(prep, m):
                if prep in GAIN:
                    if isinstance(m, int):
                        act.wait_ge(x_ready, x_before(prep) + m + 1)
                    else:
                        wait_x(prep, m)
                    hi_of_x(prep, m)
                    if isinstance(m, int):
                        act.wait_ge(sq_added, 9 * PREP_OF[prep] + m + 1)
                else:
                    wait_x(prep, m)
                square(prep, m)

            def conv_up(l):
                stage = f"up{l}"
                n0, j0, s0 = l * NF, J0[stage], SEG0[stage]

                split_w(j0 + 1)
                root(stage)

                def body(i):
                    for u in range(2):
                        f, j = 2 * i + u, j0 + u + 2
                        if not isinstance(i, int):
                            split_w(j, 16 * (j // 2 + 1) + 16 * i, s0 + 2 * f + 2)
                        elif f < NF - 1:
                            split_w(j0 + f + 2)
                        act.wait_ge(hid_done, n0 + f)
                        for g in (1, 0):
                            wait_apart(acc_free, FREE0[stage] + 2 * f + 2)
                            act.activation(bank[CONV_A + g][:], taps_in[:, g, PAD:], ACT.Identity,
                                           bias=col(f"conv{l}_b", g * NF + f), scale=col(f"conv{l}_2", g * NF + f))\
                                .then_inc(seeded, 1)
                        act.wait_ge(tapped, 4 * (n0 + f) + 3)
                        act.activation(silu_g[:], bank[CONV_G][:], ACT.Silu).then_inc(silu_done, 1)
                        wait_apart(hid_done, n0 + f + 1)
                        act.activation(act_hi[:, f], hid[:, u], ACT.Copy).then_inc(act_hi_done, 1)
                pairs(act, NF // 2, body)

            def glu_up(n):
                stage = f"up{n}"
                n0, j0, s0 = n * NF, J0[stage], SEG0[stage]

                def body(i):
                    for u in range(2):
                        f, j = 2 * i + u, j0 + u
                        if isinstance(i, int):
                            split_w(j0 + f + 1)
                            if f == 0:
                                root(stage)
                        else:
                            split_w(j + 1, 16 * ((j + 1) // 2 + 1) + 16 * i, s0 + 2 * f)
                        act.wait_ge(acc_free, FREE0[stage] + 2 * f + 1)
                        act.wait_ge(hid_done, n0 + f)
                        act.activation(silu_g[:], taps_in[:, u, PAD:], ACT.Silu).then_inc(silu_done, 1)
                        wait_apart(hid_done, n0 + f + 1)
                        act.activation(act_hi[:, f], hid[:, u], ACT.Copy).then_inc(act_hi_done, 1)
                pairs(act, NF // 2, body, peel=1)

            def down(n):
                stage, nxt = f"down{n}", NEXT_PREP[f"down{n}"]
                j0, s0 = J0[stage], SEG0[stage]

                def body(i):
                    for u in range(4):
                        q, j = 4 * i + u, j0 + u
                        if isinstance(i, int):
                            split_w(j0 + q + 1)
                        else:
                            split_w(j + 1, 16 * ((j + 1) // 2 + 1) + 32 * i, s0 + q)
                        if u % 2 == 1:
                            prepare(nxt, 2 * i + u // 2)
                pairs(act, ND // 2, body)

            def ple(l):
                stage, nxt = f"ple{l}", NEXT_PREP[f"ple{l}"]
                j0, s0 = J0[stage], SEG0[stage]
                act.wait_ge(p_loaded, 16 * (l + 1))
                for k in range(2):
                    act.activation(p_hi[:, k], taps_in[:, k, PAD:], ACT.Copy).then_inc(p_hi_done, 1)
                root(stage)

                def body(i):
                    for u in range(2):
                        m, j = 2 * i + u, j0 + u
                        if isinstance(i, int):
                            split_w(j0 + m + 1)
                        else:
                            split_w(j + 1, 16 * ((j + 1) // 2 + 1) + 16 * i, s0 + 2 * m)
                        act.wait_ge(acc_free, FREE0[stage] + 2 * m + 1)
                        act.activation(ple_t[:, u], ple_t[:, u], ACT.Sigmoid).then_inc(sig_done, 1)
                        wait_x(nxt, m)
                        square(nxt, m)
                pairs(act, ND // 2, body)
                if nxt in GAIN:
                    act.wait_ge(seg_done, SEGS_BEFORE[J0[stage] + ND])
                    for m in range(ND):
                        hi_of_x(nxt, m)

            def start():
                act.wait_ge(const_set, 3)
                act.wait_ge(vec_loaded, 48)
                for m in range(ND):
                    prepare("start", m)
                split_w(0)
                root("start")

            def pool():
                split_w(1)
                for m in range(ND):
                    act.wait_ge(pool_step, POOL_U[m // 2])
                    act.activation(h_hi[:, m], pool_u[:, m // 2 % 2, m % 2], ACT.Copy).then_inc(pool_hi_done, 1)
                act.wait_ge(seg_done, ND)
                for m in range(ND):
                    prepare("up0", m)

            def attention_inputs():
                for m in range(ND):
                    act.activation(o_hi[:, m], x[:, m], ACT.Copy, scale=col("mix1", m)).then_inc(h2_hi_done, 1)
                root("kv")
                split_w(J0["kproj"] + 1)
                for i in range(2):
                    act.wait_ge(trig_step, 9 + 3 * i)
                    act.activation(rsin[:] if i == 0 else rcos[:], ang[2 + i][:], ACT.Sin).then_inc(sin_done, 1)
                for j in range(J0["kproj"] + 2, J0["qproj"] + 1):
                    split_w(j)
                act.wait_ge(acc_free, FREE0["gates"] + 2)
                act.activation(gates[:], gates[:], ACT.Sigmoid).then_inc(gates_done, 1)
                act.wait_ge(cmp_mm, 2)
                act.activation(cpos_b[:], bank[STAT][:, 256:258], ACT.Copy).then_inc(cmp_act, 1)
                act.wait_ge(cmp_act, 1)
                act.wait_ge(cmp_vec, 1)
                hk = taps_in[:, 0, PAD:PAD + NG * NC].rearrange("p (g c) -> p g c", g=NG)
                act.activation(hk[:, :, 0:NCMP], bank[STAT][:, 0:NG * NCMP].rearrange("p (g c) -> p g c", g=NG),
                               ACT.Gelu_apprx_tanh, bias=cpos_b[:, 0:1]).then_inc(cmp_act, 1)
                hv = taps_in[:, 1, PAD:].rearrange("p (g r c) -> p g r c", g=NG, r=4)
                for r in range(4):
                    act.activation(hv[:, :, r, 0:NCMP],
                                   bank[STAT][:, P:P + NG * NCMP].rearrange("p (g c) -> p g c", g=NG),
                                   ACT.Gelu_apprx_tanh, bias=cpos_b[:, 1:2]).then_inc(cmp_act, 1)
                for j in range(J0["qproj"] + 1, J0["wout0"] + 1):
                    split_w(j)

            def attention():
                def exps(u, t):
                    st, at, n = stat4[:, u % 2], t * (t + 1) // 2 * P, (t + 1) * P
                    act.wait_ge(nmax_done, 4 * u + t + 1)
                    if t == 0 and u >= 3:
                        act.wait_ge(turned, 4 * (u - 2))
                    act.activation(probs[u % 3][:, at:at + n], bank[t][:, 0:n], ACT.Exp, bias=st[:, 1, t:t + 1],
                                   accum_out=st[:, 2, t:t + 1]).then_inc(exp_done, 1)

                def scale_last(u):
                    to = probs[u % 3][:, 6 * P:10 * P]
                    act.wait_ge(fac_done, 2 * u + 2)
                    act.activation(to, to, ACT.Copy, scale=stat4[:, u % 2, 3, 3:4]).then_inc(scaled_a, 1)

                def keep(u, kb):
                    act.wait_ge(turned, 4 * u + kb + 1)
                    if 4 * u + kb >= 2:
                        act.wait_ge(pv_done, 4 * u + kb - 1)
                    act.activation(hid[:, 1, kb * P:T], bank[5][:, kb * P:T], ACT.Copy).then_inc(kept_a, 1)

                def keep_o(c):
                    act.wait_ge(pv_done, 16 * (c + 1))
                    act.activation(o_hi[:, c], bank[6 + c % 2][:], ACT.Copy).then_inc(o_hi_done, 1)

                for half in range(2):
                    act.wait_ge(cs_vec, CS_SHIFTED + half)
                    act.activation(e4[:, 2 * half:2 * half + 2], e4[:, 2 * half:2 * half + 2], ACT.Exp).then_inc(cs_exp, 1)
                for u in range(UNITS + 2):
                    now, back = u < UNITS, u >= 2
                    for part, kb in UNIT_ORDER_ACT:
                        if part == "exp" and now:
                            exps(u, kb)
                        elif part == "scale" and 1 <= u <= UNITS:
                            scale_last(u - 1)
                        elif part == "keep" and back:
                            keep(u - 2, kb)
                    if u >= 6 and u % 4 == 2:
                        keep_o((u - 6) // 4)
                    if u == 0:
                        for t in range(NT):
                            act.wait_ge(cs_turned, t + 1)
                            act.activation(pcT[:, :, t * P:(t + 1) * P],
                                           bank[4 + t % 2][:].rearrange("p (g q) -> p g q", g=NG), ACT.Copy)\
                                .then_inc(cs_kept, 1)
                keep_o(ND - 1)

            def residual(stage):
                nxt = NEXT_PREP[stage]
                for q in range(4):
                    split_w(J0[stage] + q + 1)
                    for g in range(2):
                        prepare(nxt, 2 * q + g)

            def even():
                for c in range(6):
                    split_w(J0["ein"] + c + 1)
                    if c == 0:
                        root("mixe")
                    if c < 4:
                        act.wait_ge(acc_free, FREE0["ein"] + 2 * c + 2)
                        act.activation(taps_in[:, c % 2, PAD:], taps_in[:, c % 2, PAD:], ACT.Sigmoid).then_inc(glu_sig, 1)
                        act.wait_ge(glu_done, c + 1)
                        act.activation(cy[:, c], glu[:, c, TAPS - 1:], ACT.Identity, bias=col("cb_b", c),
                                       scale=col("cb_w", (TAPS - 1) * CC + c)).then_inc(y_seed, 1)
                split_w(J0["wout1"])

                def exps(u):
                    st = estat[:, u % 2]
                    act.wait_ge(nmax_done, 4 * UNITS + u + 1)
                    for t in range(NT):
                        cols = slice(P if t == 0 else 0, 2 * P)
                        e = eprobs[u % 3][:, t, cols]
                        act.activation(e, e, ACT.Exp, bias=st[:, 1, t:t + 1], accum_out=st[:, 2, t:t + 1])\
                            .then_inc(exp_done, 1)
                    act.activation(st[:, 0], st[:, 1], ACT.Exp, bias=sinks[:, u:u + 1]).then_inc(exp_done, 1)

                def keep(u, t):
                    n = 4 * u + t
                    act.wait_ge(turned, E_TURNED0 + n + 1)
                    if n >= 2:
                        act.wait_ge(pv_done, E_PV0 + n - 1)
                    cols = slice(P if t == 0 else 0, 2 * P)
                    act.activation(hid[:, t % 2, cols], bank[4 + t % 2][:, cols], ACT.Copy).then_inc(kept_a, 1)

                for u in range(E_UNITS + 3):
                    if u == LN_AT[1] + 1:
                        act.wait_ge(ln_mm, 2)
                        act.activation(silu_g[:], bank[LN][:], ACT.Sqrt, bias=eps[:, 1:2], scale=1.0 / (CC * P))\
                            .then_inc(ln_act, 1)
                    if 2 <= u < E_UNITS + 2:
                        for t in (0, 1):
                            keep(u - 2, t)
                    if u >= 4 and u % 2 == 0:
                        r = (u - 4) // 2
                        act.wait_ge(pv_done, E_PV0 + 8 * (r + 1))
                        act.activation(e_hi[:, r], bank[6][:], ACT.Copy).then_inc(o_hi_done, 1)
                    if 2 <= u < E_UNITS + 2:
                        for t in (2, 3):
                            keep(u - 2, t)
                    if u < E_UNITS:
                        exps(u)
                    if u == LN_AT[0] + 1:
                        for c in range(CC):
                            act.wait_ge(ln_vec, c + 1)
                            if c >= 1:
                                act.wait_ge(ln_add, 4 + c)
                            act.activation(sq[:], cy[:, c], ACT.Square).then_inc(ln_sq, 1)
                    if u == LN_AT[1] + 2:
                        for c in range(CC):
                            act.wait_ge(ln_vec, CC + 2 + c)
                            act.activation(cy[:, c], cy[:, c], ACT.Silu, bias=col("ln_b", c), scale=col("ln_g", c))\
                                .then_inc(ln_act, 1)
                        for c in range(CC):
                            act.wait_ge(ln_act, 2 + c)
                            act.activation(e_hi[:, CC + c], cy[:, c], ACT.Copy).then_inc(ln_hi, 1)
            def odd():
                act.wait_ge(lam_vec, 1)
                act.activation(lt[:, 1], lt[:, 0], ACT.Exp, scale=-1.0).then_inc(lam_act, 1)
                for q in range(4):
                    split_w(J0["rec"] + q + 1)
                    if q == 0:
                        root("mixo")
                    for g in range(2):
                        c = 2 * q + g
                        act.wait_ge(acc_free, FREE0["rec"] + c + 1)
                        act.activation(rc[:, c], taps_in[:, g, PAD:], ACT.Identity, bias=col("lru_b", c),
                                       scale=col("lru_w", 3 * ND + c)).then_inc(r_seed, 1)
                        act.wait_ge(r_tap, 3 * c + 3)
                        act.activation(r_hi[:, c], rc[:, c], ACT.Copy).then_inc(rc_hi, 1)
                split_w(J0["ogate"])
                for c in range(ND):
                    for g, (to, bias) in enumerate(((ra, "ga_b"), (ri, "gx_b"))):
                        act.wait_ge(lgate_done, 2 * c + g + 1)
                        act.activation(to[:, c], bank[4 + (2 * c + g) % 4][:], ACT.Sigmoid, bias=col(bias, c))\
                            .then_inc(g_sig, 1)
                split_w(J0["ogate"] + 1)
                act.wait_ge(lam_vec, LAM_STEPS)
                act.wait_ge(g_sig, 2 * ND)

                def factors(hh):
                    for k in range(4):
                        if hh:
                            act.wait_ge(lru_vec, 4 * k + 2)
                        c = 4 * hh + k
                        act.activation(expv[:, k], ra[:, c], ACT.Exp, scale=sp8[:, c:c + 1]).then_inc(lru_act, 1)
                    for k in range(4):
                        c = 4 * hh + k
                        act.wait_ge(lru_act, 12 * hh + k + 1)
                        act.activation(ra[:, c], ra[:, c], ACT.Tanh, scale=sp4[:, c:c + 1]).then_inc(lru_act, 1)
                    for k in range(4):
                        c = 4 * hh + k
                        act.wait_ge(lru_act, 12 * hh + 4 + k + 1)
                        act.wait_ge(lru_pool, c + 1)
                        act.activation(rc[:, c], ra[:, c], ACT.Sqrt).then_inc(lru_act, 1)

                def gate_chunk(c):
                    act.wait_ge(acc_free, FREE0["ogate"] + c + 1)
                    act.activation(taps_in[:, c % 2, PAD:], taps_in[:, c % 2, PAD:], ACT.Gelu_apprx_tanh)\
                        .then_inc(gel_done, 1)
                    act.wait_ge(y_done, c + 1)
                    act.activation(r_hi[:, c], hid[:, c % 2], ACT.Copy).then_inc(y_hi, 1)

                factors(0)
                split_w(J0["ogate"] + 2)
                factors(1)
                for c in range(ND):
                    if c in (2, 4):
                        split_w(J0["ogate"] + 2 + c // 2)
                    gate_chunk(c)

            for stage in enabled:
                if stage == "pool":
                    start()
                    pool()
                elif stage in ("up0", "up1"):
                    conv_up(int(stage[2:]))
                elif stage.startswith("up"):
                    glu_up(int(stage[2:]))
                elif stage.startswith("down"):
                    down(int(stage[4:]))
                elif stage.startswith("ple"):
                    ple(int(stage[3:]))
                elif stage == "kproj":
                    attention_inputs()
                elif stage == "attn":
                    attention()
                elif stage == "final1":
                    root("final1")
                    for m in range(ND):
                        prepare("up2", m)
                elif stage == "final2":
                    root("final2")
                elif stage in ("wout0", "wout1", "wout2"):
                    residual(stage)
                elif stage == "ein":
                    even()
                elif stage == "rec":
                    odd()

        @block.vector
        def _(dve):
            def split_w(j, count=None):
                if j >= n_jobs:
                    return
                dve.wait_ge(w_hi_done, j + 1 if count is None else count)
                n = TILES[j] * P
                dve.tensor_tensor(w_lo[j % 2][:, 0:n], w_raw[j % 2][:, 0:n], w_hi[j % 2][:, 0:n].bitcast(F32),
                                  ALU.subtract).then_inc(w_lo_done, 1)

            def norm_factors(prep):
                n = PREP_OF[prep]
                dve.wait_ge(root_done, n + 1)
                dve.reciprocal(rs[:], rs[:]).then_inc(rs_done, 1)
                dve.wait_ge(rs_done, n + 1)

            def split_x(prep, m):
                dve.wait_ge(h_hi_done, H_COUNT[prep] + m + 1)
                dve.scalar_tensor_tensor(out=h_lo[:, m], in0=x[:, m], scalar=col(GAIN[prep], m),
                                         in1=h_hi[:, m].bitcast(F32), op0=ALU.mult, op1=ALU.subtract).then_inc(h_lo_done, 1)

            def add_to_x(prep, m, acc, factor):
                dve.scalar_tensor_tensor(out=x[:, m], in0=acc, scalar=factor, in1=x[:, m], op0=ALU.mult,
                                         op1=ALU.add).then_inc(x_ready, 1)
                dve.wait_ge(x_ready, x_before(prep) + m + 1)

            def start():
                dve.memset(ones[:], 1.0).then_inc(const_set, 1)
                dve.memset(eps[:, 0:1], EPS).then_inc(const_set, 1)
                dve.memset(eps[:, 1:2], LN_EPS).then_inc(const_set, 1)
                dve.memset(taps_in[:], 0.0).then_inc(acc_free, 1)
                dve.memset(pool_h[:, :, 0:CS], 0.0).then_inc(acc_free, 1)
                for i in range(2):
                    dve.memset(pool_w[i][:, :, 0:CS], 0.0).then_inc(acc_free, 1)
                dve.wait_ge(acc_free, 4)
                dve.wait_ge(x_loaded, 16)
                dve.wait_ge(vec_loaded, 48)
                split_w(0)
                norm_factors("start")

            def pool():
                for m in range(ND):
                    dve.scalar_tensor_tensor(out=pool_h[:, m, CS:], in0=x[:, m], scalar=col("mix0", m), in1=rs[:],
                                             op0=ALU.mult, op1=ALU.mult).then_inc(pool_step, 1)
                step = ND
                for g, w in enumerate(POOL_WINDOWS):
                    pair = pool_h[:, 2 * g:2 * g + 2]
                    cur = pair
                    for s in range(g + 1):
                        dve.wait_ge(pool_step, step)
                        to = pool_w[s % 2]
                        dve.tensor_tensor(to[:, :, CS:], cur[:, :, CS:], cur[:, :, CS - 2 ** s:CS - 2 ** s + T], ALU.add)\
                            .then_inc(pool_step, 1)
                        step += 1
                        cur = to
                    dve.wait_ge(pool_step, step)
                    fix = pool_fix[:, g].unsqueeze(1).broadcast_to([P, 2, CS])
                    dve.tensor_tensor(cur[:, :, CS:2 * CS], cur[:, :, CS:2 * CS], fix, ALU.mult).then_inc(pool_step, 1)
                    dve.wait_ge(pool_step, step + 1)
                    dve.scalar_tensor_tensor(out=pool_u[:, g % 2], in0=cur[:, :, CS:], scalar=1.0 / w, in1=pair[:, :, CS:],
                                             op0=ALU.mult, op1=ALU.subtract).then_inc(pool_step, 1)
                    step += 2
                    for k in range(2):
                        m = 2 * g + k
                        dve.wait_ge(pool_hi_done, m + 1)
                        dve.tensor_tensor(h_lo[:, m], pool_u[:, g % 2, k], h_hi[:, m].bitcast(F32), ALU.subtract)\
                            .then_inc(pool_lo_done, 1)
                split_w(1)
                for m in range(ND):
                    dve.wait_ge(seg_done, m + 1)
                    add_to_x("up0", m, bank[m % 4][:], col("pool_scale", m))
                for m in range(ND):
                    split_x("up0", m)

            def conv_up(l):
                stage = f"up{l}"
                n0, j0, s0 = l * NF, J0[stage], SEG0[stage]

                split_w(j0 + 1)
                norm_factors(stage)

                def body(i):
                    for u in range(2):
                        f = 2 * i + u
                        for g in range(2):
                            dve.wait_ge(seg_done, s0 + 2 * f + g + 1)
                            dve.tensor_tensor(taps_in[:, g, PAD:], bank[2 * u + g][:], rs[:], ALU.mult).then_inc(acc_free, 1)
                        if not isinstance(i, int) or f < NF - 1:
                            split_w(j0 + u + 2 if not isinstance(i, int) else j0 + f + 2, j0 + f + 3)
                        for n, (tap, g) in enumerate(((1, 1), (1, 0), (0, 1), (0, 0))):
                            if tap == 1:
                                dve.wait_ge(seeded, 2 * (n0 + f) + n + 1)
                            else:
                                dve.wait_ge(tapped, 4 * (n0 + f) + n - 1)
                            acc, back = bank[CONV_A + g][:], 2 - tap
                            dve.scalar_tensor_tensor(out=acc, in0=taps_in[:, g, PAD - back:PAD - back + T],
                                                     scalar=col(f"conv{l}_{tap}", g * NF + f), in1=acc,
                                                     op0=ALU.mult, op1=ALU.add).then_inc(tapped, 1)
                        dve.wait_ge(tapped, 4 * (n0 + f) + 4)
                        dve.wait_ge(silu_done, n0 + f + 1)
                        dve.wait_ge(act_lo_done, n0 + f)
                        dve.tensor_tensor(hid[:, u], bank[CONV_A][:], silu_g[:], ALU.mult).then_inc(hid_done, 1)
                        dve.wait_ge(hid_done, n0 + f + 1)
                pairs(dve, NF // 2, body)

            def glu_up(n):
                stage = f"up{n}"
                n0, j0, s0 = n * NF, J0[stage], SEG0[stage]

                def body(i):
                    for u in range(2):
                        f = 2 * i + u
                        split_w(j0 + u + 1 if not isinstance(i, int) else j0 + f + 1, j0 + f + 2)
                        if isinstance(i, int) and f == 0:
                            norm_factors(stage)
                        dve.wait_ge(seg_done, s0 + 2 * f + 1)
                        dve.tensor_tensor(taps_in[:, u, PAD:], bank[2 * u][:], rs[:], ALU.mult).then_inc(acc_free, 1)
                        dve.wait_ge(seg_done, s0 + 2 * f + 2)
                        dve.wait_ge(act_lo_done, n0 + f)
                        dve.tensor_tensor(hid[:, u], bank[2 * u + 1][:], rs[:], ALU.mult).then_inc(acc_free, 1)
                        dve.wait_ge(acc_free, FREE0[stage] + 2 * f + 2)
                        dve.wait_ge(silu_done, n0 + f + 1)
                        dve.tensor_tensor(hid[:, u], hid[:, u], silu_g[:], ALU.mult).then_inc(hid_done, 1)
                pairs(dve, NF // 2, body, peel=1)

            def down(n):
                stage, nxt = f"down{n}", NEXT_PREP[f"down{n}"]
                j0, s0 = J0[stage], SEG0[stage]
                factor = 1.0 if n < 2 else 0.5

                def body(i):
                    for u in range(4):
                        q = 4 * i + u
                        split_w(j0 + u + 1 if not isinstance(i, int) else j0 + q + 1, j0 + q + 2)
                        if u % 2 == 1:
                            m = 2 * i + u // 2
                            dve.wait_ge(seg_done, s0 + q + 1)
                            add_to_x(nxt, m, bank[u // 2][:], factor)
                            if nxt in GAIN:
                                split_x(nxt, m)
                pairs(dve, ND // 2, body)

            def ple(l):
                stage, nxt = f"ple{l}", NEXT_PREP[f"ple{l}"]
                j0, s0 = J0[stage], SEG0[stage]
                for k in range(2):
                    dve.wait_ge(p_hi_done, 2 * l + k + 1)
                    dve.tensor_tensor(p_lo[:, k], taps_in[:, k, PAD:], p_hi[:, k].bitcast(F32), ALU.subtract)\
                        .then_inc(p_lo_done, 1)
                norm_factors(stage)

                def body(i):
                    for u in range(2):
                        m = 2 * i + u
                        split_w(j0 + u + 1 if not isinstance(i, int) else j0 + m + 1, j0 + m + 2)
                        dve.wait_ge(seg_done, s0 + 2 * m + 1)
                        dve.tensor_tensor(ple_t[:, u], bank[2 * u][:], rs[:], ALU.mult).then_inc(acc_free, 1)
                        dve.wait_ge(seg_done, s0 + 2 * m + 2)
                        dve.wait_ge(sig_done, ND * l + m + 1)
                        dve.tensor_tensor(ple_t[:, u], bank[2 * u + 1][:], ple_t[:, u], ALU.mult).then_inc(acc_free, 1)
                        dve.wait_ge(acc_free, FREE0[stage] + 2 * m + 2)
                        add_to_x(nxt, m, ple_t[:, u], 1.0)
                pairs(dve, ND // 2, body)
                if nxt in GAIN:
                    for m in range(ND):
                        split_x(nxt, m)

            def rope_start(r, acc):
                if r >= 2:
                    dve.wait_ge(roped, r - 1)
                if r < 5:
                    dve.tensor_tensor(hid[:, r % 2], acc, rs[:], ALU.mult).then_inc(acc_free, 1)
                else:
                    dve.scalar_tensor_tensor(out=hid[:, r % 2], in0=acc, scalar=QK_SCALE, in1=rs[:], op0=ALU.mult,
                                             op1=ALU.mult).then_inc(acc_free, 1)

            def rope_end(r, out):
                dve.wait_ge(rot_done, r + 1)
                dve.wait_ge(cos_mul, r + 1)
                if r == 4:
                    s = rsin[:, 2 * CS - 1::CS].unsqueeze(1).broadcast_to([P, NG, NCMP])
                    t = hid[:, 0, 0:NG * NC].rearrange("p (g c) -> p g c", g=NG)[:, :, 0:NCMP]
                    partner = bank[5][:, 0:NG * NC].rearrange("p (g c) -> p g c", g=NG)[:, :, 0:NCMP]
                    c = silu_g[:, 0:NG * NC].rearrange("p (g c) -> p g c", g=NG)[:, :, 0:NCMP]
                else:
                    s, t, partner, c = rsin[:], hid[:, r % 2], bank[5 + r % 2][:], silu_g[:]
                dve.tensor_tensor(t, partner, s, ALU.mult).then_inc(sin_mul, 1)
                dve.wait_ge(sin_mul, r + 1)
                if r == 4:
                    for half in range(2):
                        rows = slice(half * HD, (half + 1) * HD)
                        ins = dve.tensor_tensor(out[rows, :, half, 0:NCMP], t[rows, half::2], c[rows, half::2, 0:NCMP],
                                                ALU.add)
                        ins.then_inc(roped if half else kvc_done, 1)
                else:
                    dve.tensor_tensor(out, t, c, ALU.add).then_inc(roped, 1)

            def attention_inputs():
                norm_factors("kv")
                dve.memset(taps_in[:, :, PAD:], 0.0).then_inc(cmp_vec, 1)
                dve.memset(kcT[:], 0.0).then_inc(trig_step, 1)
                for m in range(ND):
                    dve.wait_ge(h2_hi_done, m + 1)
                    dve.scalar_tensor_tensor(out=o_lo[:, m], in0=x[:, m], scalar=col("mix1", m),
                                             in1=o_hi[:, m].bitcast(F32), op0=ALU.mult, op1=ALU.subtract)\
                        .then_inc(h2_lo_done, 1)
                split_w(J0["kproj"] + 1)
                dve.wait_ge(pos_loaded, 16)
                dve.tensor_copy(ang[0][:], pos_i[:]).then_inc(trig_step, 1)
                dve.wait_ge(trig_step, 2)
                dve.tensor_scalar(ang[1][:], ang[0][:], col("freq", 0), None, ALU.mult).then_inc(trig_step, 1)
                dve.wait_ge(trig_step, 3)
                dve.tensor_scalar(ang[0][:], ang[1][:], 1.0 / TWO_PI, MAGIC, ALU.mult, ALU.add).then_inc(trig_step, 1)
                dve.wait_ge(trig_step, 4)
                dve.tensor_scalar(ang[0][:], ang[0][:], -MAGIC, None, ALU.add).then_inc(trig_step, 1)
                for i, c in enumerate((C1, C2, C3)):
                    dve.wait_ge(trig_step, 5 + i)
                    dve.scalar_tensor_tensor(out=ang[2 if i == 2 else 1][:], in0=ang[0][:], scalar=-c, in1=ang[1][:],
                                             op0=ALU.mult, op1=ALU.add).then_inc(trig_step, 1)
                dve.wait_ge(trig_step, 8)
                dve.tensor_scalar(ang[2][:], ang[2][:], PI32, -PI32, ALU.min, ALU.max).then_inc(trig_step, 1)
                dve.wait_ge(trig_step, 9)
                dve.tensor_scalar(ang[0][:], ang[2][:], np.pi / 2, -TWO_PI, ALU.is_gt, ALU.mult).then_inc(trig_step, 1)
                dve.wait_ge(trig_step, 10)
                dve.scalar_tensor_tensor(out=ang[3][:], in0=ang[2][:], scalar=np.pi / 2, in1=ang[0][:], op0=ALU.add,
                                         op1=ALU.add).then_inc(trig_step, 1)
                dve.wait_ge(trig_step, 11)
                dve.tensor_scalar(ang[3][:], ang[3][:], PI32, -PI32, ALU.min, ALU.max).then_inc(trig_step, 1)
                dve.wait_ge(sin_done, 2)
                for q in range(4):
                    for n in (2 * q, 2 * q + 1):
                        dve.wait_ge(seg_done, SEG0["kproj"] + n + 1)
                        if n < 4:
                            for half in range(2):
                                src = slice(half * HD, (half + 1) * HD)
                                g = 2 * (n % 2) + half
                                dve.tensor_tensor(kvc[0:HD, n // 2, g], bank[n % 4][src], rs[src], ALU.mult).then_inc(kvc_done, 1)
                                ins = dve.tensor_tensor(kvc[HD:P, n // 2, g, 0:T - 1], bank[n % 4][src, 1:T],
                                                        rs[src, 1:T], ALU.mult)
                                ins.then_inc(acc_free if half else kvc_done, 1)
                        else:
                            r = n - 4
                            if r >= 2:
                                rope_end(r - 2, kT[:, r - 2])
                            rope_start(r, bank[n % 4][:])
                    split_w(J0["kproj"] + q + 2)
                rope_end(2, kT[:, 2])
                rope_end(3, kT[:, 3])
                dve.wait_ge(rs_turned, 1)
                dve.tensor_copy(rs_col[:], bank[MISC][:].rearrange("p (t q) -> p t q", t=NT)[:, :, 0]).then_inc(rs_col_done, 1)
                dve.wait_ge(rs_col_done, 1)
                split_w(J0["gates"])
                for t in range(NT):
                    dve.wait_ge(seg_done, SEG0["vproj"] + t + 2)
                    dve.tensor_scalar(vsw[:, t], bank[t][:], rs_col[:, t:t + 1], None, ALU.mult).then_inc(acc_free, 1)
                dve.wait_ge(seg_done, SEG0["gates"] + 1)
                dve.tensor_copy(sq[0:3 * NH], bank[2][0:3 * NH]).then_inc(acc_free, 1)
                split_w(J0["qproj"])
                dve.wait_ge(seg_done, SEG0["gates"] + 2)
                dve.tensor_tensor(gates[:], bank[3][:, 0:NT * 3 * NH].rearrange("p (t g) -> p t g", t=NT),
                                  rs_col[:].unsqueeze(2).broadcast_to([P, NT, 3 * NH]), ALU.mult).then_inc(acc_free, 1)
                split_w(J0["qproj"] + 1)
                dve.wait_ge(cmp_mm, 3)
                dve.tensor_copy(hid[:, 0, 0:NG * NC], bank[MISC][:, 0:NG * NC]).then_inc(cmp_vec, 1)
                dve.tensor_copy(vcm[:], bank[MISC][:, P:P + NG * HD].rearrange("p (g d) -> p g d", g=NG)).then_inc(cmp_vec, 1)
                for n in range(2 * 4):
                    if n % 2 == 0 and n:
                        split_w(J0["qproj"] + n // 2 + 1)
                    dve.wait_ge(seg_done, SEG0["qproj"] + n + 1)
                    if n == 1:
                        rope_end(4, kcT)
                    if n >= 2:
                        rope_end(n + 3, qT[:, n - 2])
                    rope_start(n + 5, bank[n % 4][:])
                rope_end(11, qT[:, 6])
                rope_end(12, qT[:, 7])

            def attention():
                dve.wait_ge(gates_done, 1)
                count = 0

                def step(ins):
                    nonlocal count
                    ins.then_inc(cs_vec, 1)
                    count += 1

                dve.wait_ge(roped, 13)
                for t in range(NT):
                    dve.wait_ge(cs_mm, t + 1)
                    to, got = (v.rearrange("p (s c) -> p s c", s=NH) for v in (e4[:, t], bank[t][:]))
                    step(dve.tensor_tensor(to, got, cmask[:, t].unsqueeze(1).broadcast_to([P, NH, NC]), ALU.add))
                e = [e4[:, 2 * i:2 * i + 2].rearrange("p t (s c) -> p (t s) c", s=NH) for i in range(2)]
                s, f = ([cstat[:, k, 2 * i:2 * i + 2].rearrange("p t s -> p (t s)") for i in range(2)] for k in range(2))

                def both(fn):
                    for i in range(2):
                        dve.wait_ge(cs_vec, 2 if count == NT else count - 1)
                        step(fn(i))

                def spread(v):
                    return v.unsqueeze(2).broadcast_to([P, 2 * NH, NC])

                both(lambda i: dve.tensor_reduce(s[i], e[i], AX, ALU.max))
                both(lambda i: dve.tensor_scalar(s[i], s[i], NEG / 10, None, ALU.max))
                both(lambda i: dve.tensor_tensor(e[i], e[i], spread(s[i]), ALU.subtract))
                assert count == CS_SHIFTED + 1
                peaks_first()
                dve.wait_ge(cs_exp, 1)
                step(dve.tensor_reduce(s[0], e[0], AX, ALU.add))
                dve.wait_ge(cs_exp, 2)
                step(dve.tensor_reduce(s[1], e[1], AX, ALU.add))
                both(lambda i: dve.tensor_scalar(s[i], s[i], 1e-30, None, ALU.max))
                both(lambda i: dve.reciprocal(f[i], s[i]))
                both(lambda i: dve.tensor_tensor(f[i].rearrange("p (t s) -> p t s", t=2),
                                                 f[i].rearrange("p (t s) -> p t s", t=2),
                                                 gates[:, 2 * i:2 * i + 2, 0:NH], ALU.mult))
                both(lambda i: dve.tensor_tensor(e[i], e[i], spread(f[i]), ALU.mult))
                assert count == CS_DONE + 1

                for u in range(UNITS + 2):
                    for part, k in UNIT_ORDER_DVE:
                        if part == "peak" and 1 <= u < UNITS:
                            peak(u, k)
                        elif part == "negate" and 1 <= u < UNITS:
                            negate(u, k)
                        elif part == "factor" and 1 <= u <= UNITS:
                            factor(u - 1, k)
                        elif part == "scale" and 1 <= u <= UNITS:
                            scale(u - 1, k)
                        elif part == "keep" and u >= 2:
                            keep(u - 2, k)
                    if u >= 6 and u % 4 == 2:
                        keep_o((u - 6) // 4)
                keep_o(ND - 1)

            def peak(u, t):
                dve.wait_ge(qk_done, 4 * u + t + 1)
                dve.tensor_reduce(stat4[:, u % 2, 0, t:t + 1], bank[t][:, 0:(t + 1) * P], AX, ALU.max).then_inc(max_done, 1)

            def negate(u, t):
                dve.wait_ge(max_done, 4 * u + t + 1)
                dve.tensor_scalar(stat4[:, u % 2, 1, t:t + 1], stat4[:, u % 2, 0, t:t + 1], -1.0, None, ALU.mult)\
                    .then_inc(nmax_done, 1)

            def peaks_first():
                for t in range(NT):
                    peak(0, t)
                for t in range(NT):
                    negate(0, t)

            def factor(u, k):
                c, half, b, g, s = unit(u)
                st = stat4[:, u % 2]
                if k == 0:
                    dve.wait_ge(exp_done, 4 * u + 4)
                    dve.reciprocal(st[:, 3], st[:, 2]).then_inc(fac_done, 1)
                else:
                    dve.wait_ge(fac_done, 2 * u + 1)
                    dve.tensor_tensor(st[:, 3], st[:, 3], gates[:, :, (1 + b) * NH + s], ALU.mult).then_inc(fac_done, 1)

            def scale(u, t):
                at, n = t * (t + 1) // 2 * P, (t + 1) * P
                dve.wait_ge(fac_done, 2 * u + 2)
                dve.tensor_scalar(probs[u % 3][:, at:at + n], probs[u % 3][:, at:at + n], stat4[:, u % 2, 3, t:t + 1],
                                  None, ALU.mult).then_inc(scaled, 1)

            def keep(u, kb):
                dve.wait_ge(turned, 4 * u + kb + 1)
                if 4 * u + kb >= 2:
                    dve.wait_ge(pv_done, 4 * u + kb - 1)
                dve.tensor_copy(hid[:, 0, kb * P:T], bank[4][:, kb * P:T]).then_inc(kept_v, 1)

            def keep_o(c):
                dve.wait_ge(o_hi_done, c + 1)
                dve.tensor_tensor(o_lo[:, c], bank[6 + c % 2][:], o_hi[:, c].bitcast(F32), ALU.subtract).then_inc(o_lo_done, 1)

            def residual(stage):
                nxt = NEXT_PREP[stage]
                for q in range(4):
                    split_w(J0[stage] + q + 1)
                    for m in (2 * q, 2 * q + 1):
                        dve.wait_ge(seg_done, SEG0[stage] + m + 1)
                        add_to_x(nxt, m, bank[m % 4][:], 1.0)
                        split_x(nxt, m)

            def final(prep, gain, done, base):
                norm_factors(prep)
                for m in range(ND):
                    dve.scalar_tensor_tensor(out=x[:, m], in0=x[:, m], scalar=col(gain, m), in1=rs[:], op0=ALU.mult,
                                             op1=ALU.mult).then_inc(done, 1)
                    dve.wait_ge(done, base + m + 1)

            def even():
                todo = [(1, tap) for tap in range(TAPS - 1)] + [(c, tap) for tap in range(TAPS - 1) for c in (2, 3)]
                taps_made = 0

                def conv_taps(count):
                    nonlocal taps_made
                    for i in range(taps_made, min(taps_made + count, len(todo))):
                        c, tap = todo[i]
                        if tap == 0:
                            dve.wait_ge(glu_zero, 1)
                            dve.wait_ge(glu_done, c + 1)
                            dve.wait_ge(y_seed, c + 1)
                        else:
                            dve.wait_ge(y_tap, i - 1 if c > 1 else i)
                        dve.scalar_tensor_tensor(out=cy[:, c], in0=glu[:, c, tap:tap + T], scalar=col("cb_w", tap * CC + c),
                                                 in1=cy[:, c], op0=ALU.mult, op1=ALU.add).then_inc(y_tap, 1)
                    taps_made += count

                dve.memset(glu[:, :, 0:TAPS - 1], 0.0).then_inc(glu_zero, 1)
                for q in range(6):
                    split_w(J0["ein"] + q + 1)
                    if q == 0:
                        norm_factors("mixe")
                    for n in (2 * q, 2 * q + 1):
                        dve.wait_ge(seg_done, SEG0["ein"] + n + 1)
                        c = n // 2
                        to = eq[:, n - 8] if n >= 8 else hid[:, c % 2] if n % 2 == 0 else taps_in[:, c % 2, PAD:]
                        dve.tensor_tensor(to, bank[n % 4][:], rs[:], ALU.mult).then_inc(acc_free, 1)
                    if q < 4:
                        dve.wait_ge(glu_sig, q + 1)
                        dve.tensor_tensor(glu[:, q, TAPS - 1:], hid[:, q % 2], taps_in[:, q % 2, PAD:], ALU.mult)\
                            .then_inc(glu_done, 1)
                    if q >= 2:
                        conv_taps(8)
                dve.wait_ge(diag_mm, 1)
                dve.tensor_tensor(diag[:], bank[MISC][0:8, 0:BLOCK_F + 1], outside[:], ALU.add).then_inc(diag_vec, 1)
                dve.wait_ge(seg_done, SEG0["einv"] + 1)
                dve.tensor_tensor(eq[:, 4], bank[0][:], rs[:], ALU.mult).then_inc(acc_free, 1)
                conv_taps(10)
                dve.wait_ge(rs_turned, 2)
                dve.tensor_copy(e_rs[:], bank[MISC][:].rearrange("p (t q) -> p t q", t=NT)[:, :, 0]).then_inc(rs_col_done, 1)
                dve.wait_ge(rs_col_done, 2)
                for t in range(NT):
                    dve.wait_ge(seg_done, SEG0["einv"] + t + 2)
                    dve.tensor_scalar(ev[:, t], bank[(t + 1) % 4][:, 0:P], e_rs[:, t:t + 1], None, ALU.mult)\
                        .then_inc(acc_free, 1)
                for i in range(4):
                    dve.wait_ge(flipped, i + 1)
                    dve.tensor_copy(ebias[:, 2 * i:2 * i + 2].rearrange("p h s -> p (h s)"), bank[5 + i % 2][:])\
                        .then_inc(bias_kept, 1)
                    conv_taps(1)
                dve.wait_ge(bias_kept, 4)
                split_w(J0["wout1"])

                def bias(u, t):
                    cols = slice(P if t == 0 else 0, 2 * P)
                    if u >= 3 and t == 0:
                        dve.wait_ge(turned, E_TURNED0 + 4 * (u - 2))
                    dve.wait_ge(qk_done, 4 * UNITS + 4 * u + t + 1)
                    dve.scalar_tensor_tensor(out=eprobs[u % 3][:, t, cols], in0=bank[t][:, 0:P if t == 0 else 2 * P],
                                             scalar=QK_SCALE, in1=ebias[:, u, cols], op0=ALU.mult, op1=ALU.add)\
                        .then_inc(scaled, 1)

                def maxima(u):
                    st = estat[:, u % 2]
                    for t in range(NT):
                        cols = slice(P if t == 0 else 0, 2 * P)
                        dve.wait_ge(scaled, E_SCALED0 + 4 * u + t + 1)
                        dve.tensor_reduce(st[:, 0, t:t + 1], eprobs[u % 3][:, t, cols], AX, ALU.max).then_inc(max_done, 1)
                    dve.wait_ge(max_done, 4 * UNITS + 4 * u + 4)
                    dve.tensor_scalar(st[:, 1], st[:, 0], sinks[:, u:u + 1], -1.0, ALU.max, ALU.mult).then_inc(nmax_done, 1)

                def factor(u, k):
                    st = estat[:, u % 2]
                    if k == 0:
                        dve.wait_ge(exp_done, E_EXP0 + 5 * (u + 1))
                        dve.tensor_tensor(st[:, 2], st[:, 2], st[:, 0], ALU.add).then_inc(fac_done, 1)
                    else:
                        dve.wait_ge(fac_done, E_FAC0 + 2 * u + 1)
                        dve.reciprocal(st[:, 3], st[:, 2]).then_inc(fac_done, 1)

                def scale(u, t):
                    dve.wait_ge(fac_done, E_FAC0 + 2 * u + 2)
                    e = eprobs[u % 3][:, t, P if t == 0 else 0:]
                    dve.tensor_scalar(e, e, estat[:, u % 2, 3, t:t + 1], None, ALU.mult).then_inc(e_norm, 1)

                def keep_o(r):
                    dve.wait_ge(o_hi_done, ND + r + 1)
                    dve.tensor_tensor(e_lo[:, r], bank[6][:], e_hi[:, r].bitcast(F32), ALU.subtract)\
                        .then_inc(o_lo_done, 1)

                for u in range(E_UNITS + 3):
                    now, back = u < E_UNITS, 1 <= u <= E_UNITS
                    if u == LN_AT[0] + 1:
                        dve.wait_ge(ln_mm, 1)
                        for c in range(CC):
                            dve.scalar_tensor_tensor(out=cy[:, c], in0=bank[LN][:], scalar=-1.0 / (CC * P), in1=cy[:, c],
                                                     op0=ALU.mult, op1=ALU.add).then_inc(ln_vec, 1)
                    if back:
                        factor(u - 1, 0)
                        factor(u - 1, 1)
                    for t in range(NT):
                        if now:
                            bias(u, t)
                        if back:
                            scale(u - 1, t)
                        if t == 1 and u >= 4 and u % 2 == 0:
                            keep_o((u - 4) // 2)
                    if now:
                        maxima(u)
                    if u <= LN_AT[0]:
                        conv_taps(8)
                    if u == LN_AT[1] + 1:
                        dve.wait_ge(ln_act, 1)
                        dve.reciprocal(silu_g[:], silu_g[:]).then_inc(ln_vec, 1)
                        dve.wait_ge(ln_vec, CC + 1)
                        for c in range(CC):
                            dve.tensor_tensor(cy[:, c], cy[:, c], silu_g[:], ALU.mult).then_inc(ln_vec, 1)
                    if u == LN_AT[1] + 3:
                        for c in range(CC):
                            dve.wait_ge(ln_hi, c + 1)
                            dve.tensor_tensor(e_lo[:, CC + c], cy[:, c], e_hi[:, CC + c].bitcast(F32), ALU.subtract)\
                                .then_inc(ln_lo, 1)
            def odd():
                lam = vec[:, VC["lam"]:VC["lam"] + ND]
                count = 0

                def step(ins):
                    nonlocal count
                    ins.then_inc(lam_vec, 1)
                    count += 1
                    dve.wait_ge(lam_vec, count)

                step(dve.scalar_tensor_tensor(out=lt[:, 0], in0=lam, scalar=-1.0, in1=lam, op0=ALU.mult, op1=ALU.max))
                dve.wait_ge(lam_act, 1)
                step(dve.tensor_scalar(lt[:, 2], lt[:, 1], 2.0, None, ALU.add))
                step(dve.reciprocal(lt[:, 2], lt[:, 2]))
                step(dve.tensor_tensor(lt[:, 3], lt[:, 1], lt[:, 2], ALU.mult))
                step(dve.tensor_tensor(lt[:, 4], lt[:, 3], lt[:, 3], ALU.mult))
                step(dve.tensor_scalar(lt[:, 5], lt[:, 4], 1.0 / 17, None, ALU.mult))
                for d in (15, 13, 11, 9, 7, 5, 3):
                    step(dve.scalar_tensor_tensor(out=lt[:, 5], in0=lt[:, 5], scalar=1.0 / d, in1=lt[:, 4], op0=ALU.add,
                                                  op1=ALU.mult))
                step(dve.scalar_tensor_tensor(out=lt[:, 5], in0=lt[:, 5], scalar=1.0, in1=lt[:, 3], op0=ALU.add, op1=ALU.mult))
                step(dve.tensor_scalar(lt[:, 2], lam, -1.0, 0.0, ALU.mult, ALU.max))
                step(dve.scalar_tensor_tensor(out=lt[:, 0], in0=lt[:, 5], scalar=2.0, in1=lt[:, 2], op0=ALU.mult, op1=ALU.add))
                step(dve.tensor_scalar(sp4[:], lt[:, 0], 4.0, None, ALU.mult))
                step(dve.tensor_scalar(sp8[:], lt[:, 0], -8.0, None, ALU.mult))
                assert count == LAM_STEPS
                for q in range(4):
                    split_w(J0["rec"] + q + 1)
                    if q == 0:
                        norm_factors("mixo")
                    for c in (2 * q, 2 * q + 1):
                        dve.wait_ge(seg_done, SEG0["rec"] + c + 1)
                        src = taps_in[:, c % 2]
                        dve.tensor_tensor(src[:, PAD:], bank[c % 4][:], rs[:], ALU.mult).then_inc(acc_free, 1)
                        dve.wait_ge(r_seed, c + 1)
                        for i, tap in enumerate((2, 1, 0)):
                            if i:
                                dve.wait_ge(r_tap, 3 * c + i)
                            dve.scalar_tensor_tensor(out=rc[:, c], in0=src[:, tap:tap + T], scalar=col("lru_w", tap * ND + c),
                                                     in1=rc[:, c], op0=ALU.mult, op1=ALU.add).then_inc(r_tap, 1)
                        dve.wait_ge(rc_hi, c + 1)
                        dve.tensor_tensor(r_lo[:, c], rc[:, c], r_hi[:, c].bitcast(F32), ALU.subtract).then_inc(rc_lo, 1)
                split_w(J0["ogate"])
                split_w(J0["ogate"] + 1)

                def recurrence(c):
                    k = c % 4
                    dve.wait_ge(lru_act, 12 * (c // 4) + 8 + k + 1)
                    dve.scalar_tensor_tensor(out=ra[:, c], in0=expv[:, k], scalar=1.0, in1=ra[:, c], op0=ALU.add,
                                             op1=ALU.mult).then_inc(lru_vec, 1)
                    dve.wait_ge(lru_pool, ND + c + 1)
                    dve.scalar_tensor_tensor(out=ri[:, c], in0=expv[:, k], scalar=1.0, in1=ri[:, c], op0=ALU.add,
                                             op1=ALU.mult).then_inc(lru_vec, 1)
                    dve.wait_ge(lru_vec, 4 * c + 1)
                    dve.tensor_scalar(ra[:, c], ra[:, c], -1.0, 1.0, ALU.mult, ALU.add).then_inc(lru_vec, 1)
                    dve.wait_ge(lru_vec, 4 * c + 3)
                    dve.tensor_tensor_scan(rc[:, c], ra[:, c], ri[:, c], 0.0, ALU.mult, ALU.add).then_inc(lru_vec, 1)

                def gate_in(c):
                    dve.wait_ge(seg_done, SEG0["ogate"] + c + 1)
                    if c >= 2:
                        dve.wait_ge(y_done, c - 1)
                    dve.tensor_tensor(taps_in[:, c % 2, PAD:], bank[c % 4][:], rs[:], ALU.mult).then_inc(acc_free, 1)

                def gate_state(c):
                    dve.wait_ge(gel_done, c + 1)
                    dve.wait_ge(lru_vec, 4 * c + 4)
                    if c >= 2:
                        dve.wait_ge(y_lo, c - 1)
                    dve.tensor_tensor(hid[:, c % 2], taps_in[:, c % 2, PAD:], rc[:, c], ALU.mult).then_inc(y_done, 1)

                def gate_lo(c):
                    dve.wait_ge(y_hi, c + 1)
                    dve.tensor_tensor(r_lo[:, c], hid[:, c % 2], r_hi[:, c].bitcast(F32), ALU.subtract).then_inc(y_lo, 1)

                for c in range(4):
                    recurrence(c)
                split_w(J0["ogate"] + 2)
                gate_in(0)
                gate_in(1)
                for c in range(4, 8):
                    recurrence(c)
                for c in range(ND):
                    if c in (2, 4):
                        split_w(J0["ogate"] + 2 + c // 2)
                    gate_state(c)
                    if c + 2 < ND:
                        gate_in(c + 2)
                    gate_lo(c)

            for stage in enabled:
                if stage == "pool":
                    start()
                    pool()
                elif stage in ("up0", "up1"):
                    conv_up(int(stage[2:]))
                elif stage.startswith("up"):
                    glu_up(int(stage[2:]))
                elif stage.startswith("down"):
                    down(int(stage[4:]))
                elif stage.startswith("ple"):
                    ple(int(stage[3:]))
                elif stage == "kproj":
                    attention_inputs()
                elif stage == "attn":
                    attention()
                elif stage == "final1":
                    final("final1", "final1", x_ready, x_before("up2"))
                    for m in range(ND):
                        split_x("up2", m)
                elif stage == "final2":
                    final("final2", "final2", out_ready, 0)
                elif stage in ("wout0", "wout1", "wout2"):
                    residual(stage)
                elif stage == "ein":
                    even()
                elif stage == "rec":
                    odd()

        @block.gpsimd
        def _(pool):
            def clear(prep):
                n = PREP_OF[prep]
                if n:
                    pool.wait_ge(stat_done, n)
                pool.memset(sq_sum[:], 0.0).then_inc(sq_added, 1)

            def add(prep, m):
                n = PREP_OF[prep]
                pool.wait_ge(sq_done, ND * n + m + 1)
                pool.wait_ge(sq_added, 9 * n + m + 1)
                pool.tensor_tensor(sq_sum[:], sq_sum[:], sq[:], ALU.add).then_inc(sq_added, 1)

            def squares(prep):
                clear(prep)
                for m in range(ND):
                    add(prep, m)

            def split_hidden(n):
                def body(i):
                    for u in range(2):
                        f = 2 * i + u
                        pool.wait_ge(act_hi_done, NF * n + f + 1)
                        pool.tensor_tensor(act_lo[:, f], hid[:, u], act_hi[:, f].bitcast(F32), ALU.subtract)\
                            .then_inc(act_lo_done, 1)
                pairs(pool, NF // 2, body)

            def down(n):
                prep = NEXT_PREP[f"down{n}"]
                clear(prep)
                pairs(pool, ND // 2, lambda i: [add(prep, 2 * i + u) for u in range(2)])

            def rope_cos():
                for r in range(13):
                    pool.wait_ge(cmp_vec if r == 4 else acc_free, 2 if r == 4 else ROPE_FREE[r])
                    if r:
                        pool.wait_ge(roped, r)
                    if r == 4:
                        c = rcos[:, 2 * CS - 1::CS].unsqueeze(1).broadcast_to([P, NG, NCMP])
                        to, src = (b[:, 0:NG * NC].rearrange("p (g c) -> p g c", g=NG)[:, :, 0:NCMP]
                                   for b in (silu_g, hid[:, 0]))
                        pool.tensor_tensor(to, src, c, ALU.mult).then_inc(cos_mul, 1)
                    else:
                        pool.tensor_tensor(silu_g[:], hid[:, r % 2], rcos[:], ALU.mult).then_inc(cos_mul, 1)

            def convolution_branch():
                pool.wait_ge(glu_zero, 1)
                pool.wait_ge(glu_done, 1)
                pool.wait_ge(y_seed, 1)
                for tap in range(TAPS - 1):
                    if tap:
                        pool.wait_ge(y_tap_p, 2 * tap)
                    pool.tensor_scalar(sq[:], glu[:, 0, tap:tap + T], col("cb_w", tap * CC), None, ALU.mult)\
                        .then_inc(y_tap_p, 1)
                    pool.wait_ge(y_tap_p, 2 * tap + 1)
                    pool.tensor_tensor(cy[:, 0], cy[:, 0], sq[:], ALU.add).then_inc(y_tap_p, 1)
                pool.wait_ge(y_tap_p, 2 * (TAPS - 1))
                pool.wait_ge(y_tap, 3 * (TAPS - 1))
                pool.tensor_copy(sq[:], cy[:, 0]).then_inc(ln_add, 1)
                for c in range(1, CC):
                    pool.wait_ge(ln_add, c)
                    pool.tensor_tensor(sq[:], sq[:], cy[:, c], ALU.add).then_inc(ln_add, 1)
                for c in range(CC):
                    pool.wait_ge(ln_sq, c + 1)
                    if c == 0:
                        pool.tensor_copy(sq_sum[:], sq[:]).then_inc(ln_add, 1)
                    else:
                        pool.wait_ge(ln_add, 4 + c)
                        pool.tensor_tensor(sq_sum[:], sq_sum[:], sq[:], ALU.add).then_inc(ln_add, 1)
                pool.wait_ge(ln_mm, 2)

            def recurrence_inputs():
                for k in range(2):
                    for c in range(ND):
                        if k == 0:
                            pool.wait_ge(g_sig, 2 * c + 2)
                        else:
                            pool.wait_ge(lru_pool, c + 1)
                            pool.wait_ge(lru_act, 12 * (c // 4) + 8 + c % 4 + 1)
                        pool.tensor_tensor(ri[:, c], ri[:, c], rc[:, c], ALU.mult).then_inc(lru_pool, 1)

            pool.memset(pool_tap[:], 0.0).then_inc(act_lo_done, 1)
            squares("start")
            for stage in enabled:
                if stage.startswith("up"):
                    split_hidden(int(stage[2:]))
                elif stage.startswith("down"):
                    down(int(stage[4:]))
                elif stage == "kproj":
                    rope_cos()
                elif stage == "ein":
                    convolution_branch()
                elif stage == "rec":
                    recurrence_inputs()
                elif stage in NEXT_PREP:
                    squares(NEXT_PREP[stage])


def constants():
    c, freq = np.zeros((P, 3 * P), np.float32), np.zeros(P, np.float32)
    c[:, 0:P] = np.eye(P)
    half = HD // 8
    for base in (0, HD):
        for d in range(half):
            c[base + d + half, P + base + d] = -1.0
            c[base + d, P + base + d + half] = 1.0
            f = np.float32(500000.0) ** np.float32(-2.0 * d / (2 * half))
            freq[base + d] = freq[base + d + half] = f
    c[:, 2 * P:3 * P] = np.eye(P)[::-1]
    return c, freq


def pool_fixes():
    t = np.arange(CS)
    fix = np.stack([w / np.minimum(t + 1, w) for w in POOL_WINDOWS]).astype(np.float32)
    return np.ascontiguousarray(np.broadcast_to(fix, (P, 4, CS)))


def compression_masks():
    t = np.arange(P)[:, None, None] + P * np.arange(NT)[None, :, None]
    end = CS * np.arange(NC) + 2 * CS - 1
    seen = (end <= t) & (np.arange(NC) < NCMP)
    return np.where(seen, 0.0, NEG).astype(np.float32)


def relative_buckets():
    dist = 2 * P - 1 - np.arange(BLOCK_F + 1)
    n = np.maximum(dist, 0)
    nf = np.maximum(n, 16).astype(np.float32)
    large = 16 + (np.log(nf / np.float32(16)) / np.float32(np.log(8.0)) * np.float32(16)).astype(np.int32)
    bucket = np.where(n < 16, n, np.minimum(large, 31))
    onehot = (np.arange(32)[:, None] == bucket[None]).astype(np.float32)
    outside = np.where((dist >= 0) & (dist < P), 0.0, NEG).astype(np.float32)
    return onehot, np.ascontiguousarray(np.broadcast_to(outside, (8, BLOCK_F + 1)))


Q_ORDER = [h for i in range(2) for r in range(4) for h in (8 * i + r, 8 * i + 4 + r)]
E_ORDER = [h for r in range(4) for h in (r, 4 + r)]


def tiles(w):
    k, m = w.shape
    return w.reshape(k // P, P, m // P, P).transpose(2, 1, 0, 3)


def jobs(*parts):
    t = np.concatenate([tiles(w) for w in parts], 0)
    n, p, k, m = t.shape
    return np.ascontiguousarray(t.reshape(n // 2, 2, p, k, m).transpose(0, 2, 1, 3, 4)).reshape(n // 2, p, 2 * k * m)


def interleaved(a, b):
    t = np.stack([tiles(a), tiles(b)], 1)
    n, _, p, k, m = t.shape
    return np.ascontiguousarray(t.transpose(0, 2, 1, 3, 4)).reshape(n, p, 2 * k * m)


def halves(w):
    t = tiles(w)
    n, p, k, m = t.shape
    return np.ascontiguousarray(t.reshape(n, p, 2, k // 2, m).transpose(0, 2, 1, 3, 4)).reshape(2 * n, p, k // 2 * m)


def by_rows(w, k0, k1):
    return w.reshape(-1, P, w.shape[1])[k0:k1].transpose(1, 0, 2).reshape(P, -1)


def heads(w, order, axis):
    shape = list(w.shape)
    shape[axis:axis + 1] = [shape[axis] // HD, HD]
    return np.take(w.reshape(shape), order, axis).reshape(w.shape)


def layout(i):
    a = {k: np.asarray(v) for k, v in i.items()}
    cols = lambda v: np.asarray(v).reshape(-1, P).T
    parts = {
        "mix0": a["norm_mix"][0], "mix1": a["norm_mix"][1], "pool_scale": a["pool_scale"][0], "kv": a["norm_kv"],
        "ffn0": a["norm_ffn"][0], "ffn1": a["norm_ffn"][1], "ple0": a["norm_ple"][0], "ple1": a["norm_ple"][1],
        "final1": a["norm_final"], "ffn2": a["norm_ffn1_2"][0], "ffn3": a["norm_ffn2_2"][0],
        "ffn4": a["norm_ffn1_2"][1], "ffn5": a["norm_ffn2_2"][1], "mixe": a["norm_mix_2"][0], "mixo": a["norm_mix_2"][1],
        "final2": a["norm_final_2"], "cb_w": a["conv_b_w_2"][0], "cb_b": a["conv_b_b_2"][0], "ln_g": a["conv_ln_g_2"][0],
        "ln_b": a["conv_ln_b_2"][0], "lru_w": a["lru_conv_w_2"][0], "lru_b": a["lru_conv_b_2"][0],
        "ga_b": a["gate_a_b_2"][0], "gx_b": a["gate_x_b_2"][0], "lam": a["lru_lambda_2"][0],
    }
    consts, parts["freq"] = constants()
    for l in range(2):
        for j in range(3):
            parts[f"conv{l}_{j}"] = a["ffn_conv"][l, j]
        parts[f"conv{l}_b"] = a["ffn_conv_b"][l]
    out = {"x": a["x"][0].T.reshape(ND, P, T).transpose(1, 0, 2), "vec": np.concatenate([cols(parts[n]) for n, _ in VEC_LIST], 1)}
    out["p"] = a["p"][:, 0].transpose(0, 2, 1).reshape(2, 2, P, T).transpose(0, 2, 1, 3)
    out["positions"] = a["positions"]
    out["w_pool"] = a["pool_w"][0].reshape(4, 2, P, 2, P).transpose(2, 0, 3, 1, 4).reshape(1, P, SLOT * P)
    for l in range(2):
        up = a["ffn_up"][l]
        out[f"w_up{l}"] = interleaved(up[:, :DFF], up[:, DFF:])
        out[f"w_down{l}"] = halves(a["ffn_down"][l])
        gate, proj = tiles(a["ple_gate"][l]), tiles(a["ple_proj"][l])
        out[f"w_ple{l}"] = np.concatenate([gate, proj], 2).reshape(ND, P, 10 * P)
    kv = a["w_kv"]
    out["w_kproj"] = jobs(kv[:, 0:512], kv[:, 512:768], kv[:, 1024:1280])
    v = np.concatenate([kv[:, 768:1024], kv[:, 1280:1536]], 1)
    out["w_vproj"] = np.stack([by_rows(v, 0, 4), by_rows(v, 4, 8)])
    w_in = a["w_in_b"][0]
    gate = w_in[:, D:].reshape(D, NH, 3)[:, Q_ORDER].transpose(0, 2, 1).reshape(D, 3 * NH)
    out["w_gates"] = by_rows(gate, 0, 8)[None]
    out["w_qproj"] = jobs(heads(w_in[:, :D], Q_ORDER, 1))
    out["w_wout0"] = jobs(heads(a["w_out_b"][0], Q_ORDER, 0))
    for n, (kind, l) in enumerate((("ffn1", 0), ("ffn2", 0), ("ffn1", 1), ("ffn2", 1))):
        out[f"w_up{n + 2}"] = interleaved(a[kind + "_wg_2"][l], a[kind + "_wu_2"][l])
        out[f"w_down{n + 2}"] = halves(a[kind + "_wd_2"][l])
    e = a["even_w_in_2"][0]
    ga, gb = tiles(e[:, 768:1280]), tiles(e[:, 1280:1792])
    glu = np.stack([ga, gb], 1).transpose(0, 2, 1, 3, 4).reshape(4, P, SLOT * P)
    out["w_ein"] = np.concatenate([glu, jobs(heads(e[:, 0:512], E_ORDER, 1))], 0)
    out["w_einv"] = np.concatenate([tiles(e[:, 512:640])[0].reshape(P, -1), by_rows(e[:, 640:768], 0, 8)], 1)[None]
    eo = a["even_w_out_2"][0]
    out["w_wout1"] = jobs(np.concatenate([heads(eo[:512], E_ORDER, 0), eo[512:]], 0))
    o = a["odd_w_in_2"][0]
    out["w_rec"] = jobs(o[:, D:])
    out["w_ogate"] = jobs(o[:, :D])
    gates = np.stack([a["gate_a_w_2"][0], a["gate_x_w_2"][0]])
    out["w_lgate"] = gates.transpose(2, 0, 1, 3).reshape(1, P, SLOT * P)
    out["w_wout2"] = jobs(a["odd_w_out_2"][0])
    for s in "kv":
        out[f"cmp_w1_{s}"] = a[f"cmp_w1_{s}"].reshape(CS, P, P).transpose(1, 0, 2)
        out[f"cmp_w2_{s}"] = a[f"cmp_w2_{s}"]
        out[f"cmp_pos_{s}"] = a[f"cmp_pos_{s}"].reshape(CS, P).T
    out["rel_bias"] = a["rel_bias_2"][:, E_ORDER]
    out["sinks"] = a["attn_sinks_2"][:, E_ORDER]
    out["consts"] = consts
    out["pool_fix"] = pool_fixes()
    out["cmask"] = compression_masks()
    out["onehot"], out["outside"] = relative_buckets()
    return {k: np.ascontiguousarray(v) for k, v in out.items()}


def kernel(stop_after=None, **inputs):
    import concourse.bacc as bacc
    from concourse.bass_utils import run_bass_kernel_spmd
    from ml_dtypes import bfloat16

    arrays = layout(inputs)
    ahead = np.arange(P)[None, :] > np.arange(P)[:, None]
    arrays["mask_bf"] = np.ascontiguousarray(np.stack([np.eye(P), np.where(ahead, NEG, 0.0)], 1).astype(bfloat16))
    nc = bacc.Bacc("TRN2", target_bir_lowering=False, num_devices=1)
    a = {n: nc.dram_tensor("in_" + n, v.shape, mybir.dt.from_np(v.dtype), kind="ExternalInput").ap()
         for n, v in arrays.items()}
    a["out"] = nc.dram_tensor("out", (ND, P, T), F32, kind="ExternalOutput").ap()
    build(nc, a, stop_after)
    r = run_bass_kernel_spmd(nc, [{"in_" + n: v for n, v in arrays.items()}], core_ids=[0])
    return r.results[0]["out"].reshape(D, T).T.reshape(1, T, D)
```
